# Optimizing a Trainium2 kernel written in Bass

```python
import math
import jax, jax.numpy as jnp
from jax import lax
import numpy as np

D_MODEL = 1024
BATCH = 1
SEQ = 256
DEPTH = 1

D_MIX = D_MODEL
EPS = 1e-6
NEG = -1e30
FORCE = 1e6
F_FLOOR = 1e-30
NSA_HEADS = 8
NSA_KV_GROUPS = 2
NSA_HD = 64
CMP_LEN = 32
CMP_STRIDE = 16
CMP_HID = 256
SEL_BLOCK = 64
SEL_TOPK = 16
SEL_QBLOCK = 32
WINDOW = 512
WIN_QBLOCK = 128
HG_HEADS = 4
HG_DK = 128
HG_DV = 128
HG_CHUNK = 64
D_FF = 2752

NSA_WIDTH = NSA_HEADS * NSA_HD
HG_WIDTH = HG_HEADS * HG_DV
KV_W = NSA_KV_GROUPS * NSA_HD
IN_SIZES = (NSA_WIDTH, KV_W, KV_W, KV_W, KV_W, KV_W, KV_W, NSA_HEADS * 3,
            HG_HEADS * HG_DK, HG_HEADS * HG_DK, HG_WIDTH, HG_WIDTH)
IN_COLS = sum(IN_SIZES)
IN_SPLITS = tuple(int(v) for v in np.cumsum(IN_SIZES)[:-1])


def rms_norm(x, g):
    xf = x.astype(jnp.float32)
    y = xf * lax.rsqrt(jnp.mean(xf * xf, axis=-1, keepdims=True) + EPS)
    return (y * g.astype(jnp.float32)).astype(x.dtype)

def swiglu(x, w_gu, w_down):
    gate, up = jnp.split(x @ w_gu, 2, axis=-1)
    return (jax.nn.silu(gate) * up) @ w_down

def alibi_slopes(n):
    return jnp.asarray([2.0 ** (-8.0 * (i + 1) / n) for i in range(n)], dtype=jnp.float32)

def compress(kv, pos_emb, w1, w2):
    B, S, G, dk = kv.shape
    chunks = kv.reshape(B, S // CMP_STRIDE, CMP_STRIDE, G, dk)
    blocks = jnp.concatenate([chunks[:, :-1], chunks[:, 1:]], axis=2) + pos_emb[:, None, :]
    nb = blocks.shape[1]
    flat = blocks.transpose(0, 1, 3, 2, 4).reshape(B, nb, G, CMP_LEN * dk)
    return jax.nn.gelu(flat @ w1) @ w2

def nsa_group(q, k_c, v_c, k_s, v_s, k_w, v_w, gate_logits,
              cmp_pos_k, cmp_pos_v, cmp_k_w1, cmp_k_w2, cmp_v_w1, cmp_v_w2):
    B, S = q.shape[:2]
    G, Hg, dk = NSA_KV_GROUPS, NSA_HEADS // NSA_KV_GROUPS, NSA_HD
    scale = dk ** -0.5
    slopes = alibi_slopes(NSA_HEADS).reshape(G, Hg)
    q5 = q.reshape(B, S, G, Hg, dk)
    kv4 = lambda t: t.reshape(B, S, G, dk)
    pos = jnp.arange(S, dtype=jnp.int32)

    kc = compress(kv4(k_c), cmp_pos_k, cmp_k_w1, cmp_k_w2)
    vc = compress(kv4(v_c), cmp_pos_v, cmp_v_w1, cmp_v_w2)
    nb = kc.shape[1]
    blk_end = jnp.arange(nb, dtype=jnp.int32) * CMP_STRIDE + (CMP_LEN - 1)
    dist_c = pos[:, None] - blk_end[None, :]
    s_c = jnp.einsum('bsgnd,bcgd->bsgnc', q5, kc).astype(jnp.float32) * scale
    s_c = s_c - slopes[:, :, None] * dist_c.astype(jnp.float32)[:, None, None, :]
    s_c = jnp.where((dist_c >= 0)[:, None, None, :], s_c, NEG)
    p_c = jax.nn.softmax(s_c, axis=-1)
    p_c = jnp.where((pos >= CMP_LEN - 1)[:, None, None, None], p_c, 0.0)
    o_cmp = jnp.einsum('bsgnc,bcgd->bsgnd', p_c.astype(vc.dtype), vc)

    imp = p_c.sum(axis=3)
    padded = jnp.pad(imp, ((0, 0), (0, 0), (0, 0), (1, 1)))
    chunk_imp = padded[..., :-1] + padded[..., 1:]
    ns = S // SEL_BLOCK
    p_slc = chunk_imp.reshape(B, S, G, ns, SEL_BLOCK // CMP_STRIDE).sum(-1)
    blk = jnp.arange(ns, dtype=jnp.int32)
    cur = pos // SEL_BLOCK
    forced = (blk[None] == 0) | (blk[None] == cur[:, None]) | (blk[None] == cur[:, None] - 1)
    causal = blk[None] * SEL_BLOCK <= pos[:, None]
    score = jnp.where(forced[:, None], FORCE, jnp.where(causal[:, None], p_slc, NEG))
    n_sel = min(SEL_TOPK, ns)
    _, sel_idx = lax.top_k(score, n_sel)

    k_blocks = kv4(k_s).reshape(B, ns, SEL_BLOCK, G, dk).transpose(0, 3, 1, 2, 4)
    v_blocks = kv4(v_s).reshape(B, ns, SEL_BLOCK, G, dk).transpose(0, 3, 1, 2, 4)
    nq = S // SEL_QBLOCK
    b_ix = jnp.arange(B)[:, None, None, None]
    g_ix = jnp.arange(G)[None, None, :, None]
    l_ar = jnp.arange(SEL_BLOCK, dtype=jnp.int32)

    def sel_step(args):
        qb, idx, qi = args
        kg = k_blocks[b_ix, g_ix, idx]
        vg = v_blocks[b_ix, g_ix, idx]
        s = jnp.einsum('btgnd,btgkld->btgnkl', qb, kg).astype(jnp.float32) * scale
        qpos = qi * SEL_QBLOCK + jnp.arange(SEL_QBLOCK, dtype=jnp.int32)
        kpos = idx[..., None] * SEL_BLOCK + l_ar
        dist = qpos[None, :, None, None, None] - kpos
        s = s - slopes[None, None, :, :, None, None] * dist.astype(jnp.float32)[:, :, :, None]
        s = jnp.where((dist >= 0)[:, :, :, None], s, NEG)
        p = jax.nn.softmax(s.reshape(s.shape[:4] + (-1,)), axis=-1).reshape(s.shape)
        return jnp.einsum('btgnkl,btgkld->btgnd', p.astype(vg.dtype), vg)

    o_sel = lax.map(sel_step, (q5.reshape(B, nq, SEL_QBLOCK, G, Hg, dk).swapaxes(0, 1),
                               sel_idx.reshape(B, nq, SEL_QBLOCK, G, n_sel).swapaxes(0, 1),
                               jnp.arange(nq, dtype=jnp.int32)))
    o_sel = o_sel.swapaxes(0, 1).reshape(B, S, G, Hg, dk)

    nwq = S // WIN_QBLOCK
    n_kb = WINDOW // WIN_QBLOCK + 1
    kw_len = n_kb * WIN_QBLOCK

    def band(t):
        tp = jnp.pad(kv4(t), ((0, 0), (WINDOW, 0), (0, 0), (0, 0)))
        tp = tp.reshape(B, nwq + WINDOW // WIN_QBLOCK, WIN_QBLOCK, G, dk)
        return jnp.concatenate([tp[:, j:j + nwq] for j in range(n_kb)], axis=2).swapaxes(0, 1)

    def win_step(args):
        qb, kb, vb, qi = args
        s = jnp.einsum('btgnd,bkgd->btgnk', qb, kb).astype(jnp.float32) * scale
        qpos = qi * WIN_QBLOCK + jnp.arange(WIN_QBLOCK, dtype=jnp.int32)
        kpos = qi * WIN_QBLOCK - WINDOW + jnp.arange(kw_len, dtype=jnp.int32)
        dist = qpos[:, None] - kpos[None, :]
        valid = (dist >= 0) & (dist < WINDOW) & (kpos >= 0)[None, :]
        s = s - slopes[None, None, :, :, None] * dist.astype(jnp.float32)[None, :, None, None, :]
        s = jnp.where(valid[None, :, None, None, :], s, NEG)
        p = jax.nn.softmax(s, axis=-1)
        return jnp.einsum('btgnk,bkgd->btgnd', p.astype(vb.dtype), vb)

    o_win = lax.map(win_step, (q5.reshape(B, nwq, WIN_QBLOCK, G, Hg, dk).swapaxes(0, 1),
                               band(k_w), band(v_w), jnp.arange(nwq, dtype=jnp.int32)))
    o_win = o_win.swapaxes(0, 1).reshape(B, S, G, Hg, dk)

    g = jax.nn.sigmoid(gate_logits.astype(jnp.float32)).reshape(B, S, G, Hg, 3)
    o = (g[..., 0:1] * o_cmp.astype(jnp.float32) + g[..., 1:2] * o_sel.astype(jnp.float32)
         + g[..., 2:3] * o_win.astype(jnp.float32))
    return o.reshape(B, S, NSA_WIDTH).astype(q.dtype)

def hgrn2_group(q, f_logit, i_in, g_in, lower_bound, out_norm):
    B, S = q.shape[:2]
    H, dk, dv, C = HG_HEADS, HG_DK, HG_DV, HG_CHUNK
    qf = jax.nn.silu(q.astype(jnp.float32)).reshape(B, S, H, dk)
    lb = lower_bound.astype(jnp.float32)
    z = f_logit.astype(jnp.float32)
    f = lb + (1.0 - lb) * jax.nn.sigmoid(z)
    logf = jnp.log(jnp.maximum(f, F_FLOOR)).reshape(B, S, H, dk)
    kf = ((1.0 - lb) * jax.nn.sigmoid(-z)).reshape(B, S, H, dk)
    vf = i_in.astype(jnp.float32).reshape(B, S, H, dv)
    nc = S // C
    to_chunks = lambda t: t.reshape(B, nc, C, H, t.shape[-1]).transpose(1, 0, 3, 2, 4)
    tril = jnp.tril(jnp.ones((C, C), dtype=bool))

    def step(state, inp):
        qc, kc, vc, lf = inp
        b = jnp.cumsum(lf, axis=2)
        decay = b[:, :, :, None, :] - b[:, :, None, :, :]
        decay = jnp.exp(jnp.where(tril[:, :, None], decay, NEG))
        a = jnp.einsum('bhtd,bhtsd,bhsd->bhts', qc, decay, kc)
        o_intra = jnp.einsum('bhts,bhsv->bhtv', a, vc)
        o_inter = jnp.einsum('bhtd,bhdv->bhtv', qc * jnp.exp(b), state)
        b_last = b[:, :, -1]
        new_state = (jnp.exp(b_last)[..., None] * state
                     + jnp.einsum('bhsd,bhsv->bhdv', kc * jnp.exp(b_last[:, :, None] - b), vc))
        return new_state, o_intra + o_inter

    state0 = jnp.zeros((B, H, dk, dv), jnp.float32)
    _, o = lax.scan(step, state0, (to_chunks(qf), to_chunks(kf), to_chunks(vf), to_chunks(logf)))
    o = o.transpose(1, 0, 3, 2, 4).reshape(B, S, H, dv)
    o = o * lax.rsqrt(jnp.mean(o * o, axis=-1, keepdims=True) + EPS) * out_norm.astype(jnp.float32)
    o = o.reshape(B, S, HG_WIDTH) * jax.nn.silu(g_in.astype(jnp.float32))
    return o.astype(q.dtype)

def hybrid_mixer(h, w_in, cmp_pos_k, cmp_pos_v, cmp_k_w1, cmp_k_w2, cmp_v_w1, cmp_v_w2,
                 lower_bound, hg_norm, w_out):
    parts = jnp.split(h @ w_in, IN_SPLITS, axis=-1)
    nq, k_c, v_c, k_s, v_s, k_w, v_w, gl, hq, hf, hi, hg = parts
    o_nsa = nsa_group(nq, k_c, v_c, k_s, v_s, k_w, v_w, gl,
                      cmp_pos_k, cmp_pos_v, cmp_k_w1, cmp_k_w2, cmp_v_w1, cmp_v_w2)
    o_hg = hgrn2_group(hq, hf, hi, hg, lower_bound, hg_norm)
    return jnp.concatenate([o_nsa, o_hg], axis=-1) @ w_out

def first_inputs(seed: int = 0) -> dict:
    key = jax.random.key(seed)
    ks = jax.random.split(key, 20)
    nrm = lambda k, shape, s: jax.random.normal(k, shape, jnp.float32) * s
    gain = lambda k, shape: 1.0 + 0.02 * jax.random.normal(k, shape, jnp.float32)
    L = DEPTH
    return {
        "x": jax.random.normal(ks[0], (BATCH, SEQ, D_MODEL), jnp.float32),
        "ffn1_norm": gain(ks[1], (L, D_MODEL)),
        "ffn1_w_gu": nrm(ks[2], (L, D_MODEL, 2 * D_FF), D_MODEL ** -0.5),
        "ffn1_w_down": nrm(ks[3], (L, D_FF, D_MODEL), D_FF ** -0.5),
        "mix_norm": gain(ks[4], (L, D_MODEL)),
        "w_in": nrm(ks[5], (L, D_MODEL, IN_COLS), D_MODEL ** -0.5),
        "cmp_pos_k": nrm(ks[6], (L, CMP_LEN, NSA_HD), 0.02),
        "cmp_pos_v": nrm(ks[7], (L, CMP_LEN, NSA_HD), 0.02),
        "cmp_k_w1": nrm(ks[8], (L, CMP_LEN * NSA_HD, CMP_HID), (CMP_LEN * NSA_HD) ** -0.5),
        "cmp_k_w2": nrm(ks[9], (L, CMP_HID, NSA_HD), CMP_HID ** -0.5),
        "cmp_v_w1": nrm(ks[10], (L, CMP_LEN * NSA_HD, CMP_HID), (CMP_LEN * NSA_HD) ** -0.5),
        "cmp_v_w2": nrm(ks[11], (L, CMP_HID, NSA_HD), CMP_HID ** -0.5),
        "hgrn_lower_bound": nrm(ks[12], (L, HG_HEADS * HG_DK), 0.1),
        "hgrn_out_norm": gain(ks[13], (L, HG_DV)),
        "w_out": nrm(ks[14], (L, D_MIX, D_MODEL), D_MIX ** -0.5),
        "ffn2_norm": gain(ks[15], (L, D_MODEL)),
        "ffn2_w_gu": nrm(ks[16], (L, D_MODEL, 2 * D_FF), D_MODEL ** -0.5),
        "ffn2_w_down": nrm(ks[17], (L, D_FF, D_MODEL), D_FF ** -0.5),
        "final_norm": gain(ks[18], (D_MODEL,)),
    }

def first_block(x, ffn1_norm, ffn1_w_gu, ffn1_w_down, mix_norm, w_in, cmp_pos_k, cmp_pos_v,
              cmp_k_w1, cmp_k_w2, cmp_v_w1, cmp_v_w2, hgrn_lower_bound, hgrn_out_norm, w_out,
              ffn2_norm, ffn2_w_gu, ffn2_w_down, final_norm):
    lb_sm = jax.nn.softmax(hgrn_lower_bound.astype(jnp.float32), axis=0)
    lower_bounds = jnp.cumsum(lb_sm, axis=0) - lb_sm[0]
    h = x
    for l in range(DEPTH):
        h = h + 0.5 * swiglu(rms_norm(h, ffn1_norm[l]), ffn1_w_gu[l], ffn1_w_down[l])
        h = h + hybrid_mixer(rms_norm(h, mix_norm[l]), w_in[l], cmp_pos_k[l], cmp_pos_v[l],
                             cmp_k_w1[l], cmp_k_w2[l], cmp_v_w1[l], cmp_v_w2[l],
                             lower_bounds[l], hgrn_out_norm[l], w_out[l])
        h = h + 0.5 * swiglu(rms_norm(h, ffn2_norm[l]), ffn2_w_gu[l], ffn2_w_down[l])
    return rms_norm(h, final_norm)


DEPTH_2 = 2

N_A = DEPTH_2 // 2
N_B = DEPTH_2 - N_A
PLE_DIM = 256
FOX_HEADS = 16
FOX_HEAD_DIM = D_MODEL // FOX_HEADS
FOX_IN = 3 * D_MODEL + FOX_HEADS
FOX_GATE_BIAS = 3.0
MLA_HEADS = 16
QK_NOPE_DIM = 128
QK_ROPE_DIM = 64
V_HEAD_DIM = 128
Q_LORA_RANK = 384
KV_LORA_RANK = 256
ROPE_THETA = 10000.0
D_FF_2 = 2816
BLOCK_Q = 128
LN_EPS = 1e-5
RMS_EPS = 1e-6
ALPHA = (2 * DEPTH_2) ** 0.25
BETA = (8 * DEPTH_2) ** -0.25


def layer_norm(x, g, b):
    xf = x.astype(jnp.float32)
    mu = jnp.mean(xf, axis=-1, keepdims=True)
    xc = xf - mu
    var = jnp.mean(xc * xc, axis=-1, keepdims=True)
    y = xc * lax.rsqrt(var + LN_EPS) * g.astype(jnp.float32) + b.astype(jnp.float32)
    return y.astype(x.dtype)

def rms_norm_2(x, g):
    xf = x.astype(jnp.float32)
    y = xf * lax.rsqrt(jnp.mean(xf * xf, axis=-1, keepdims=True) + RMS_EPS) * g.astype(jnp.float32)
    return y.astype(x.dtype)

def post_norm(x, delta, g, b):
    return layer_norm(ALPHA * x + delta, g, b)

def swiglu_2(x, w_in, w_out):
    h = x @ w_in
    gate, up = h[..., :D_FF_2], h[..., D_FF_2:]
    return (jax.nn.silu(gate) * up) @ w_out

def rope_tables(seq_len):
    half = QK_ROPE_DIM // 2
    inv = ROPE_THETA ** (-jnp.arange(half, dtype=jnp.float32) * (2.0 / QK_ROPE_DIM))
    ang = jnp.arange(seq_len, dtype=jnp.float32)[:, None] * inv[None, :]
    return jnp.cos(ang), jnp.sin(ang)

def rope(x, cos, sin):
    half = x.shape[-1] // 2
    xf = x.astype(jnp.float32)
    x1, x2 = xf[..., :half], xf[..., half:]
    return jnp.concatenate([x1 * cos - x2 * sin, x2 * cos + x1 * sin], axis=-1).astype(x.dtype)

def causal_block_attention(score_fn, v):
    B, S, H, Dv = v.shape
    n_blocks = S // BLOCK_Q
    k_pos = jnp.arange(S)

    def one_block(blk):
        start = blk * BLOCK_Q
        s = score_fn(start)
        q_pos = start + jnp.arange(BLOCK_Q)
        s = jnp.where(k_pos[None, :] <= q_pos[:, None], s, -jnp.inf)
        w = jax.nn.softmax(s, axis=-1).astype(v.dtype)
        return jnp.einsum('bhqk,bkhd->bqhd', w, v)

    o = lax.map(one_block, jnp.arange(n_blocks))
    return jnp.moveaxis(o, 0, 1).reshape(B, S, H, Dv)

def fox_mixer(x, w_in, b_f, w_o):
    B, S, _ = x.shape
    h = x @ w_in
    q = h[..., :D_MODEL].reshape(B, S, FOX_HEADS, FOX_HEAD_DIM)
    k = h[..., D_MODEL:2 * D_MODEL].reshape(B, S, FOX_HEADS, FOX_HEAD_DIM)
    v = h[..., 2 * D_MODEL:3 * D_MODEL].reshape(B, S, FOX_HEADS, FOX_HEAD_DIM)
    f_logit = h[..., 3 * D_MODEL:].astype(jnp.float32) + b_f.astype(jnp.float32)
    cum = jnp.cumsum(jax.nn.log_sigmoid(f_logit), axis=1).transpose(0, 2, 1)
    scale = FOX_HEAD_DIM ** -0.5

    def scores(start):
        qb = lax.dynamic_slice_in_dim(q, start, BLOCK_Q, axis=1)
        cb = lax.dynamic_slice_in_dim(cum, start, BLOCK_Q, axis=2)
        s = jnp.einsum('bqhd,bkhd->bhqk', qb, k).astype(jnp.float32) * scale
        return s + cb[:, :, :, None] - cum[:, :, None, :]

    o = causal_block_attention(scores, v)
    return o.reshape(B, S, D_MODEL) @ w_o

def shared_kv(x, w_down, kv_norm, w_up, cos, sin):
    B, S, _ = x.shape
    h = x @ w_down
    c_kv = rms_norm_2(h[..., :KV_LORA_RANK], kv_norm)
    k_rope = rope(h[..., KV_LORA_RANK:], cos, sin)
    kv = jnp.einsum('bsc,chd->bshd', c_kv, w_up)
    return kv[..., :QK_NOPE_DIM], k_rope, kv[..., QK_NOPE_DIM:]

def mla_mixer(x, w_dq, q_norm, w_uq, w_o, k_nope, k_rope, v, cos, sin):
    B, S, _ = x.shape
    c_q = rms_norm_2(x @ w_dq, q_norm)
    q = jnp.einsum('bsc,chd->bshd', c_q, w_uq)
    q_nope = q[..., :QK_NOPE_DIM]
    q_rope = rope(q[..., QK_NOPE_DIM:], cos[:, None, :], sin[:, None, :])
    scale = (QK_NOPE_DIM + QK_ROPE_DIM) ** -0.5

    def scores(start):
        qn = lax.dynamic_slice_in_dim(q_nope, start, BLOCK_Q, axis=1)
        qr = lax.dynamic_slice_in_dim(q_rope, start, BLOCK_Q, axis=1)
        s = jnp.einsum('bqhd,bkhd->bhqk', qn, k_nope) + jnp.einsum('bqhr,bkr->bhqk', qr, k_rope)
        return s.astype(jnp.float32) * scale

    o = causal_block_attention(scores, v)
    return o.reshape(B, S, MLA_HEADS * V_HEAD_DIM) @ w_o

def second_inputs(seed: int = 0) -> dict:
    key = jax.random.key(seed)
    ks = iter(jax.random.split(key, 32))
    f32 = jnp.float32

    def nrm(shape, fan_in, scale=1.0):
        return jax.random.normal(next(ks), shape, f32) * (scale * fan_in ** -0.5)

    def gain(shape):
        return 1.0 + 0.02 * jax.random.normal(next(ks), shape, f32)

    def small(shape, s=0.02):
        return s * jax.random.normal(next(ks), shape, f32)

    x = jax.random.normal(next(ks), (BATCH, SEQ, D_MODEL), f32)
    p = jax.random.normal(next(ks), (DEPTH_2, BATCH, SEQ, PLE_DIM), f32)
    ffn1_w_in = nrm((DEPTH_2, D_MODEL, 2 * D_FF_2), D_MODEL)
    ffn1_w_out = nrm((DEPTH_2, D_FF_2, D_MODEL), D_FF_2, BETA)
    ffn2_w_in = nrm((DEPTH_2, D_MODEL, 2 * D_FF_2), D_MODEL)
    ffn2_w_out = nrm((DEPTH_2, D_FF_2, D_MODEL), D_FF_2, BETA)
    ln_g = gain((DEPTH_2, 4, D_MODEL))
    ln_b = small((DEPTH_2, 4, D_MODEL))
    ple_w_gate = nrm((DEPTH_2, D_MODEL, D_MODEL), D_MODEL)
    ple_b_gate = small((DEPTH_2, D_MODEL))
    ple_w_proj = nrm((DEPTH_2, PLE_DIM, D_MODEL), PLE_DIM, BETA)
    fox_w_in = nrm((N_A, D_MODEL, FOX_IN), D_MODEL)
    fox_w_in = fox_w_in.at[:, :, 2 * D_MODEL:3 * D_MODEL].multiply(BETA)
    fox_b_f = FOX_GATE_BIAS + 0.5 * jax.random.normal(next(ks), (N_A, FOX_HEADS), f32)
    fox_w_o = nrm((N_A, D_MODEL, D_MODEL), D_MODEL, BETA)
    mla_w_dq = nrm((N_B, D_MODEL, Q_LORA_RANK), D_MODEL)
    mla_q_norm = gain((N_B, Q_LORA_RANK))
    mla_w_uq = nrm((N_B, Q_LORA_RANK, MLA_HEADS, QK_NOPE_DIM + QK_ROPE_DIM), Q_LORA_RANK)
    mla_w_o = nrm((N_B, MLA_HEADS * V_HEAD_DIM, D_MODEL), MLA_HEADS * V_HEAD_DIM, BETA)
    kv_w_down = nrm((D_MODEL, KV_LORA_RANK + QK_ROPE_DIM), D_MODEL)
    kv_norm = gain((KV_LORA_RANK,))
    kv_w_up = nrm((KV_LORA_RANK, MLA_HEADS, QK_NOPE_DIM + V_HEAD_DIM), KV_LORA_RANK)
    kv_w_up = kv_w_up.at[:, :, QK_NOPE_DIM:].multiply(BETA)
    return {'x': x, 'p': p,
            'ffn1_w_in': ffn1_w_in, 'ffn1_w_out': ffn1_w_out,
            'ffn2_w_in': ffn2_w_in, 'ffn2_w_out': ffn2_w_out,
            'ln_g': ln_g, 'ln_b': ln_b,
            'ple_w_gate': ple_w_gate, 'ple_b_gate': ple_b_gate, 'ple_w_proj': ple_w_proj,
            'fox_w_in': fox_w_in, 'fox_b_f': fox_b_f, 'fox_w_o': fox_w_o,
            'mla_w_dq': mla_w_dq, 'mla_q_norm': mla_q_norm, 'mla_w_uq': mla_w_uq, 'mla_w_o': mla_w_o,
            'kv_w_down': kv_w_down, 'kv_norm': kv_norm, 'kv_w_up': kv_w_up}

def second_block(x, p, ffn1_w_in, ffn1_w_out, ffn2_w_in, ffn2_w_out, ln_g, ln_b,
              ple_w_gate, ple_b_gate, ple_w_proj, fox_w_in, fox_b_f, fox_w_o,
              mla_w_dq, mla_q_norm, mla_w_uq, mla_w_o, kv_w_down, kv_norm, kv_w_up):
    S = x.shape[1]
    cos, sin = rope_tables(S)
    k_nope = k_rope = v_shared = None
    for i in range(DEPTH_2):
        if i == N_A:
            k_nope, k_rope, v_shared = shared_kv(x, kv_w_down, kv_norm, kv_w_up, cos, sin)
        x = post_norm(x, 0.5 * swiglu_2(x, ffn1_w_in[i], ffn1_w_out[i]), ln_g[i, 0], ln_b[i, 0])
        if i < N_A:
            mix = fox_mixer(x, fox_w_in[i], fox_b_f[i], fox_w_o[i])
        else:
            j = i - N_A
            mix = mla_mixer(x, mla_w_dq[j], mla_q_norm[j], mla_w_uq[j], mla_w_o[j],
                            k_nope, k_rope, v_shared, cos, sin)
        x = post_norm(x, mix, ln_g[i, 1], ln_b[i, 1])
        x = post_norm(x, 0.5 * swiglu_2(x, ffn2_w_in[i], ffn2_w_out[i]), ln_g[i, 2], ln_b[i, 2])
        gate = jax.nn.sigmoid((x @ ple_w_gate[i] + ple_b_gate[i]).astype(jnp.float32)).astype(x.dtype)
        x = post_norm(x, gate * (p[i] @ ple_w_proj[i]), ln_g[i, 3], ln_b[i, 3])
    return x


def setup_inputs(seed=0):
    out = dict(first_inputs(seed))
    for name, value in second_inputs(seed + 1).items():
        if name != "x":
            out[name + "_2"] = value
    return out


def reference(
    x, ffn1_norm, ffn1_w_gu, ffn1_w_down, mix_norm, w_in, cmp_pos_k, cmp_pos_v, cmp_k_w1,
    cmp_k_w2, cmp_v_w1, cmp_v_w2, hgrn_lower_bound, hgrn_out_norm, w_out, ffn2_norm, ffn2_w_gu,
    ffn2_w_down, final_norm, p_2, ffn1_w_in_2, ffn1_w_out_2, ffn2_w_in_2, ffn2_w_out_2, ln_g_2,
    ln_b_2, ple_w_gate_2, ple_b_gate_2, ple_w_proj_2, fox_w_in_2, fox_b_f_2, fox_w_o_2,
    mla_w_dq_2, mla_q_norm_2, mla_w_uq_2, mla_w_o_2, kv_w_down_2, kv_norm_2, kv_w_up_2,
):
    x = first_block(
        x, ffn1_norm, ffn1_w_gu, ffn1_w_down, mix_norm, w_in, cmp_pos_k, cmp_pos_v, cmp_k_w1,
        cmp_k_w2, cmp_v_w1, cmp_v_w2, hgrn_lower_bound, hgrn_out_norm, w_out, ffn2_norm,
        ffn2_w_gu, ffn2_w_down, final_norm,
    )
    return second_block(
        x, p_2, ffn1_w_in_2, ffn1_w_out_2, ffn2_w_in_2, ffn2_w_out_2, ln_g_2, ln_b_2,
        ple_w_gate_2, ple_b_gate_2, ple_w_proj_2, fox_w_in_2, fox_b_f_2, fox_w_o_2, mla_w_dq_2,
        mla_q_norm_2, mla_w_uq_2, mla_w_o_2, kv_w_down_2, kv_norm_2, kv_w_up_2,
    )


_drawn_inputs = setup_inputs


def setup_inputs(seed=0):
    import zlib

    import numpy as np

    out = dict(_drawn_inputs(seed))
    spreads = {}
    factors = {'ffn1_norm': 5.764,
     'mix_norm': 4.595,
     'cmp_pos_k': 8.0,
     'cmp_pos_v': 22.148,
     'hgrn_out_norm': 7.341,
     'ffn2_norm': 8.0,
     'final_norm': 2.926,
     'ple_b_gate_2': 8.0,
     'fox_b_f_2': 44.448,
     'mla_q_norm_2': 8.0,
     'kv_norm_2': 8.0}
    for name, (base, spread) in spreads.items():
        noise = np.random.default_rng([zlib.crc32(name.encode()), seed]).standard_normal(out[name].shape)
        drawn = base * np.exp(spread * noise) if base else spread * noise
        out[name] = __import__('jax').numpy.asarray(drawn.astype(out[name].dtype))
    for name, factor in factors.items():
        out[name] = (out[name] * factor).astype(out[name].dtype)
    return out
```

```python
from contextlib import ExitStack

import numpy as np

import concourse.bass as bass
from concourse import mybir

F32 = mybir.dt.float32
F32R = mybir.dt.float32r
ALU = mybir.AluOpType
ACTF = mybir.ActivationFunctionType
AX_X = mybir.AxisListType.X

P = 128
SEQ = 256
TB = SEQ // P
D = 1024
KD = D // P
RMS_EPS = 1e-6
LN_EPS = 1e-5
ALPHA = (2 * 2) ** 0.25
MASKED = -1e30

FF_TILES = 22
GU = KD * 2 * P
FF_COLS = GU + D

HEADS = 8
GROUPS = 2
HD = 64
CMP_LEN = 32
STRIDE = 16
NB = SEQ // STRIDE - 1
CMP_HID = 256
LP = CMP_LEN // 2
GATES = HEADS * 3
VSW = 2 * GROUPS * HD + GATES

HG = 4
CH = 16
CPB = P // CH
F_FLOOR = 1e-30
LN_SPLIT = 2.0 ** 50
LN_RANGE = 2.0 ** -50

FOX_H = 16
MLA_H = 16
QL = 384
KL = 256
ROPE = 64

CHUNK = 3072
RAW_SLOTS = 4

CONST_COLS = {}
_at = 0
for _name, _n in (("ident", P), ("causal", 3 * P), ("dist", 3 * P), ("cmp_dist", TB * NB),
                  ("cmp_row", TB), ("chunk_pair", P), ("chunk_row", CPB), ("restart", SEQ),
                  ("mean", P), ("cos", SEQ), ("sin", SEQ)):
    CONST_COLS[_name] = (_at, _n)
    _at += _n
N_CONST = _at + _at % 2


def const_table():
    t = np.zeros((P, N_CONST), np.float32)

    def put(name, value):
        a, n = CONST_COLS[name]
        t[:value.shape[0], a:a + n] = value.reshape(value.shape[0], n)

    put("ident", np.eye(P, dtype=np.float32))
    row = np.arange(P)[:, None]
    col = np.arange(P)[None, :]
    diag = np.where(col <= row, 0.0, MASKED).astype(np.float32)
    put("causal", np.concatenate([diag, np.zeros((P, P), np.float32), diag], 1))
    near = np.where(col <= row, row - col, 1e33).astype(np.float32)
    put("dist", np.concatenate([near, (row + P - col).astype(np.float32), near], 1))
    tok = np.arange(SEQ).reshape(TB, P).T
    end = np.arange(NB) * STRIDE + CMP_LEN - 1
    away = tok[:, :, None] - end[None, None, :]
    put("cmp_dist", np.where(away >= 0, away, 1e33).astype(np.float32))
    put("cmp_row", (tok >= CMP_LEN - 1).astype(np.float32))
    put("chunk_pair", ((row // CH == col // CH) & (row <= col)).astype(np.float32))
    put("chunk_row", (row // CH == np.arange(CPB)[None, :]).astype(np.float32))
    put("restart", np.broadcast_to((np.arange(SEQ) % CH != 0).astype(np.float32), (P, SEQ)))
    put("mean", np.full((P, P), 1.0 / P, np.float32))
    inv = np.float32(10000.0) ** (-np.arange(ROPE // 2, dtype=np.float32) * np.float32(2.0 / ROPE))
    ang = (np.arange(SEQ, dtype=np.float32)[:, None] * inv[None, :]).astype(np.float32)
    cos, sin = np.cos(ang).T.astype(np.float32), np.sin(ang).T.astype(np.float32)
    put("cos", np.concatenate([cos, cos, cos, cos], 0))
    put("sin", np.concatenate([-sin, sin, -sin, sin], 0))
    return t


class Engine:

    def __init__(self, queue, semaphore):
        self.queue, self.semaphore = queue, semaphore
        self.count = 0
        self.waited = {}

    def after(self, *marks):
        for who, value in marks:
            if self.waited.get(id(who), 0) < value:
                self.queue.wait_ge(who.semaphore, value)
                self.waited[id(who)] = value
        return self.queue

    def done(self, instruction, by=1):
        instruction.then_inc(self.semaphore, by)
        self.count += by
        return (self, self.count)


class WeightStream:

    def __init__(self, sp, act, dve, raw, hi, lo, slot_loads):
        self.sp, self.act, self.dve = sp, act, dve
        self.raw, self.hi, self.lo = raw, hi, lo
        self.slot_loads = slot_loads
        self.chunks = []
        self.loaded = {}
        self.raw_free = {}
        self.split_at = {}
        self.released = {}
        self.n_loaded = 0
        self.at = 0
        self.seq = []

    def add(self, source, cols, split=True):
        self.chunks.append((source, cols, split))
        if split:
            self.seq.append(len(self.chunks) - 1)

    def load(self, i, *free):
        if i >= len(self.chunks):
            return
        source, cols, _ = self.chunks[i]
        slot = i % RAW_SLOTS
        loads = self.slot_loads[slot]
        queue = self.sp.after(*free)
        self.loaded[i] = loads.done(queue.dma_start(self.raw[slot][:, 0:cols], source), 16)

    def start(self):
        for i in range(RAW_SLOTS):
            self.load(i)

    def pair(self, i):
        return self.seq.index(i) % 2

    def split(self, i, a, b, *free, last=False):
        if i >= len(self.chunks):
            return
        raw = self.raw[i % RAW_SLOTS][:, a:b]
        hi, lo = self.hi[self.pair(i)][:, a:b], self.lo[self.pair(i)][:, a:b]
        h = self.act.done(self.act.after(self.loaded[i], *free).activation(hi, raw, ACTF.Copy))
        l = self.dve.done(self.dve.after(self.loaded[i], h, *free).tensor_tensor(
            lo, raw, hi.bitcast(F32), ALU.subtract))
        self.split_at.setdefault(i, []).append((a, b, h, l))
        if last:
            self.load(i + RAW_SLOTS, h, l)

    def split_whole(self, i):
        if i >= len(self.chunks) or not self.chunks[i][2] or i in self.split_at:
            return
        cols = self.chunks[i][1]
        k = self.seq.index(i)
        free = self.released.get(self.seq[k - 2], ()) if k >= 2 else ()
        half = cols // 4 * 2
        self.split(i, 0, half, *free)
        self.split(i, half, cols, *free, last=True)

    def take(self):
        i = self.at
        self.at += 1
        if not self.chunks[i][2]:
            self.split_whole(i + 1)
            return i, self.raw[i % RAW_SLOTS], None, (self.loaded[i],)
        self.split_whole(i)
        self.split_whole(i + 1)
        return i, self.hi[self.pair(i)], self.lo[self.pair(i)], tuple(m for s in self.split_at[i] for m in s[2:])

    def release(self, i, mark):
        self.released[i] = (mark,)
        if not self.chunks[i][2]:
            self.load(i + RAW_SLOTS, mark)


def build(nc, t, out, stop=99):
    with ExitStack() as ctx:
        def sb(name, shape, dt=F32):
            return ctx.enter_context(nc.sbuf_tensor(name, shape, dt))

        def counter(queue, name):
            return Engine(queue, ctx.enter_context(nc.semaphore(name)))

        pe = counter(nc.tensor, "pe_done")
        act = counter(nc.scalar, "act_done")
        dve = counter(nc.vector, "dve_done")
        pool = counter(nc.gpsimd, "pool_done")
        sp = counter(nc.sync, "sp_done")
        slot_loads = [counter(None, f"weights_landed_{i}") for i in range(RAW_SLOTS)]
        small_landed = counter(None, "small_landed")
        gains_landed = counter(None, "gains_landed")
        out_landed = counter(None, "out_landed")

        raw = [sb(f"w_raw{i}", [P, CHUNK]) for i in range(RAW_SLOTS)]
        w_hi = [sb(f"w_hi{i}", [P, CHUNK], F32R) for i in range(2)]
        w_lo = [sb(f"w_lo{i}", [P, CHUNK], F32R) for i in range(2)]
        x = sb("x", [P, TB, D])
        xn = sb("xn", [P, TB, D])
        xT_hi = sb("xT_hi", [P, KD, SEQ], F32R)
        xT_lo = sb("xT_lo", [P, KD, SEQ], F32R)
        gains = sb("gains", [P, 2 * D])
        const = sb("const", [P, N_CONST])
        sig = [sb(f"ff_silu{i}", [P, SEQ]) for i in range(2)]
        hT_hi = [sb(f"hT_hi{i}", [P, SEQ], F32R) for i in range(2)]
        hT_lo = [sb(f"hT_lo{i}", [P, SEQ], F32R) for i in range(2)]
        stats = sb("stats", [P, TB, 2, 6])
        mv = sb("mean_var", [P, TB, 2])
        rstd = sb("rstd", [P, TB])
        expo = sb("minus_half", [P, SEQ])
        small = sb("small", [P, 64])
        psum = [ctx.enter_context(nc.psum_tensor(f"bank{i}", [P, 512], F32)) for i in range(8)]
        psum_read = [() for _ in range(8)]

        def cst(name, rows=P):
            a, n = CONST_COLS[name]
            return const[0:rows, a:a + n]

        ident = cst("ident")
        c_mark = small_landed.done(sp.after().dma_start(const[:, :], t["const"]), 16)
        x_mark = small_landed.done(sp.after().dma_start(x[:, :, :], t["x"].rearrange("(b p) d -> p b d", p=P)), 16)
        SMALL = {"lb": (0, HG), "out_norm": (HG, 1), "b_f": (HG + 1, 1)}
        s_mark = small_landed.done(sp.after().dma_start(small[:, 0:HG + 2], t["small"]), 16)
        c_mark = x_mark = s_mark
        minus_half = pool.done(pool.after().memset(expo[:, :], -0.5))

        stream = WeightStream(sp, act, dve, raw, w_hi, w_lo, slot_loads)
        ws = stream

        def add_all(name, split=True):
            n, _, cols = t[name].shape
            for i in range(n):
                ws.add(t[name][i, :, :], cols, split)

        for name, split in (("ffn_a", True), ("nsa_cmp_in", True), ("cmp_w1", False), ("nsa_qk", True),
                            ("nsa_v", True), ("hg_v", True), ("hg", True), ("w_out1", True),
                            ("w_out2", True), ("ffn_b", True),
                            ("ffn_c", True), ("fox_v", True), ("fox_f", True), ("fox_qk", True),
                            ("fox_o1", True), ("fox_o2", True), ("ffn_d", True), ("ple0_p", True),
                            ("ple0_g1", True), ("ple0_g2", True),
                            ("kv_down1", True), ("kv_down2", True), ("ffn_e", True), ("mla_dq", True),
                            ("mla_up", True), ("mla_o1", True), ("mla_o2", True), ("ffn_f", True), ("ple1_p", True),
                            ("ple1_g1", True), ("ple1_g2", True)):
            add_all(name, split)
        ws.start()

        everyone = (pe, act, dve, pool)

        def meet():
            marks = [(e, e.count) for e in everyone if e.count]
            for e in everyone:
                e.after(*(m for m in marks if m[0] is not e))

        def bank_for(i):
            pe.after(*psum_read[i])
            psum_read[i] = ()
            return psum[i]

        def read_by(i, *marks):
            psum_read[i] = psum_read[i] + marks

        def feature_major(o, hi, lo, cols, k_tiles, a_hi, a_lo):
            last = 3 * k_tiles - 1
            n = 0
            for k in range(k_tiles):
                c = slice(cols(k), cols(k) + P)
                for w, a in ((hi, a_hi), (hi, a_lo), (lo, a_hi)):
                    ins = nc.tensor.matmul(o, w[:, c], a[:, k, :], start=(n == 0), stop=(n == last))
                    n += 1
            return ins

        def token_major(o, hi, lo, cols, width, ks, a_hi, a_lo, b, first, final):
            total = 3 * len(ks)
            n = 0
            for j, k in enumerate(ks):
                c = slice(cols(j), cols(j) + width)
                tok = slice(b * P, (b + 1) * P)
                for a, w in ((a_hi, hi), (a_lo, hi), (a_hi, lo)):
                    ins = nc.tensor.matmul(o, a(k)[:, tok], w[:, c], start=(first and n == 0),
                                           stop=(final and n == total - 1))
                    n += 1
            return ins

        ACC = (0, 1, 2, 3)
        SPARE = (4, 5, 6, 7)

        def load_gains(row):
            src = t["gains"][row:row + 1, :].to_broadcast([P, 2 * D])
            return gains_landed.done(sp.after(*gains_read[0]).dma_start(gains[:, :], src), 16)

        gains_read = [()]

        def statistics(src, width, b, ready, eps):
            n = max(1, width // 512)
            w = width // n
            for j in range(n):
                m = dve.done(dve.after(*ready).bn_stats(out=stats[:, b, j, :], in_=src[:, j * w:(j + 1) * w]))
            m = dve.done(dve.after(m).bn_aggr(out=mv[:, b, :], in_=stats[:, b, 0:n, :]))
            return m

        def root(b, var, ready, eps):
            m = dve.done(dve.after(*ready).tensor_scalar(rstd[:, b:b + 1], var, eps, None, ALU.add))
            return pool.done(pool.after(m, minus_half).tensor_tensor(
                rstd[:, b:b + 1], rstd[:, b:b + 1], expo[:, 0:1], ALU.pow))

        def rms_rows(src, dst, gain, width, b, ready, free):
            m = statistics(src, width, b, ready, RMS_EPS)
            m = dve.done(dve.after(m).scalar_tensor_tensor(
                rstd[:, b:b + 1], mv[:, b, 0:1], mv[:, b, 0:1], mv[:, b, 1:2], ALU.mult, ALU.add))
            m = root(b, rstd[:, b:b + 1], (m,), RMS_EPS)
            return dve.done(dve.after(m, *free).scalar_tensor_tensor(
                dst, src, rstd[:, b:b + 1], gain, ALU.mult, ALU.mult))

        def ln_rows(src, dst, b, ready, free):
            m = statistics(src, D, b, ready, LN_EPS)
            m = root(b, mv[:, b, 1:2], (m,), LN_EPS)
            m = dve.done(dve.after(m, *free).tensor_scalar(dst, src, mv[:, b, 0:1], rstd[:, b:b + 1],
                                                           ALU.subtract, ALU.mult))
            m = dve.done(dve.after(m).tensor_tensor(dst, dst, gains[:, 0:D], ALU.mult))
            return dve.done(dve.after(m).tensor_tensor(dst, dst, gains[:, D:2 * D], ALU.add))

        def turn(src, ready, kts, dst_hi, dst_lo, free):
            marks = []
            for j in range(0, kts, 2):
                bank = SPARE[j // 2 % 4]
                o = bank_for(bank)
                n = min(2, kts - j)
                for i in range(n):
                    for b in range(TB):
                        pe.after(ready[b])
                        ins = nc.tensor.transpose(o[:, i * SEQ + b * P:i * SEQ + (b + 1) * P],
                                                  src(b)[:, (j + i) * P:(j + i + 1) * P], ident)
                turned = pe.done(ins)
                flat = lambda z: z[:, j:j + n, :].rearrange("p k s -> p (k s)")
                h = act.done(act.after(turned, *free).activation(flat(dst_hi), o[:, 0:n * SEQ], ACTF.Copy))
                l = dve.done(dve.after(turned, h).tensor_tensor(
                    flat(dst_lo), o[:, 0:n * SEQ], flat(dst_hi).bitcast(F32), ALU.subtract))
                read_by(bank, h, l)
                marks += [h, l]
            return tuple(marks)

        def split_to(hi, lo, src, ready, free=()):
            h = act.done(act.after(*ready, *free).activation(hi, src, ACTF.Copy))
            l = dve.done(dve.after(h, *ready, *free).tensor_tensor(lo, src, hi.bitcast(F32), ALU.subtract))
            return h, l

        def ffn(xT_ready):
            first = ws.at
            n = FF_TILES
            ws.at += n
            h_ready = {}
            h_read = {}
            down = {}

            def gate_up(i):
                c = first + i
                w = ws.pair(c)
                bank = SPARE[i % 4]
                o = bank_for(bank)
                pe.after(*xT_ready, *(m for s in ws.split_at[c] if s[0] < GU for m in s[2:]))
                feature_major(o[:, 0:SEQ], w_hi[w], w_lo[w], lambda k: 2 * P * k, KD, xT_hi, xT_lo)
                return pe.done(feature_major(o[:, SEQ:2 * SEQ], w_hi[w], w_lo[w],
                                             lambda k: 2 * P * k + P, KD, xT_hi, xT_lo))

            def activate(i, made):
                bank = SPARE[i % 4]
                o = psum[bank]
                s = i % 2
                free = (h_read[i - 2],) if i >= 2 else ()
                a = act.done(act.after(made, *free).activation(sig[s][:, :], o[:, 0:SEQ], ACTF.Silu))
                m = dve.done(dve.after(a).tensor_tensor(sig[s][:, :], sig[s][:, :], o[:, SEQ:2 * SEQ], ALU.mult))
                read_by(bank, a, m)
                h, l = split_to(hT_hi[s][:, :], hT_lo[s][:, :], sig[s][:, :], (m,), free)
                h_ready[i] = (h, l)

            def down_product(i):
                c = first + i
                w = ws.pair(c)
                s = i % 2
                if i == 0:
                    for a in ACC:
                        bank_for(a)
                pe.after(*h_ready[i], *(m for q in ws.split_at[c] if q[1] > GU for m in q[2:]))
                for b in range(TB):
                    for half in range(2):
                        ins = token_major(psum[ACC[2 * b + half]][:, :], w_hi[w], w_lo[w],
                                          lambda j: GU + 512 * half, 512, (0,),
                                          lambda k: hT_hi[s], lambda k: hT_lo[s], b, i == 0, i == n - 1)
                h_read[i] = pe.done(ins)
                down[i] = h_read[i]
                ws.released[c] = (h_read[i],)

            made = {}
            ws.split_whole(first)
            for i in range(n):
                c = first + i
                made[i] = gate_up(i)
                if i + 1 < n:
                    free = (made[i - 1],) if i >= 1 else ws.released.get(c - 1, ())
                    ws.split(c + 1, 0, GU // 2, *free)
                    ws.split(c + 1, GU // 2, GU, *free)
                activate(i, made[i])
                if i >= 1:
                    down_product(i - 1)
                if i + 1 < n:
                    free = (down[i - 1],) if i >= 1 else ws.released.get(c - 1, ())
                    ws.split(c + 1, GU, FF_COLS, *free, last=True)
            ws.split_whole(first + n)
            down_product(n - 1)
            return down[n - 1]

        def out_product(a_hi, a_lo, ready, n_chunks, k_tiles, per=3):
            for a in ACC:
                bank_for(a)
            k = 0
            for _ in range(n_chunks):
                i, hi, lo, there = ws.take()
                ks = list(range(k, min(k + per, k_tiles)))
                pe.after(*there)
                for b in range(TB):
                    for half in range(2):
                        for kk in ks:
                            pe.after(*(ready[kk] if isinstance(ready, dict) else ready))
                        ins = token_major(psum[ACC[2 * b + half]][:, :], hi, lo,
                                          lambda j: D * j + 512 * half, 512, ks, a_hi, a_lo,
                                          b, k == 0, ks[-1] == k_tiles - 1)
                done = pe.done(ins)
                ws.release(i, done)
                k += per
            return done

        def bcast(ap, axis, shape):
            return ap.unsqueeze(axis).to_broadcast(shape)

        def feature_tiles(n, banks, ready, sinks, a_hi=None, a_lo=None, k_tiles=KD):
            i, hi, lo, there = ws.take()
            pe.after(*there, *ready)
            for j in range(n):
                bank = banks[j % len(banks)]
                o = bank_for(bank)
                m = pe.done(feature_major(o[:, 0:SEQ], hi, lo, lambda k: (n * k + j) * P, k_tiles,
                                          a_hi or xT_hi, a_lo or xT_lo))
                read_by(bank, *sinks[j](o[:, 0:SEQ], m))
            ws.release(i, m)

        def token_tiles(width, banks, ready, sink, a_hi=None, a_lo=None, k_tiles=KD):
            i, hi, lo, there = ws.take()
            pe.after(*there, *ready)
            for b in range(TB):
                bank = banks[b % len(banks)]
                o = bank_for(bank)
                m = pe.done(token_major(o[:, 0:width], hi, lo, lambda k: width * k, width, range(k_tiles),
                                        lambda k: (a_hi or xT_hi)[:, k, :], lambda k: (a_lo or xT_lo)[:, k, :],
                                        b, True, True))
                read_by(bank, *sink(b, o[:, 0:width], m))
            ws.release(i, m)

        def keep(dst, scale=1.0, free=(), on=None):
            def sink(o, m):
                c = act.done(act.after(m, *free).activation(dst, o, ACTF.Copy, scale=scale))
                kept.append(c)
                return (c,)
            return sink

        kept = []

        def skewed(n, *stages):
            for step in range(n + len(stages) - 1):
                for s, stage in enumerate(stages):
                    if 0 <= step - s < n:
                        stage(step - s)

        def nsa(xT_ready, oT_hi, oT_lo):
            with ExitStack() as scope:
                def tile(name, shape, dt=F32):
                    return scope.enter_context(nc.sbuf_tensor("nsa_" + name, shape, dt))

                q = tile("q", [P, HEADS // 2, SEQ])
                keys = tile("keys", [P, 2 * GROUPS, SEQ])
                vals = tile("vals", [P, TB, VSW])
                pairs = tile("pairs", [P, 2 * GROUPS, SEQ])
                blocks = tile("blocks", [P, 2, LP, GROUPS * NB])
                pos = tile("pos", [P, 2, LP])
                w2 = tile("w2", [P, 2, 2, P])
                hid = tile("hid", [P, 2, CMP_HID])
                hidT = tile("hidT", [P, 2, 2, GROUPS * NB])
                k_cmp = tile("k_cmp", [P, GROUPS * NB])
                v_cmp = tile("v_cmp", [P, GROUPS, HD])
                gates = tile("gates", [P, TB, GATES])
                s1 = [tile(f"s1_{i}", [P, 2, SEQ]) for i in range(2)]
                s0 = [tile(f"s0_{i}", [P, 2, P]) for i in range(2)]
                sc = [tile(f"sc_{i}", [P, TB, NB]) for i in range(2)]
                pT = [tile(f"pT_{i}", [P, 1024]) for i in range(2)]
                nm = [tile(f"nm_{i}", [P, 6]) for i in range(2)]
                sums = [tile(f"sums_{i}", [P, 6]) for i in range(2)]
                wgt = [tile(f"wgt_{i}", [P, 6]) for i in range(2)]

                landed = small_landed.done(sp.after().dma_start(pos[:, :, :], t["cmp_pos"]), 16)
                landed = small_landed.done(sp.after().dma_start(w2[:, :, :, :], t["cmp_w2"]), 16)

                def pair_sink(i):
                    def sink(o, m):
                        a = act.done(act.after(m).activation(pairs[0:64, i, :], o[0:64, :], ACTF.Copy))
                        b = act.done(act.after(m).activation(pairs[64:P, i, 0:SEQ - 1], o[64:P, 1:SEQ], ACTF.Copy))
                        z = act.done(act.after(m).activation(pairs[64:P, i, SEQ - 1:SEQ], o[64:P, SEQ - 1:SEQ], ACTF.Copy))
                        kept.append(z)
                        return (z,)
                    return sink

                feature_tiles(3, SPARE, xT_ready, [pair_sink(0), pair_sink(1), pair_sink(2)])
                feature_tiles(3, SPARE, xT_ready, [pair_sink(3), keep(keys[:, 0, :]), keep(keys[:, 1, :])])
                for kv in range(2):
                    for g in range(GROUPS):
                        row = pairs[:, 2 * kv + g, :]
                        for part in range(2):
                            lp = slice(part * LP // 2, (part + 1) * LP // 2)
                            v = row[:, STRIDE * part:STRIDE * (part + NB)].rearrange(
                                "p (b l two) -> p l b two", l=LP // 2, two=2)[:, :, :, 0]
                            m = dve.done(dve.after(landed, *kept).tensor_tensor(
                                blocks[:, kv, lp, g * NB:(g + 1) * NB], v,
                                bcast(pos[:, kv, lp], 2, [P, LP // 2, NB]), ALU.add))
                blocks_ready = m
                for kv in range(2):
                    o = bank_for(ACC[kv])
                    for part in range(2):
                        i, w, _, there = ws.take()
                        pe.after(blocks_ready, *there)
                        for j in range(LP // 2):
                            lp = part * LP // 2 + j
                            ins = nc.tensor.matmul(o[0:GROUPS * NB, 0:CMP_HID], blocks[:, kv, lp, :],
                                                   w[:, j * CMP_HID:(j + 1) * CMP_HID],
                                                   start=(lp == 0), stop=(lp == LP - 1))
                        m = pe.done(ins)
                        ws.release(i, m)
                    m = act.done(act.after(m).activation(hid[0:GROUPS * NB, kv, :],
                                                         o[0:GROUPS * NB, 0:CMP_HID], ACTF.Gelu_apprx_tanh))
                    read_by(ACC[kv], m)
                hid_ready = m
                feature_tiles(3, SPARE, xT_ready, [keep(keys[:, 2, :]), keep(keys[:, 3, :]), keep(q[:, 0, :], HD ** -0.5)])
                feature_tiles(3, SPARE, xT_ready, [keep(q[:, j, :], HD ** -0.5) for j in (1, 2, 3)])

                o = bank_for(ACC[2])
                pe.after(hid_ready)
                n = GROUPS * NB
                for kv in range(2):
                    for h in range(2):
                        ins = nc.tensor.transpose(o[:, (2 * kv + h) * n:(2 * kv + h + 1) * n],
                                                  hid[0:n, kv, h * P:(h + 1) * P], ident[0:n, 0:n])
                m = pe.done(ins)
                m = dve.done(dve.after(m).tensor_copy(hidT[:, :, :, :].rearrange("p a b c -> p (a b c)"), o[:, 0:4 * n]))
                read_by(ACC[2], m)
                o = bank_for(ACC[3])
                pe.after(m)
                for h in range(2):
                    ins = nc.tensor.matmul(o[:, 0:n], w2[:, 0, h, :], hidT[:, 0, h, :], start=(h == 0), stop=(h == 1))
                m = pe.done(ins)
                kc_ready = act.done(act.after(m).activation(k_cmp[:, :], o[:, 0:n], ACTF.Copy))
                read_by(ACC[3], kc_ready)
                o = bank_for(ACC[3])
                for g in range(GROUPS):
                    for h in range(2):
                        ins = nc.tensor.matmul(o[0:NB, g * HD:(g + 1) * HD], hidT[:, 1, h, g * NB:(g + 1) * NB],
                                               w2[:, 1, h, 0:HD], start=(h == 0), stop=(h == 1))
                m = pe.done(ins)
                vc_ready = act.done(act.after(m).activation(
                    v_cmp[0:NB, :, :].rearrange("p g d -> p (g d)"), o[0:NB, 0:GROUPS * HD], ACTF.Copy))
                read_by(ACC[3], vc_ready)

                def vals_sink(b, o, m):
                    c = act.done(act.after(m).activation(vals[:, b, :], o, ACTF.Copy))
                    kept.append(c)
                    return (c,)
                token_tiles(VSW, SPARE, xT_ready, vals_sink)
                m = act.done(act.after(*kept).activation(gates[:, :, :], vals[:, :, VSW - GATES:VSW], ACTF.Sigmoid))
                cmp_gates = gates[:, :, :].rearrange("p b (h three) -> p b h three", three=3)[:, :, :, 0]
                gates_ready = dve.done(dve.after(m).tensor_tensor(
                    cmp_gates, cmp_gates, bcast(cst("cmp_row"), 2, [P, TB, HEADS]), ALU.mult))

                dist = cst("dist")
                cmp_dist = cst("cmp_dist").rearrange("p (b n) -> p b n", b=TB)
                made, soft, turned, read = {}, {}, {}, {}

                def scores(h):
                    g, half, base = h // 4, h // 2, 64 * (h % 2)
                    rows = slice(base, base + HD)
                    a, b = (0, 1) if h % 2 == 0 else (2, 3)
                    oa, ob = bank_for(a), bank_for(b)
                    pe.after(*kept, kc_ready)
                    q0, q1 = q[rows, half, 0:P], q[rows, half, P:SEQ]
                    for i, kk in enumerate((g, 2 + g)):
                        nc.tensor.matmul(oa[:, i * SEQ:(i + 1) * SEQ], q1, keys[rows, kk, :], start=True, stop=True)
                    for i, kk in enumerate((g, 2 + g)):
                        nc.tensor.matmul(ob[:, i * P:(i + 1) * P], q0, keys[rows, kk, 0:P], start=True, stop=True)
                    for i, qq in enumerate((q0, q1)):
                        ins = nc.tensor.matmul(ob[:, 2 * P + i * NB:2 * P + (i + 1) * NB], qq,
                                               k_cmp[rows, g * NB:(g + 1) * NB], start=True, stop=True)
                    made[h] = pe.done(ins)

                def softmax(h):
                    a, b = (0, 1) if h % 2 == 0 else (2, 3)
                    oa, ob = psum[a], psum[b]
                    z = h % 2
                    slope = -2.0 ** (-(h + 1))
                    free = (turned[h - 2],) if h >= 2 else ()
                    dve.after(made[h], *free)
                    m = dve.done(nc.vector.scalar_tensor_tensor(
                        s1[z][:, :, :], bcast(dist[:, P:3 * P], 1, [P, 2, SEQ]), slope,
                        oa[:, :].rearrange("p (a s) -> p a s", a=2), ALU.mult, ALU.add))
                    read_by(a, m)
                    nc.vector.scalar_tensor_tensor(
                        s0[z][:, :, :], bcast(dist[:, 0:P], 1, [P, 2, P]), slope,
                        ob[:, 0:2 * P].rearrange("p (a s) -> p a s", a=2), ALU.mult, ALU.add)
                    m = dve.done(nc.vector.scalar_tensor_tensor(
                        sc[z][:, :, :], cmp_dist, slope,
                        ob[:, 2 * P:2 * P + TB * NB].rearrange("p (a s) -> p a s", a=TB), ALU.mult, ALU.add))
                    read_by(b, m)
                    parts = [(s1[z], 0), (s0[z], 2), (sc[z], 4)]
                    dve.after(m)
                    for s, c in parts:
                        m = dve.done(nc.vector.tensor_reduce(nm[z][:, c:c + 2], s[:, :, :], AX_X, ALU.max, negate=True))
                    act.after(m)
                    for s, c in parts:
                        for i in range(2):
                            m = act.done(nc.scalar.activation(s[:, i, :], s[:, i, :], ACTF.Exp,
                                                              bias=nm[z][:, c + i:c + i + 1],
                                                              accum_out=sums[z][:, c + i:c + i + 1]))
                    m = dve.done(dve.after(m).reciprocal(sums[z][:, :], sums[z][:, :]))
                    dve.after(m, gates_ready)
                    for c, gate in ((0, gates[:, 1, 3 * h + 1:3 * h + 3]), (2, gates[:, 0, 3 * h + 1:3 * h + 3]),
                                    (4, gates[:, :, 3 * h])):
                        m = dve.done(nc.vector.tensor_tensor(wgt[z][:, c:c + 2], sums[z][:, c:c + 2], gate, ALU.mult))
                    dve.after(m)
                    for (s, c), w in zip(parts, (SEQ, P, NB)):
                        m = dve.done(nc.vector.tensor_tensor(s[:, :, :], s[:, :, :],
                                                             bcast(wgt[z][:, c:c + 2], 2, [P, 2, w]), ALU.mult))
                    soft[h] = m

                def transposes(h):
                    z = h % 2
                    oc, od = bank_for(4), bank_for(5)
                    pe.after(soft[h])
                    for i in range(2):
                        nc.tensor.transpose(oc[:, i * SEQ:i * SEQ + P], s0[z][:, i, :], ident)
                        nc.tensor.transpose(oc[:, i * SEQ + P:(i + 1) * SEQ], s1[z][:, i, 0:P], ident)
                        nc.tensor.transpose(od[:, i * P:(i + 1) * P], s1[z][:, i, P:SEQ], ident)
                    for i in range(TB):
                        ins = nc.tensor.transpose(od[0:NB, SEQ + i * P:SEQ + (i + 1) * P], sc[z][:, i, :], ident)
                    turned[h] = pe.done(ins)
                    free = (read[h - 2],) if h >= 2 else ()
                    act.after(turned[h], *free)
                    m = act.done(nc.scalar.activation(pT[z][:, 0:512], oc[:, :], ACTF.Copy))
                    read_by(4, m)
                    dve.after(turned[h], *free)
                    nc.vector.tensor_copy(pT[z][:, 512:512 + SEQ], od[:, 0:SEQ])
                    d = dve.done(nc.vector.tensor_copy(pT[z][0:NB, 768:1024], od[0:NB, SEQ:512]))
                    read_by(5, d)
                    soft[h] = (m, d)

                def values(h):
                    g, half, base, z = h // 4, h // 2, 64 * (h % 2), h % 2
                    rows = slice(base, base + HD)
                    bank = 6 + h % 2
                    o = bank_for(bank)[rows, 0:SEQ]
                    pe.after(*soft[h], vc_ready)
                    p = pT[z]
                    for i in range(2):
                        c = slice((2 * i + g) * HD, (2 * i + g + 1) * HD)
                        nc.tensor.matmul(o, vals[:, 0, c], p[:, i * SEQ:(i + 1) * SEQ], start=(i == 0), stop=False)
                        nc.tensor.matmul(o[:, P:SEQ], vals[:, 1, c], p[:, 512 + i * P:512 + (i + 1) * P],
                                         start=False, stop=False)
                    read[h] = pe.done(nc.tensor.matmul(o, v_cmp[0:NB, g, :], p[0:NB, 768:1024], start=False, stop=True))
                    hi, lo = oT_hi[rows, half, :], oT_lo[rows, half, :]
                    m = split_to(hi, lo, o, (read[h],))
                    read_by(bank, *m)
                    return m

                skewed(HEADS, lambda h: (scores(h), softmax(h)), transposes, values)
                kept.clear()
                meet()

        def hgrn(xT_ready, oT_hi, oT_lo):
            with ExitStack() as scope:
                def tile(name, shape, dt=F32):
                    return scope.enter_context(nc.sbuf_tensor("hg_" + name, shape, dt))

                v = tile("v", [P, TB, HG * P])
                qf, kf, gf, b_cum, tmp, tmp2, k_end, exp_b = (tile(n, [P, SEQ]) for n in (
                    "q", "k", "g", "b", "tmp", "tmp2", "k_end", "exp_b"))
                lbt = tile("lb", [P, 4 * HG])
                pair = [tile(f"pair{i}", [P, CH, P]) for i in range(2)]
                aT = [tile(f"aT{i}", [P, P]) for i in range(2)]
                vm = tile("v_masked", [P, CPB, P])
                keT = tile("k_endT", [P, P])
                state = tile("state", [P, CPB + 1, P])

                def v_sink(half):
                    def sink(b, o, m):
                        c = act.done(act.after(m).activation(v[:, b, half * SEQ:(half + 1) * SEQ], o, ACTF.Copy))
                        kept.append(c)
                        return (c,)
                    return sink
                for half in range(2):
                    token_tiles(SEQ, SPARE, xT_ready, v_sink(half))
                v_ready = tuple(kept)
                kept.clear()
                lb = small[:, 0:HG]
                lb_diff, lb_soft, lb_val, lb_rest = (lbt[:, i * HG:(i + 1) * HG] for i in range(4))
                m = dve.done(dve.after(s_mark).tensor_tensor(lb_diff, lb, lb, ALU.subtract))
                m = act.done(act.after(m).activation(lb_soft, lb_diff, ACTF.Exp))
                m = dve.done(dve.after(m).reciprocal(lb_val, lb_soft))
                m = dve.done(dve.after(m).tensor_tensor(lb_soft, lb_soft, lb_val, ALU.mult))
                m = dve.done(dve.after(m).tensor_tensor(lb_val, lb_soft, lb_soft, ALU.subtract))
                lb_ready = dve.done(dve.after(m).tensor_scalar(lb_rest, lb_val, -1.0, 1.0, ALU.mult, ALU.add))

                for h in range(HG):
                    fin = {}

                    def q_sink(o, m):
                        fin["q"] = act.done(act.after(m).activation(qf[:, :], o, ACTF.Silu))
                        return (fin["q"],)

                    def g_sink(o, m):
                        fin["g"] = act.done(act.after(m).activation(gf[:, :], o, ACTF.Silu))
                        return (fin["g"],)

                    def f_sink(o, m):
                        act.after(m)
                        nc.scalar.activation(tmp[:, :], o, ACTF.Sigmoid)
                        a = act.done(nc.scalar.activation(kf[:, :], o, ACTF.Sigmoid, scale=-1.0))
                        fin["f"] = a
                        return (a,)

                    feature_tiles(3, SPARE, xT_ready, [q_sink, f_sink, g_sink])
                    val, rest = lb_val[:, h:h + 1], lb_rest[:, h:h + 1]
                    dve.after(fin["f"], lb_ready)
                    nc.vector.tensor_scalar(kf[:, :], kf[:, :], rest, None, ALU.mult)
                    m = dve.done(nc.vector.tensor_scalar(tmp[:, :], tmp[:, :], rest, val, ALU.mult, ALU.add))
                    m = dve.done(dve.after(m).tensor_scalar(tmp[:, :], tmp[:, :], F_FLOOR, None, ALU.max))
                    m = dve.done(dve.after(m).tensor_scalar(tmp2[:, :], tmp[:, :], LN_SPLIT, 1.0, ALU.mult, ALU.min))
                    m = dve.done(dve.after(m).tensor_scalar(tmp[:, :], tmp[:, :], LN_RANGE, None, ALU.max))
                    act.after(m)
                    nc.scalar.activation(tmp[:, :], tmp[:, :], ACTF.Ln)
                    m = act.done(nc.scalar.activation(tmp2[:, :], tmp2[:, :], ACTF.Ln))
                    m = dve.done(dve.after(m).tensor_tensor(tmp[:, :], tmp[:, :], tmp2[:, :], ALU.add))
                    b_ready = dve.done(dve.after(m).tensor_tensor_scan(b_cum[:, :], cst("restart"), tmp[:, :], 0.0,
                                                                       ALU.mult, ALU.add))
                    chunks = b_cum[:, :].rearrange("p (c j) -> p c j", j=CH)
                    m = dve.done(dve.after(b_ready).tensor_tensor(
                        tmp2[:, :].rearrange("p (c j) -> p c j", j=CH),
                        chunks[:, :, CH - 1:CH].to_broadcast([P, TB * CPB, CH]), chunks, ALU.subtract))
                    act.after(m)
                    nc.scalar.activation(k_end[:, :], tmp2[:, :], ACTF.Exp)
                    m = act.done(nc.scalar.activation(exp_b[:, :], b_cum[:, :], ACTF.Exp))
                    dve.after(m, fin["q"])
                    nc.vector.tensor_tensor(tmp[:, :], qf[:, :], exp_b[:, :], ALU.mult)
                    m = dve.done(nc.vector.tensor_tensor(k_end[:, :], k_end[:, :], kf[:, :], ALU.mult))
                    decayed = m
                    o_bank = ACC[2 + h % 2]
                    state_read = ()
                    zero_ready = dve.done(dve.after((pe, pe.count)).memset(state[:, 0, :], 0.0))
                    o_psum = bank_for(o_bank)
                    for b in range(TB):
                        z = b
                        bb = chunks[:, b * CPB:(b + 1) * CPB, :]
                        later = bcast(bb.rearrange("p c j -> p j c"), 3, [P, CH, CPB, CH])
                        earlier = bcast(bb, 1, [P, CH, CPB, CH])
                        pz = pair[z][:, :, :].rearrange("p j (c s) -> p j c s", c=CPB)
                        for j in range(CH):
                            m = dve.done(dve.after(decayed).tensor_tensor(pz[:, j], later[:, j], earlier[:, j], ALU.subtract))
                        flat = pair[z][:, :, :].rearrange("p j s -> p (j s)")
                        m = dve.done(dve.after(m).tensor_scalar(flat, flat, 0.0, None, ALU.min))
                        m = act.done(act.after(m).activation(flat, flat, ACTF.Exp))
                        m = dve.done(dve.after(m).tensor_tensor(
                            pair[z][:, :, :], pair[z][:, :, :],
                            bcast(kf[:, b * P:(b + 1) * P], 1, [P, CH, P]), ALU.mult))
                        o = bank_for(SPARE[3])
                        pe.after(m, fin["q"])
                        qj = qf[:, b * P:(b + 1) * P].rearrange("p (c j) -> p j c", j=CH)
                        oj = o[:, 0:P].rearrange("p (c j) -> p j c", j=CH)
                        for j in range(CH):
                            ins = nc.tensor.matmul(oj[:, j], pair[z][:, j, :], qj[:, j], start=True, stop=True)
                        m = pe.done(ins)
                        a_ready = dve.done(dve.after(m).tensor_tensor(aT[z][:, :], o[:, 0:P], cst("chunk_pair"), ALU.mult))
                        read_by(SPARE[3], a_ready)
                        o = bank_for(SPARE[3])
                        pe.after(decayed)
                        m = pe.done(nc.tensor.transpose(o[:, 0:P], k_end[:, b * P:(b + 1) * P], ident))
                        kt_ready = act.done(act.after(m).activation(keT[:, :], o[:, 0:P], ACTF.Copy))
                        read_by(SPARE[3], kt_ready)
                        vb = v[:, b, h * P:(h + 1) * P]
                        vm_ready = pool.done(pool.after(*v_ready, (pe, pe.count)).tensor_tensor(
                            vm[:, :, :], bcast(vb, 1, [P, CPB, P]), bcast(cst("chunk_row"), 2, [P, CPB, P]), ALU.mult))
                        pe.after(kt_ready, vm_ready)
                        for half in range(2):
                            o = bank_for(ACC[half])
                            m = pe.done(nc.tensor.matmul(
                                o[:, :], keT[:, :], vm[:, 4 * half:4 * half + 4, :].rearrange("p c v -> p (c v)"),
                                start=True, stop=True))
                            for c4 in range(4):
                                c = b * CPB + 4 * half + c4
                                if c == TB * CPB - 1:
                                    continue
                                end = c * CH + CH - 1
                                prev = ((dve, dve.count),)
                                s = dve.done(dve.after(m, zero_ready, *prev, *state_read).scalar_tensor_tensor(
                                    state[:, (c + 1) % (CPB + 1), :], state[:, c % (CPB + 1), :], exp_b[:, end:end + 1],
                                    o[:, c4 * P:(c4 + 1) * P], ALU.mult, ALU.add))
                            read_by(ACC[half], s)
                        state_ready = s
                        pe.after(a_ready, state_ready, *v_ready)
                        ob = o_psum[:, b * P:(b + 1) * P]
                        nc.tensor.matmul(ob, vb, aT[z][:, :], start=True, stop=False)
                        for c in range(CPB):
                            t0 = b * P + c * CH
                            ins = nc.tensor.matmul(o_psum[:, t0:t0 + CH], state[:, (b * CPB + c) % (CPB + 1), :], tmp[:, t0:t0 + CH],
                                                   start=False, stop=(c == CPB - 1))
                        made = pe.done(ins)
                        state_read = (made,)
                    m = act.done(act.after(made).activation(exp_b[:, :], o_psum[:, 0:SEQ], ACTF.Square))
                    o = bank_for(SPARE[3])
                    pe.after(m)
                    m = pe.done(nc.tensor.matmul(o[:, 0:SEQ], cst("mean"), exp_b[:, :], start=True, stop=True))
                    m = dve.done(dve.after(m).tensor_scalar(tmp2[:, :], o[:, 0:SEQ], RMS_EPS, None, ALU.add))
                    read_by(SPARE[3], m)
                    m = pool.done(pool.after(m).tensor_tensor(tmp2[:, :], tmp2[:, :], expo[:, :], ALU.pow))
                    m = dve.done(dve.after(m).scalar_tensor_tensor(tmp2[:, :], o_psum[:, 0:SEQ], small[:, HG:HG + 1],
                                                                   tmp2[:, :], ALU.mult, ALU.mult))
                    read_by(o_bank, m)
                    m = dve.done(dve.after(m, fin["g"]).tensor_tensor(tmp2[:, :], tmp2[:, :], gf[:, :], ALU.mult))
                    split_to(oT_hi[:, HG + h, :], oT_lo[:, HG + h, :], tmp2[:, :], (m,))
                    meet()

        def mixer(xT_ready):
            with ExitStack() as scope:
                oT_hi = scope.enter_context(nc.sbuf_tensor("mix_oT_hi", [P, KD, SEQ], F32R))
                oT_lo = scope.enter_context(nc.sbuf_tensor("mix_oT_lo", [P, KD, SEQ], F32R))
                nsa(xT_ready, oT_hi, oT_lo)
                hgrn(xT_ready, oT_hi, oT_lo)
                made = out_product(lambda k: oT_hi[:, k, :], lambda k: oT_lo[:, k, :],
                                   ((act, act.count), (dve, dve.count)), 3, KD)
                meet()
                return made

        def attention(n, tile, scores, value, scale, dv, sink, score_banks, turn_banks, out_banks):
            s = [tile(f"s{i}", [P, 3 * P]) for i in range(2)]
            pT = [tile(f"pT{i}", [P, 3 * P]) for i in range(2)]
            nm = [tile(f"nm{i}", [P, 2]) for i in range(2)]
            sums = [tile(f"sums{i}", [P, 2]) for i in range(2)]
            soft, turned, read = {}, {}, {}
            spans = ((0, 0, P), (1, P, 3 * P))

            def softmax(h):
                z = h % 2
                bank = score_banks[z]
                o = bank_for(bank)
                scores(h, 0, o[:, 0:P], P)
                made = pe.done(scores(h, 1, o[:, P:3 * P], SEQ))
                free = (turned[h - 2],) if h >= 2 else ()
                m = dve.done(dve.after(made, *free).tensor_tensor(s[z][:, :], o[:, 0:3 * P], cst("causal"), ALU.add))
                read_by(bank, m)
                dve.after(m)
                for b, c0, c1 in spans:
                    m = dve.done(nc.vector.tensor_reduce(nm[z][:, b:b + 1], s[z][:, c0:c1], AX_X, ALU.max, negate=True))
                if scale != 1.0:
                    m = dve.done(dve.after(m).tensor_scalar(nm[z][:, :], nm[z][:, :], scale, None, ALU.mult))
                act.after(m)
                for b, c0, c1 in spans:
                    m = act.done(nc.scalar.activation(s[z][:, c0:c1], s[z][:, c0:c1], ACTF.Exp, scale=scale,
                                                      bias=nm[z][:, b:b + 1], accum_out=sums[z][:, b:b + 1]))
                m = dve.done(dve.after(m).reciprocal(sums[z][:, :], sums[z][:, :]))
                dve.after(m)
                for b, c0, c1 in spans:
                    m = dve.done(nc.vector.tensor_scalar(s[z][:, c0:c1], s[z][:, c0:c1], sums[z][:, b:b + 1], None, ALU.mult))
                soft[h] = m

            def transposes(h):
                z = h % 2
                bank = turn_banks[z]
                o = bank_for(bank)
                pe.after(soft[h])
                for i in range(3):
                    ins = nc.tensor.transpose(o[:, i * P:(i + 1) * P], s[z][:, i * P:(i + 1) * P], ident)
                turned[h] = pe.done(ins)
                free = (read[h - 2],) if h >= 2 else ()
                soft[h] = act.done(act.after(turned[h], *free).activation(pT[z][:, :], o[:, 0:3 * P], ACTF.Copy))
                read_by(bank, soft[h])

            def values(h):
                z = h % 2
                bank = out_banks[z]
                base = dv * h % P
                o = bank_for(bank)[base:base + dv, 0:SEQ]
                pe.after(soft[h])
                nc.tensor.matmul(o, value(h, 0), pT[z][:, 0:SEQ], start=True, stop=False)
                read[h] = pe.done(nc.tensor.matmul(o[:, P:SEQ], value(h, 1), pT[z][:, SEQ:3 * P], start=False, stop=True))
                read_by(bank, *sink(h, o, read[h]))

            return softmax, transposes, values

        def fox(xT_ready):
            with ExitStack() as scope:
                def tile(name, shape, dt=F32):
                    return scope.enter_context(nc.sbuf_tensor("fox_" + name, shape, dt))

                oT_hi, oT_lo = tile("oT_hi", [P, KD, SEQ], F32R), tile("oT_lo", [P, KD, SEQ], F32R)
                v = tile("v", [P, TB, D])
                q = [tile(f"q{i}", [P, SEQ]) for i in range(2)]
                k = [tile(f"k{i}", [P, SEQ]) for i in range(2)]
                z_f, ones, cum, neg = (tile(x, [FOX_H, SEQ]) for x in ("f", "ones", "cum", "neg_cum"))
                spare = tile("spare", [FOX_H, SEQ])

                ones_ready = pool.done(pool.after().memset(ones[:, :], 1.0))

                def v_sink(i):
                    def sink(b, o, m):
                        c = act.done(act.after(m).activation(v[:, b, i * SEQ:(i + 1) * SEQ], o, ACTF.Copy))
                        kept.append(c)
                        return (c,)
                    return sink
                for i in range(4):
                    token_tiles(SEQ, (6, 7), xT_ready, v_sink(i))

                fin = {}

                def f_sink(o, m):
                    fin["f"] = act.done(act.after(m, s_mark).activation(
                        z_f[:, :], o[0:FOX_H, :], ACTF.Identity, bias=small[0:FOX_H, HG + 1:HG + 2]))
                    return (fin["f"],)
                feature_tiles(1, (6, 7), xT_ready, [f_sink])
                m = act.done(act.after(fin["f"]).activation(spare[:, :], z_f[:, :], ACTF.Abs))
                m = act.done(act.after(m).activation(spare[:, :], spare[:, :], ACTF.Exp, scale=-1.0))
                m = act.done(act.after(m).activation(spare[:, :], spare[:, :], ACTF.Ln, bias=1.0))
                m = dve.done(dve.after(m).scalar_tensor_tensor(z_f[:, :], z_f[:, :], 0.0, spare[:, :], ALU.min, ALU.subtract))
                m = dve.done(dve.after(m, ones_ready).tensor_tensor_scan(cum[:, :], ones[:, :], z_f[:, :], 0.0, ALU.mult, ALU.add))
                cum_ready = dve.done(dve.after(m).tensor_scalar(neg[:, :], cum[:, :], -1.0, None, ALU.mult))
                qk = {}
                softdone = {}

                def scores(h, b, o, width):
                    z = h // 2 % 2
                    rows = slice(64 * (h % 2), 64 * (h % 2) + 64)
                    pick = ident[0:FOX_H, h:h + 1]
                    pe.after(*qk[h // 2], cum_ready)
                    nc.tensor.matmul(o, q[z][rows, b * P:(b + 1) * P], k[z][rows, 0:width], start=True, stop=False)
                    nc.tensor.matmul(o, cum[:, b * P:(b + 1) * P], pick.to_broadcast([FOX_H, width]), start=False, stop=False)
                    return nc.tensor.matmul(o, pick.to_broadcast([FOX_H, P]), neg[:, 0:width], start=False, stop=True)

                def sink(h, o, m):
                    rows = slice(64 * (h % 2), 64 * (h % 2) + 64)
                    return split_to(oT_hi[rows, h // 2, :], oT_lo[rows, h // 2, :], o, (m, *kept))

                softmax, transposes, values = attention(
                    FOX_H, tile, scores, lambda h, b: v[:, b, h * 64:(h + 1) * 64], 1.0, 64, sink, (0, 1), (2, 3), (4, 5))

                def first(h):
                    if h % 2 == 0:
                        z = h // 2 % 2
                        got = []
                        free = (softdone[h // 2 - 2],) if h // 2 >= 2 else ()

                        def to(dst, scale):
                            def s(o, m):
                                got.append(act.done(act.after(m, *free).activation(dst[:, :], o, ACTF.Copy, scale=scale)))
                                return (got[-1],)
                            return s
                        feature_tiles(2, (6, 7), xT_ready, [to(q[z], 64 ** -0.5), to(k[z], 1.0)])
                        qk[h // 2] = got
                    if h == 0:
                        pe.after(*kept)
                    softmax(h)
                    if h % 2:
                        softdone[h // 2] = (pe, pe.count)

                skewed(FOX_H, first, transposes, values)
                kept.clear()
                made = out_product(lambda i: oT_hi[:, i, :], lambda i: oT_lo[:, i, :],
                                   ((act, act.count), (dve, dve.count)), 3, KD)
                meet()
                return made

        def shared_kv(xT_ready, g_mark, ckv_hi, ckv_lo, k_rope, tmp):
            got = []

            def c_sink(b, o, m):
                r = rms_rows(o, xn[:, b, 0:KL], gains[:, 0:KL], KL, b, (m, g_mark), xn_read[0])
                got.append(r)
                return (r,)
            token_tiles(KL, SPARE, xT_ready, c_sink)
            gains_read[0] = tuple(got)
            fin = []

            def rope_sink(o, m):
                fin.append(dve.done(dve.after(m).tensor_tensor(k_rope[:, :], o, cst("cos"), ALU.mult)))
                return (fin[-1],)

            def swap_sink(o, m):
                a = dve.done(dve.after(m).tensor_tensor(tmp[:, :], o, cst("sin"), ALU.mult))
                fin.append(dve.done(dve.after(a, fin[0]).tensor_tensor(k_rope[:, :], k_rope[:, :], tmp[:, :], ALU.add)))
                return (a,)
            feature_tiles(2, SPARE, xT_ready, [rope_sink, swap_sink])
            marks = turn(lambda b: xn[:, b, :], got, KL // P, ckv_hi, ckv_lo, ())
            xn_read[0] = ((pe, pe.count),)
            return marks, fin[-1]

        def mla(xT_ready, g_mark, ckv_hi, ckv_lo, ckv_ready, k_rope, rope_ready):
            with ExitStack() as scope:
                def tile(name, shape, dt=F32):
                    return scope.enter_context(nc.sbuf_tensor("mla_" + name, shape, dt))

                o2_hi, o2_lo = tile("oT_hi", [P, KD, SEQ], F32R), tile("oT_lo", [P, KD, SEQ], F32R)
                cq_hi, cq_lo = tile("cqT_hi", [P, QL // P, SEQ], F32R), tile("cqT_lo", [P, QL // P, SEQ], F32R)
                qn, kn = (tile(x, [P, 2, SEQ]) for x in ("q_nope", "k_nope"))
                qr, qs = (tile(x, [P, SEQ]) for x in ("q_rope", "q_swap"))
                v = tile("v", [P, TB, 2 * P])
                got = []

                def c_sink(b, o, m):
                    r = rms_rows(o, xn[:, b, 0:QL], gains[:, 0:QL], QL, b, (m, g_mark), xn_read[0])
                    got.append(r)
                    return (r,)
                token_tiles(QL, SPARE, xT_ready, c_sink)
                x_free = (pe, pe.count)
                gains_read[0] = tuple(got)
                cq_ready = turn(lambda b: xn[:, b, :], got, QL // P, cq_hi, cq_lo, ())
                xn_read[0] = ((pe, pe.count),)

                pair_ready = {}
                pair_read = {}

                def project(p):
                    i, hi, lo, there = ws.take()
                    pe.after(*there, *cq_ready, *ckv_ready)
                    free = pair_read.get(p - 1, ())
                    marks = []
                    kq, kk = QL // P, KL // P

                    def one(bank, cols, k_tiles, a_hi, a_lo):
                        o = bank_for(bank)
                        return o, pe.done(feature_major(o[:, 0:SEQ], hi, lo, cols, k_tiles, a_hi, a_lo))
                    for j in range(2):
                        o, m = one(6 + j, lambda k: 4 * P * k + j * P, kq, cq_hi, cq_lo)
                        c = act.done(act.after(m, *free).activation(qn[:, j, :], o[:, 0:SEQ], ACTF.Copy))
                        read_by(6 + j, c)
                        marks.append(c)
                    o, m = one(6, lambda k: 4 * P * k + 2 * P, kq, cq_hi, cq_lo)
                    r = dve.done(dve.after(m, *free).tensor_tensor(qr[:, :], o[:, 0:SEQ], cst("cos"), ALU.mult))
                    read_by(6, r)
                    o, m = one(7, lambda k: 4 * P * k + 3 * P, kq, cq_hi, cq_lo)
                    r = dve.done(dve.after(m, *free).tensor_tensor(qs[:, :], o[:, 0:SEQ], cst("sin"), ALU.mult))
                    read_by(7, r)
                    marks.append(dve.done(dve.after(r).tensor_tensor(qr[:, :], qr[:, :], qs[:, :], ALU.add)))
                    at = kq * 4 * P
                    for j in range(2):
                        o, m = one(6 + j, lambda k: at + 2 * P * k + j * P, kk, ckv_hi, ckv_lo)
                        c = act.done(act.after(m, *free).activation(kn[:, j, :], o[:, 0:SEQ], ACTF.Copy))
                        read_by(6 + j, c)
                        marks.append(c)
                    at2 = at + kk * 2 * P
                    for b in range(TB):
                        o = bank_for(6 + b)
                        m = pe.done(token_major(o[:, 0:2 * P], hi, lo, lambda k: at2 + 2 * P * k, 2 * P, range(kk),
                                                lambda k: ckv_hi[:, k, :], lambda k: ckv_lo[:, k, :], b, True, True))
                        c = act.done(act.after(m, *free).activation(v[:, b, :], o[:, 0:2 * P], ACTF.Copy))
                        read_by(6 + b, c)
                        marks.append(c)
                    ws.release(i, m)
                    pair_ready[p] = marks

                def scores(h, b, o, width):
                    j = h % 2
                    rows = slice(64 * j, 64 * j + 64)
                    pe.after(*pair_ready[h // 2], rope_ready)
                    nc.tensor.matmul(o, qn[:, j, b * P:(b + 1) * P], kn[:, j, 0:width], start=True, stop=False)
                    return nc.tensor.matmul(o, qr[rows, b * P:(b + 1) * P], k_rope[rows, 0:width], start=False, stop=True)

                def halves(h):
                    return (xT_hi, xT_lo) if h < KD else (o2_hi, o2_lo)

                def sink(h, o, m):
                    hi, lo = halves(h)
                    return split_to(hi[:, h % KD, :], lo[:, h % KD, :], o, (m, x_free))

                softmax, transposes, values = attention(
                    MLA_H, tile, scores, lambda h, b: v[:, b, h % 2 * P:h % 2 * P + P],
                    192 ** -0.5, P, sink, (0, 1), (2, 3), (4, 5))

                for p in range(MLA_H // 2):
                    project(p)
                    a, b = 2 * p, 2 * p + 1
                    softmax(a)
                    softmax(b)
                    transposes(a)
                    transposes(b)
                    values(a)
                    values(b)
                    pair_read[p] = ((pe, pe.count),)

                made = out_product(lambda h: halves(h)[0][:, h % KD, :], lambda h: halves(h)[1][:, h % KD, :],
                                   ((act, act.count), (dve, dve.count)), 6, MLA_H)
                meet()
                return made

        def ple(layer, xT_ready, x_ready, xs_ready, g_row):
            with ExitStack() as scope:
                def tile(name, shape, dt=F32):
                    return scope.enter_context(nc.sbuf_tensor(f"ple{layer}_" + name, shape, dt))

                pT = tile("pT", [P, 2, SEQ])
                pT_hi, pT_lo = tile("pT_hi", [P, 2, SEQ], F32R), tile("pT_lo", [P, 2, SEQ], F32R)
                proj = tile("proj", [P, TB, D])
                z = tile("z", [P, TB, D])
                bias = tile("bias", [P, D])
                small_landed.done(sp.after().dma_start(pT[:, :, :], t["pT"][layer, :, :, :]), 16)
                landed = small_landed.done(sp.after().dma_start(
                    bias[:, :], t["gains"][14 + layer:15 + layer, 0:D].to_broadcast([P, D])), 16)
                ready = split_to(pT_hi[:, :, :], pT_lo[:, :, :], pT[:, :, :], (landed,))
                made = out_product(lambda k: pT_hi[:, k, :], lambda k: pT_lo[:, k, :], ready, 1, 2, per=2)
                for b in range(TB):
                    for half in range(2):
                        c = slice(512 * half, 512 * (half + 1))
                        m = act.done(act.after(made).activation(proj[:, b, c], psum[ACC[2 * b + half]][:, :], ACTF.Copy))
                        read_by(ACC[2 * b + half], m)
                proj_ready = m
                made = out_product(lambda k: xT_hi[:, k, :], lambda k: xT_lo[:, k, :], xT_ready, 3, KD)
                xT_read[0] = (made,)
                marks = []
                for b in range(TB):
                    for half in range(2):
                        c = slice(512 * half, 512 * (half + 1))
                        bank = ACC[2 * b + half]
                        m = dve.done(dve.after(made, landed).tensor_tensor(z[:, b, c], psum[bank][:, :], bias[:, c], ALU.add))
                        read_by(bank, m)
                        m = act.done(act.after(m).activation(z[:, b, c], z[:, b, c], ACTF.Sigmoid))
                        m = dve.done(dve.after(m, proj_ready).tensor_tensor(z[:, b, c], z[:, b, c], proj[:, b, c], ALU.mult))
                        m = dve.done(dve.after(m, xs_ready).tensor_tensor(x[:, b, c], x[:, b, c], z[:, b, c], ALU.add))
                    marks.append(m)
                meet()
                return marks

        xT_read = [()]
        xn_read = [()]

        def residual(scale, made, ready):
            marks = []
            for b in range(TB):
                for half in range(2):
                    xs = x[:, b, 512 * half:512 * (half + 1)]
                    bank = ACC[2 * b + half]
                    m = dve.done(dve.after(made, *ready).scalar_tensor_tensor(
                        xs, psum[bank][:, :], scale, xs, ALU.mult, ALU.add))
                    read_by(bank, m)
                marks.append(m)
            return marks

        def rms_turn(x_ready, g_mark):
            ready = [rms_rows(x[:, b, :], xn[:, b, :], gains[:, 0:D], D, b, (x_ready[b], g_mark), xn_read[0])
                     for b in range(TB)]
            gains_read[0] = tuple(ready)
            marks = turn(lambda b: xn[:, b, :], ready, KD, xT_hi, xT_lo, xT_read[0])
            xn_read[0] = ((pe, pe.count),)
            return marks

        def turn_x(x_ready):
            marks = turn(lambda b: x[:, b, :], x_ready, KD, xT_hi, xT_lo, xT_read[0])
            m = act.done(act.after(*x_ready, (pe, pe.count)).activation(x[:, :, :], x[:, :, :], ACTF.Copy, scale=ALPHA))
            return marks, m

        def ln_x(x_ready, g_mark):
            ready = [ln_rows(x[:, b, :], x[:, b, :], b, (x_ready[b], g_mark), ()) for b in range(TB)]
            gains_read[0] = tuple(ready)
            return ready

        def finish(ready):
            m = out_landed.done(sp.after(*ready).dma_start(out.rearrange("(b p) d -> p b d", p=P), x[:, :, :]), 16)
            sp.after(m)

        for e in everyone:
            e.after(c_mark)
        g_mark = load_gains(0)
        xT_ready = rms_turn([x_mark, x_mark], g_mark)
        g_mark = load_gains(1)
        made = ffn(xT_ready)
        xT_read[0] = (made,)
        x_ready = residual(0.5, made, ())
        if stop == 1:
            return finish(x_ready)

        xT_ready = rms_turn(x_ready, g_mark)
        g_mark = load_gains(2)
        meet()
        made = mixer(xT_ready)
        xT_read[0] = (made,)
        x_ready = residual(1.0, made, ())
        if stop == 2:
            return finish(x_ready)

        xT_ready = rms_turn(x_ready, g_mark)
        g_mark = load_gains(3)
        made = ffn(xT_ready)
        xT_read[0] = (made,)
        x_ready = residual(0.5, made, ())
        x_ready = [rms_rows(x[:, b, :], x[:, b, :], gains[:, 0:D], D, b, (x_ready[b], g_mark), ()) for b in range(TB)]
        gains_read[0] = tuple(x_ready)
        if stop == 3:
            return finish(x_ready)

        ckv_hi = sb("ckvT_hi", [P, KL // P, SEQ], F32R)
        ckv_lo = sb("ckvT_lo", [P, KL // P, SEQ], F32R)
        k_rope = sb("k_rope", [P, SEQ])
        for layer in range(2):
            base = 4 + 4 * layer
            xT_ready, xs_ready = turn_x(x_ready)
            if layer == 1:
                g_mark = load_gains(12)
                ckv_ready, rope_ready = shared_kv(xT_ready, g_mark, ckv_hi, ckv_lo, k_rope, sig[0])
            g_mark = load_gains(base)
            made = ffn(xT_ready)
            xT_read[0] = (made,)
            x_ready = ln_x(residual(0.5, made, (xs_ready,)), g_mark)
            if stop == 4 + 4 * layer:
                return finish(x_ready)
            xT_ready, xs_ready = turn_x(x_ready)
            meet()
            if layer == 0:
                g_mark = load_gains(base + 1)
                made = fox(xT_ready)
            else:
                made = mla(xT_ready, load_gains(13), ckv_hi, ckv_lo, ckv_ready, k_rope, rope_ready)
                g_mark = load_gains(base + 1)
            xT_read[0] = (made,)
            x_ready = ln_x(residual(1.0, made, (xs_ready,)), g_mark)
            if stop == 5 + 4 * layer:
                return finish(x_ready)
            xT_ready, xs_ready = turn_x(x_ready)
            g_mark = load_gains(base + 2)
            made = ffn(xT_ready)
            xT_read[0] = (made,)
            x_ready = ln_x(residual(0.5, made, (xs_ready,)), g_mark)
            if stop == 6 + 4 * layer:
                return finish(x_ready)
            xT_ready, xs_ready = turn_x(x_ready)
            meet()
            g_mark = load_gains(base + 3)
            x_ready = ple(layer, xT_ready, x_ready, xs_ready, base + 3)
            x_ready = ln_x(x_ready, g_mark)
            if stop == 7 + 4 * layer:
                return finish(x_ready)
        finish(x_ready)


def rows_of(w):
    return w.reshape(w.shape[0] // P, P, w.shape[1]).transpose(1, 0, 2)


def chunk(*parts):
    return np.concatenate([rows_of(w) for w in parts], 2).reshape(1, P, -1)


def ffn_chunks(w_gu, w_down):
    f = w_down.shape[0]
    pad = FF_TILES * P - f
    wide = lambda w: np.concatenate([w, np.zeros((D, pad), np.float32)], 1)
    gate = rows_of(wide(w_gu[:, :f])).reshape(P, KD, FF_TILES, 1, P)
    up = rows_of(wide(w_gu[:, f:])).reshape(P, KD, FF_TILES, 1, P)
    gu = np.concatenate([gate, up], 3).transpose(2, 0, 1, 3, 4).reshape(FF_TILES, P, GU)
    down = np.concatenate([w_down, np.zeros((pad, D), np.float32)], 0).reshape(FF_TILES, P, D)
    return np.concatenate([gu, down], 2)


def k_chunks(w, per=3):
    r = rows_of(w)
    n = r.shape[1] // per
    whole = r[:, :n * per].reshape(P, n, per * D).transpose(1, 0, 2)
    rest = r[:, n * per:].reshape(1, P, -1)
    return whole, rest


def layouts(a):
    t = {"const": const_table(), "x": a["x"][0]}
    t["ffn_a"] = ffn_chunks(a["ffn1_w_gu"][0], a["ffn1_w_down"][0])
    t["ffn_b"] = ffn_chunks(a["ffn2_w_gu"][0], a["ffn2_w_down"][0])
    for i, n in ((0, "c"), (1, "e")):
        t["ffn_" + n] = ffn_chunks(a["ffn1_w_in_2"][i], a["ffn1_w_out_2"][i])
    for i, n in ((0, "d"), (1, "f")):
        t["ffn_" + n] = ffn_chunks(a["ffn2_w_in_2"][i], a["ffn2_w_out_2"][i])
    w = a["w_in"][0]
    kv = GROUPS * HD
    sizes = (HEADS * HD, kv, kv, kv, kv, kv, kv, GATES, HG * P, HG * P, HG * P, HG * P)
    ends = np.cumsum(sizes)
    nq, kc, vc, ks, vs, kw, vw, gl, hq, hf, hi, hg = (w[:, e - s:e] for e, s in zip(ends, sizes))
    two = lambda m, g: np.concatenate([m[:, g * HD:(g + 1) * HD]] * 2, 1)
    tile = lambda m, j: m[:, j * P:(j + 1) * P]
    t["nsa_cmp_in"] = np.concatenate([chunk(two(kc, 0), two(kc, 1), two(vc, 0)),
                                      chunk(two(vc, 1), two(ks, 0), two(ks, 1))])
    t["nsa_qk"] = np.concatenate([chunk(two(kw, 0), two(kw, 1), tile(nq, 0)),
                                  chunk(tile(nq, 1), tile(nq, 2), tile(nq, 3))])
    t["nsa_v"] = chunk(vs, vw, gl)
    t["hg_v"] = np.concatenate([chunk(hi[:, :SEQ]), chunk(hi[:, SEQ:])])
    t["hg"] = np.concatenate([chunk(tile(hq, h), tile(hf, h), tile(hg, h)) for h in range(HG)])
    w1 = [rows_of(a[n][0]).reshape(P, 2, LP // 2 * CMP_HID).transpose(1, 0, 2) for n in ("cmp_k_w1", "cmp_v_w1")]
    t["cmp_w1"] = np.concatenate(w1)
    k2, v2 = rows_of(a["cmp_k_w2"][0]), rows_of(a["cmp_v_w2"][0])
    t["cmp_w2"] = np.stack([np.concatenate([m, m], 2) for m in (k2, v2)], 1)
    t["cmp_pos"] = np.stack([a[n][0].reshape(LP, P).T for n in ("cmp_pos_k", "cmp_pos_v")], 1)
    t["w_out1"], t["w_out2"] = k_chunks(a["w_out"][0])
    small = np.zeros((P, HG + 2), np.float32)
    small[:, 0:HG] = a["hgrn_lower_bound"][0].reshape(HG, P).T
    small[:, HG] = a["hgrn_out_norm"][0]
    small[:FOX_H, HG + 1] = a["fox_b_f_2"][0]
    t["small"] = small

    gains = np.zeros((16, 2 * D), np.float32)
    for i, g in enumerate((a["ffn1_norm"][0], a["mix_norm"][0], a["ffn2_norm"][0], a["final_norm"])):
        gains[i, :D] = g
    for i in range(2):
        for j in range(4):
            gains[4 + 4 * i + j, :D] = a["ln_g_2"][i, j]
            gains[4 + 4 * i + j, D:] = a["ln_b_2"][i, j]
        gains[14 + i, :D] = a["ple_b_gate_2"][i]
    gains[12, :KL] = a["kv_norm_2"]
    gains[13, :QL] = a["mla_q_norm_2"][0]
    t["gains"] = gains

    w = a["fox_w_in_2"][0]
    fq, fk, fv, ff = w[:, :D], w[:, D:2 * D], w[:, 2 * D:3 * D], w[:, 3 * D:]
    t["fox_v"] = np.concatenate([chunk(fv[:, i * SEQ:(i + 1) * SEQ]) for i in range(4)])
    t["fox_f"] = chunk(np.concatenate([ff, np.zeros((D, P - FOX_H), np.float32)], 1))
    t["fox_qk"] = np.concatenate([chunk(tile(fq, j), tile(fk, j)) for j in range(KD)])
    t["fox_o1"], t["fox_o2"] = k_chunks(a["fox_w_o_2"][0])
    for i in range(2):
        t[f"ple{i}_p"] = chunk(a["ple_w_proj_2"][i])
        t[f"ple{i}_g1"], t[f"ple{i}_g2"] = k_chunks(a["ple_w_gate_2"][i])
    t["pT"] = a["p_2"][:, 0].transpose(0, 2, 1).reshape(2, 2, P, SEQ).transpose(0, 2, 1, 3)
    down = a["kv_w_down_2"]
    half = ROPE // 2
    rope = down[:, KL:]
    swap = lambda m: np.concatenate([m[..., half:], m[..., :half]], -1)
    t["kv_down1"] = chunk(down[:, :KL])
    t["kv_down2"] = chunk(rope, rope, swap(rope), swap(rope))
    t["mla_dq"] = chunk(a["mla_w_dq_2"][0])
    uq, up = a["mla_w_uq_2"][0], a["kv_w_up_2"]
    pairs = []
    for p in range(MLA_H // 2):
        h0, h1 = 2 * p, 2 * p + 1
        pairs.append(np.concatenate([
            chunk(uq[:, h0, :P], uq[:, h1, :P], uq[:, h0, P:], uq[:, h1, P:], swap(uq[:, h0, P:]), swap(uq[:, h1, P:])),
            chunk(up[:, h0, :P], up[:, h1, :P]), chunk(up[:, h0, P:], up[:, h1, P:])], 2))
    t["mla_up"] = np.concatenate(pairs)
    t["mla_o1"], t["mla_o2"] = k_chunks(a["mla_w_o_2"][0])
    return {n: np.ascontiguousarray(v) for n, v in t.items()}


def kernel(**inputs):
    import concourse.bacc as bacc
    from concourse.bass_utils import run_bass_kernel_spmd

    nc = bacc.Bacc("TRN2", target_bir_lowering=False, num_devices=1)
    arrays, t = {}, {}
    for name, v in layouts({n: np.asarray(v) for n, v in inputs.items()}).items():
        arrays["in_" + name] = v
        t[name] = nc.dram_tensor("in_" + name, v.shape, F32, kind="ExternalInput").ap()
    out = nc.dram_tensor("out", (SEQ, D), F32, kind="ExternalOutput").ap()
    build(nc, t, out)
    r = run_bass_kernel_spmd(nc, [arrays], core_ids=[0])
    return r.results[0]["out"].reshape(1, SEQ, D)
```

```python
from contextlib import ExitStack

import numpy as np

import concourse.bass as bass
from concourse import mybir

F32 = mybir.dt.float32
F32R = mybir.dt.float32r
ALU = mybir.AluOpType
ACTF = mybir.ActivationFunctionType
AX_X = mybir.AxisListType.X

P = 128
SEQ = 256
TB = SEQ // P
D = 1024
KD = D // P
RMS_EPS = 1e-6
LN_EPS = 1e-5
ALPHA = (2 * 2) ** 0.25
MASKED = -1e30

FF_TILES = 22
GU = KD * 2 * P
FF_COLS = GU + D

HEADS = 8
GROUPS = 2
HD = 64
CMP_LEN = 32
STRIDE = 16
NB = SEQ // STRIDE - 1
CMP_HID = 256
LP = CMP_LEN // 2
GATES = HEADS * 3
VSW = 2 * GROUPS * HD + GATES

HG = 4
CH = 16
CPB = P // CH
F_FLOOR = 1e-30
LN_SPLIT = 2.0 ** 50
LN_RANGE = 2.0 ** -50

FOX_H = 16
MLA_H = 16
QL = 384
KL = 256
ROPE = 64

CHUNK = 3072
RAW_SLOTS = 4

CONST_COLS = {}
_at = 0
for _name, _n in (("ident", P), ("causal", 3 * P), ("dist", 3 * P), ("cmp_dist", TB * NB),
                  ("cmp_row", TB), ("chunk_pair", P), ("chunk_row", CPB), ("restart", SEQ),
                  ("mean", P), ("cos", SEQ), ("sin", SEQ)):
    CONST_COLS[_name] = (_at, _n)
    _at += _n
N_CONST = _at + _at % 2


def const_table():
    t = np.zeros((P, N_CONST), np.float32)

    def put(name, value):
        a, n = CONST_COLS[name]
        t[:value.shape[0], a:a + n] = value.reshape(value.shape[0], n)

    put("ident", np.eye(P, dtype=np.float32))
    row = np.arange(P)[:, None]
    col = np.arange(P)[None, :]
    diag = np.where(col <= row, 0.0, MASKED).astype(np.float32)
    put("causal", np.concatenate([diag, np.zeros((P, P), np.float32), diag], 1))
    near = np.where(col <= row, row - col, 1e33).astype(np.float32)
    put("dist", np.concatenate([near, (row + P - col).astype(np.float32), near], 1))
    tok = np.arange(SEQ).reshape(TB, P).T
    end = np.arange(NB) * STRIDE + CMP_LEN - 1
    away = tok[:, :, None] - end[None, None, :]
    put("cmp_dist", np.where(away >= 0, away, 1e33).astype(np.float32))
    put("cmp_row", (tok >= CMP_LEN - 1).astype(np.float32))
    put("chunk_pair", ((row // CH == col // CH) & (row <= col)).astype(np.float32))
    put("chunk_row", (row // CH == np.arange(CPB)[None, :]).astype(np.float32))
    put("restart", np.broadcast_to((np.arange(SEQ) % CH != 0).astype(np.float32), (P, SEQ)))
    put("mean", np.full((P, P), 1.0 / P, np.float32))
    inv = np.float32(10000.0) ** (-np.arange(ROPE // 2, dtype=np.float32) * np.float32(2.0 / ROPE))
    ang = (np.arange(SEQ, dtype=np.float32)[:, None] * inv[None, :]).astype(np.float32)
    cos, sin = np.cos(ang).T.astype(np.float32), np.sin(ang).T.astype(np.float32)
    put("cos", np.concatenate([cos, cos, cos, cos], 0))
    put("sin", np.concatenate([-sin, sin, -sin, sin], 0))
    return t


class Engine:

    def __init__(self, queue, semaphore):
        self.queue, self.semaphore = queue, semaphore
        self.count = 0
        self.waited = {}

    def after(self, *marks):
        for who, value in marks:
            if self.waited.get(id(who), 0) < value:
                self.queue.wait_ge(who.semaphore, value)
                self.waited[id(who)] = value
        return self.queue

    def done(self, instruction, by=1):
        instruction.then_inc(self.semaphore, by)
        self.count += by
        return (self, self.count)


class WeightStream:

    def __init__(self, sp, act, dve, raw, hi, lo, slot_loads):
        self.sp, self.act, self.dve = sp, act, dve
        self.raw, self.hi, self.lo = raw, hi, lo
        self.slot_loads = slot_loads
        self.chunks = []
        self.loaded = {}
        self.raw_free = {}
        self.split_at = {}
        self.released = {}
        self.n_loaded = 0
        self.at = 0
        self.seq = []

    def add(self, source, cols, split=True):
        self.chunks.append((source, cols, split))
        if split:
            self.seq.append(len(self.chunks) - 1)

    def load(self, i, *free):
        if i >= len(self.chunks):
            return
        source, cols, _ = self.chunks[i]
        slot = i % RAW_SLOTS
        loads = self.slot_loads[slot]
        queue = self.sp.after(*free)
        self.loaded[i] = loads.done(queue.dma_start(self.raw[slot][:, 0:cols], source), 16)

    def pair(self, i):
        return self.seq.index(i) % 2

    def split(self, i, a, b, *free, last=False):
        if i >= len(self.chunks):
            return
        raw = self.raw[i % RAW_SLOTS][:, a:b]
        hi, lo = self.hi[self.pair(i)][:, a:b], self.lo[self.pair(i)][:, a:b]
        h = self.act.done(self.act.after(self.loaded[i], *free).activation(hi, raw, ACTF.Copy))
        l = self.dve.done(self.dve.after(self.loaded[i], h, *free).tensor_tensor(
            lo, raw, hi.bitcast(F32), ALU.subtract))
        self.split_at.setdefault(i, []).append((a, b, h, l))
        if last:
            self.load(i + RAW_SLOTS, h, l)

    def split_head(self, i, upto, *free):
        if i < len(self.chunks) and self.chunks[i][2]:
            cols = self.chunks[i][1]
            upto = min(cols, upto)
            self.split(i, 0, upto // 4 * 2, *free)
            self.split(i, upto // 4 * 2, upto, *free, last=(upto == cols))

    def split_whole(self, i):
        if i >= len(self.chunks) or not self.chunks[i][2]:
            return
        cols = self.chunks[i][1]
        at = self.split_at[i][-1][1] if i in self.split_at else 0
        if at == cols:
            return
        k = self.seq.index(i)
        free = self.released.get(self.seq[k - 2], ()) if k >= 2 else ()
        if at == 0:
            self.split(i, 0, cols // 4 * 2, *free)
            at = cols // 4 * 2
        self.split(i, at, cols, *free, last=True)

    def take(self):
        i = self.at
        self.at += 1
        if not self.chunks[i][2]:
            self.split_whole(i + 1)
            return i, self.raw[i % RAW_SLOTS], None, (self.loaded[i],)
        self.split_whole(i)
        self.split_whole(i + 1)
        return i, self.hi[self.pair(i)], self.lo[self.pair(i)], tuple(m for s in self.split_at[i] for m in s[2:])

    def release(self, i, mark):
        self.released[i] = (mark,)
        if not self.chunks[i][2]:
            self.load(i + RAW_SLOTS, mark)


def build(nc, t, out, stop=99):
    with ExitStack() as ctx:
        def sb(name, shape, dt=F32):
            return ctx.enter_context(nc.sbuf_tensor(name, shape, dt))

        def counter(queue, name):
            return Engine(queue, ctx.enter_context(nc.semaphore(name)))

        pe = counter(nc.tensor, "pe_done")
        act = counter(nc.scalar, "act_done")
        dve = counter(nc.vector, "dve_done")
        pool = counter(nc.gpsimd, "pool_done")
        sp = counter(nc.sync, "sp_done")
        slot_loads = [counter(None, f"weights_landed_{i}") for i in range(RAW_SLOTS)]
        small_landed = counter(None, "small_landed")
        gains_landed = counter(None, "gains_landed")
        out_landed = counter(None, "out_landed")

        raw = [sb(f"w_raw{i}", [P, CHUNK]) for i in range(RAW_SLOTS)]
        w_hi = [sb(f"w_hi{i}", [P, CHUNK], F32R) for i in range(2)]
        w_lo = [sb(f"w_lo{i}", [P, CHUNK], F32R) for i in range(2)]
        x = sb("x", [P, TB, D])
        xn = sb("xn", [P, TB, D])
        xT_hi = sb("xT_hi", [P, KD, SEQ], F32R)
        xT_lo = sb("xT_lo", [P, KD, SEQ], F32R)
        gains = sb("gains", [P, 2 * D + CH])
        const = sb("const", [P, N_CONST])
        sig = [sb(f"ff_silu{i}", [P, SEQ]) for i in range(2)]
        hT_hi = [sb(f"hT_hi{i}", [P, SEQ], F32R) for i in range(2)]
        hT_lo = [sb(f"hT_lo{i}", [P, SEQ], F32R) for i in range(2)]
        stats = sb("stats", [P, TB, 2, 6])
        mv = sb("mean_var", [P, TB, 2])
        rstd = sb("rstd", [P, TB])
        expo = sb("minus_half", [P, 1])
        small = sb("small", [P, 64])
        psum = [ctx.enter_context(nc.psum_tensor(f"bank{i}", [P, 512], F32)) for i in range(8)]
        psum_read = [() for _ in range(8)]

        def cst(name, rows=P):
            a, n = CONST_COLS[name]
            return const[0:rows, a:a + n]

        ident = cst("ident")
        x_landed = [counter(None, f"x_landed_{b}") for b in range(TB)]
        x_mark = [x_landed[b].done(sp.after().dma_start(x[:, b, :], t["x"][b * P:(b + 1) * P, :]), 16) for b in range(TB)]
        g_first = gains_landed.done(sp.after().dma_start(gains[:, 0:D], t["gains"][0:1, 0:D].to_broadcast([P, D])), 16)
        minus_half = pool.done(pool.after().memset(expo[:, :], -0.5))

        stream = WeightStream(sp, act, dve, raw, w_hi, w_lo, slot_loads)
        ws = stream

        def add_all(name, split=True):
            n, _, cols = t[name].shape
            for i in range(n):
                ws.add(t[name][i, :, :], cols, split)

        for name, split in (("ffn_a", True), ("nsa_cmp_in", True), ("cmp_w1", False), ("nsa_qk", True),
                            ("nsa_v", True), ("hg_v", True), ("hg", True), ("w_out1", True),
                            ("w_out2", True), ("ffn_b", True),
                            ("ffn_c", True), ("fox_f", True), ("fox_v", True), ("fox_qk", True),
                            ("fox_o1", True), ("fox_o2", True), ("ffn_d", True), ("ple0_p", True),
                            ("ple0_g1", True), ("ple0_g2", True),
                            ("kv_down1", True), ("kv_down2", True), ("ffn_e", True), ("mla_dq", True),
                            ("mla_up", True), ("mla_o1", True), ("mla_o2", True), ("ffn_f", True), ("ple1_p", True),
                            ("ple1_g1", True), ("ple1_g2", True)):
            add_all(name, split)
        ws.load(0)
        const_landed = counter(None, "const_landed")
        c_mark = const_landed.done(sp.after().dma_start(const[:, :], t["const"]), 16)
        for i in range(1, RAW_SLOTS):
            ws.load(i)
        s_mark = small_landed.done(sp.after().dma_start(small[:, 0:HG + 2], t["small"]), 16)

        everyone = (pe, act, dve, pool)

        def meet():
            marks = [(e, e.count) for e in everyone if e.count]
            for e in everyone:
                e.after(*(m for m in marks if m[0] is not e))

        def bank_for(i):
            pe.after(*psum_read[i])
            psum_read[i] = ()
            return psum[i]

        def read_by(i, *marks):
            psum_read[i] = psum_read[i] + marks

        def feature_major(o, hi, lo, cols, k_tiles, a_hi, a_lo, ready):
            last = 3 * k_tiles - 1
            n = 0
            for k in range(k_tiles):
                c = slice(cols(k), cols(k) + P)
                pe.after(*ready[k])
                for w, a in ((hi, a_hi), (hi, a_lo), (lo, a_hi)):
                    ins = nc.tensor.matmul(o, w[:, c], a[:, k, :], start=(n == 0), stop=(n == last))
                    n += 1
            return ins

        def token_major(o, hi, lo, cols, width, ks, a_hi, a_lo, b, first, final, ready):
            total = 3 * len(ks)
            n = 0
            for j, k in enumerate(ks):
                c = slice(cols(j), cols(j) + width)
                tok = slice(b * P, (b + 1) * P)
                pe.after(*ready[k])
                for a, w in ((a_hi, hi), (a_lo, hi), (a_hi, lo)):
                    ins = nc.tensor.matmul(o, a(k)[:, tok], w[:, c], start=(first and n == 0),
                                           stop=(final and n == total - 1))
                    n += 1
            return ins

        ACC = (0, 1, 2, 3)
        SPARE = (4, 5, 6, 7)

        def load_gains(row):
            src = t["gains"][row:row + 1, :].to_broadcast([P, 2 * D])
            return gains_landed.done(sp.after(*gains_read[0]).dma_start(gains[:, 0:2 * D], src), 16)

        gains_read = [()]

        def statistics(src, width, b, ready):
            n = max(1, width // 512)
            w = width // n
            for j in range(n):
                m = dve.done(dve.after(*ready).bn_stats(out=stats[:, b, j, :], in_=src[:, j * w:(j + 1) * w]))
            return dve.done(dve.after(m).bn_aggr(out=mv[:, b, :], in_=stats[:, b, 0:n, :]))

        def root(b, var, eps, ready):
            m = dve.done(dve.after(ready).tensor_scalar(rstd[:, b:b + 1], var, eps, None, ALU.add))
            return pool.done(pool.after(m, minus_half).tensor_tensor(
                rstd[:, b:b + 1], rstd[:, b:b + 1], expo[:, 0:1], ALU.pow))

        def rms_root(src, width, b, ready):
            m = statistics(src, width, b, ready)
            m = dve.done(dve.after(m).scalar_tensor_tensor(
                rstd[:, b:b + 1], mv[:, b, 0:1], mv[:, b, 0:1], mv[:, b, 1:2], ALU.mult, ALU.add))
            return root(b, rstd[:, b:b + 1], RMS_EPS, m)

        def rms_apply(src, dst, b, c, ready):
            return dve.done(dve.after(*ready).scalar_tensor_tensor(
                dst[:, c], src[:, c], rstd[:, b:b + 1], gains[:, c], ALU.mult, ALU.mult))

        def rms_rows(src, dst, width, b, ready, free):
            m = rms_root(src, width, b, ready)
            return rms_apply(src, dst, b, slice(0, width), (m, *free))

        def ln_apply(b, c, ready):
            xb = x[:, b, c]
            rstd_ready, *others = ready
            m = dve.done(dve.after(*others).scalar_tensor_tensor(
                xb, xb, mv[:, b, 0:1], gains[:, c], ALU.subtract, ALU.mult))
            return dve.done(dve.after(m, rstd_ready).scalar_tensor_tensor(
                xb, xb, rstd[:, b:b + 1], gains[:, D + c.start:D + c.stop], ALU.mult, ALU.add))

        def turn(pieces, kts, dst_hi, dst_lo, free):
            marks = {k: () for k in range(kts)}
            later = None
            for b, k0, src, make in pieces:
                made = make()
                n = min(4, kts - k0)
                bank = SPARE[2 * b + k0 // 4]
                o = bank_for(bank)
                pe.after(made)
                for i in range(n):
                    ins = nc.tensor.transpose(o[:, i * P:(i + 1) * P], src[:, (k0 + i) * P:(k0 + i + 1) * P], ident)
                turned = pe.done(ins)
                hi, lo = (z[:, k0:k0 + n, b * P:(b + 1) * P] for z in (dst_hi, dst_lo))
                got = o[:, 0:n * P].rearrange("p (k t) -> p k t", t=P)
                h = act.done(act.after(turned, *free).activation(hi, got, ACTF.Copy))
                if later:
                    later()

                def later(h=h, turned=turned, hi=hi, lo=lo, got=got, bank=bank, ks=range(k0, k0 + n)):
                    l = dve.done(dve.after(turned, h).tensor_tensor(lo, got, hi.bitcast(F32), ALU.subtract))
                    read_by(bank, h, l)
                    for k in ks:
                        marks[k] += (h, l)
            later()
            return marks

        def split_to(hi, lo, src, ready, free=()):
            h = act.done(act.after(*ready, *free).activation(hi, src, ACTF.Copy))
            l = dve.done(dve.after(h, *ready, *free).tensor_tensor(lo, src, hi.bitcast(F32), ALU.subtract))
            return h, l

        def ffn(xT_ready):
            first = ws.at
            n = FF_TILES
            ws.at += n
            h_ready = {}
            h_read = {}
            down = {}

            def gate_up(i):
                c = first + i
                w = ws.pair(c)
                bank = SPARE[i % 4]
                o = bank_for(bank)
                pe.after(*(m for s in ws.split_at[c] if s[0] < GU for m in s[2:]))
                feature_major(o[:, 0:SEQ], w_hi[w], w_lo[w], lambda k: 2 * P * k, KD, xT_hi, xT_lo, xT_ready)
                return pe.done(feature_major(o[:, SEQ:2 * SEQ], w_hi[w], w_lo[w],
                                             lambda k: 2 * P * k + P, KD, xT_hi, xT_lo, xT_ready))

            def activate(i, made):
                bank = SPARE[i % 4]
                o = psum[bank]
                s = i % 2
                free = (h_read[i - 2],) if i >= 2 else ()
                a = act.done(act.after(made, *free).activation(sig[s][:, :], o[:, 0:SEQ], ACTF.Silu))
                m = dve.done(dve.after(a).tensor_tensor(sig[s][:, :], sig[s][:, :], o[:, SEQ:2 * SEQ], ALU.mult))
                read_by(bank, a, m)
                h, l = split_to(hT_hi[s][:, :], hT_lo[s][:, :], sig[s][:, :], (m,), free)
                h_ready[i] = (h, l)

            def down_product(tiles):
                if tiles[0] == 0:
                    for a in ACC:
                        bank_for(a)
                marks = []
                for b in range(TB):
                    for i in tiles:
                        c = first + i
                        w = ws.pair(c)
                        s = i % 2
                        pe.after(*(m for q in ws.split_at[c] if q[1] > GU for m in q[2:]))
                        for half in range(2):
                            ins = token_major(psum[ACC[2 * b + half]][:, :], w_hi[w], w_lo[w],
                                              lambda j: GU + 512 * half, 512, (0,),
                                              lambda k: hT_hi[s], lambda k: hT_lo[s], b, i == 0, i == n - 1,
                                              (h_ready[i],))
                    marks.append(pe.done(ins))
                for i in tiles:
                    h_read[i] = down[i] = marks[-1]
                    ws.released[first + i] = (marks[-1],)
                return marks

            made = {}
            ws.split_whole(first)
            for i in range(n):
                c = first + i
                made[i] = gate_up(i)
                if i + 1 < n:
                    free = (made[i - 1],) if i >= 1 else ws.released.get(c - 1, ())
                    ws.split(c + 1, 0, GU // 2, *free)
                    ws.split(c + 1, GU // 2, GU, *free)
                else:
                    ws.split_head(first + n, GU, made[i - 1])
                activate(i, made[i])
                if 1 <= i < n - 1:
                    down_product((i - 1,))
                if i + 1 < n:
                    free = (down[i - 1],) if i >= 1 else ws.released.get(c - 1, ())
                    ws.split(c + 1, GU, FF_COLS, *free, last=True)
            marks = down_product((n - 2, n - 1))
            return marks

        def out_product(a_hi, a_lo, ready, n_chunks, k_tiles, per=3):
            for a in ACC:
                bank_for(a)
            for c in range(n_chunks):
                i, hi, lo, there = ws.take()
                ks = list(range(c * per, min(c * per + per, k_tiles)))
                pe.after(*there)
                marks = []
                for b in range(TB):
                    for half in range(2):
                        ins = token_major(psum[ACC[2 * b + half]][:, :], hi, lo,
                                          lambda j: D * j + 512 * half, 512, ks, a_hi, a_lo,
                                          b, c == 0, ks[-1] == k_tiles - 1, ready)
                    marks.append(pe.done(ins))
                ws.release(i, marks[-1])
            return marks

        def bcast(ap, axis, shape):
            return ap.unsqueeze(axis).to_broadcast(shape)

        def feature_tiles(n, banks, ready, sinks, a_hi=None, a_lo=None, k_tiles=KD):
            i, hi, lo, there = ws.take()
            pe.after(*there)
            for j in range(n):
                bank = banks[j % len(banks)]
                o = bank_for(bank)
                m = pe.done(feature_major(o[:, 0:SEQ], hi, lo, lambda k: (n * k + j) * P, k_tiles,
                                          a_hi or xT_hi, a_lo or xT_lo, ready))
                read_by(bank, *sinks[j](o[:, 0:SEQ], m))
            ws.release(i, m)

        def token_tiles(width, banks, ready, sink, a_hi=None, a_lo=None, k_tiles=KD):
            i, hi, lo, there = ws.take()
            pe.after(*there)
            for b in range(TB):
                bank = banks[b % len(banks)]
                o = bank_for(bank)
                m = pe.done(token_major(o[:, 0:width], hi, lo, lambda k: width * k, width, range(k_tiles),
                                        lambda k: (a_hi or xT_hi)[:, k, :], lambda k: (a_lo or xT_lo)[:, k, :],
                                        b, True, True, ready))
                read_by(bank, *sink(b, o[:, 0:width], m))
            ws.release(i, m)

        def keep(dst, scale=1.0, free=(), on=None):
            def sink(o, m):
                c = act.done(act.after(m, *free).activation(dst, o, ACTF.Copy, scale=scale))
                kept.append(c)
                return (c,)
            return sink

        kept = []

        def skewed(n, *stages):
            for step in range(n + len(stages) - 1):
                for s, stage in enumerate(stages):
                    if 0 <= step - s < n:
                        stage(step - s)

        def nsa(xT_ready, oT_hi, oT_lo):
            with ExitStack() as scope:
                def tile(name, shape, dt=F32):
                    return scope.enter_context(nc.sbuf_tensor("nsa_" + name, shape, dt))

                q = tile("q", [P, HEADS // 2, SEQ])
                keys = tile("keys", [P, 2 * GROUPS, SEQ])
                vals = tile("vals", [P, TB, VSW])
                pairs = tile("pairs", [P, 2 * GROUPS, SEQ])
                blocks = tile("blocks", [P, 2, LP, GROUPS * NB])
                pos = tile("pos", [P, 2, LP])
                w2 = tile("w2", [P, 2, 2, P])
                hid = tile("hid", [P, 2, CMP_HID])
                hidT = tile("hidT", [P, 2, 2, GROUPS * NB])
                k_cmp = tile("k_cmp", [P, GROUPS * NB])
                v_cmp = tile("v_cmp", [P, GROUPS, HD])
                gates = tile("gates", [P, TB, GATES])
                s1 = [tile(f"s1_{i}", [P, 2, SEQ]) for i in range(2)]
                s0 = [tile(f"s0_{i}", [P, 2, P]) for i in range(2)]
                sc = [tile(f"sc_{i}", [P, TB, NB]) for i in range(2)]
                pT = [tile(f"pT_{i}", [P, 1024]) for i in range(2)]
                nm = [tile(f"nm_{i}", [P, 6]) for i in range(2)]
                sums = [tile(f"sums_{i}", [P, 6]) for i in range(2)]
                wgt = [tile(f"wgt_{i}", [P, 6]) for i in range(2)]

                landed = small_landed.done(sp.after().dma_start(pos[:, :, :], t["cmp_pos"]), 16)
                landed = small_landed.done(sp.after().dma_start(w2[:, :, :, :], t["cmp_w2"]), 16)

                def pair_sink(i):
                    def sink(o, m):
                        a = act.done(act.after(m).activation(pairs[0:64, i, :], o[0:64, :], ACTF.Copy))
                        b = act.done(act.after(m).activation(pairs[64:P, i, 0:SEQ - 1], o[64:P, 1:SEQ], ACTF.Copy))
                        z = act.done(act.after(m).activation(pairs[64:P, i, SEQ - 1:SEQ], o[64:P, SEQ - 1:SEQ], ACTF.Copy))
                        kept.append(z)
                        return (z,)
                    return sink

                feature_tiles(3, SPARE, xT_ready, [pair_sink(0), pair_sink(1), pair_sink(2)])
                feature_tiles(3, SPARE, xT_ready, [pair_sink(3), keep(keys[:, 0, :]), keep(keys[:, 1, :])])
                for kv in range(2):
                    for g in range(GROUPS):
                        row = pairs[:, 2 * kv + g, :]
                        for part in range(2):
                            lp = slice(part * LP // 2, (part + 1) * LP // 2)
                            v = row[:, STRIDE * part:STRIDE * (part + NB)].rearrange(
                                "p (b l two) -> p l b two", l=LP // 2, two=2)[:, :, :, 0]
                            m = dve.done(dve.after(landed, *kept).tensor_tensor(
                                blocks[:, kv, lp, g * NB:(g + 1) * NB], v,
                                bcast(pos[:, kv, lp], 2, [P, LP // 2, NB]), ALU.add))
                blocks_ready = m
                for kv in range(2):
                    o = bank_for(ACC[kv])
                    for part in range(2):
                        i, w, _, there = ws.take()
                        pe.after(blocks_ready, *there)
                        for j in range(LP // 2):
                            lp = part * LP // 2 + j
                            ins = nc.tensor.matmul(o[0:GROUPS * NB, 0:CMP_HID], blocks[:, kv, lp, :],
                                                   w[:, j * CMP_HID:(j + 1) * CMP_HID],
                                                   start=(lp == 0), stop=(lp == LP - 1))
                        m = pe.done(ins)
                        ws.release(i, m)
                    m = act.done(act.after(m).activation(hid[0:GROUPS * NB, kv, :],
                                                         o[0:GROUPS * NB, 0:CMP_HID], ACTF.Gelu_apprx_tanh))
                    read_by(ACC[kv], m)
                hid_ready = m
                feature_tiles(3, SPARE, xT_ready, [keep(keys[:, 2, :]), keep(keys[:, 3, :]), keep(q[:, 0, :], HD ** -0.5)])
                feature_tiles(3, SPARE, xT_ready, [keep(q[:, j, :], HD ** -0.5) for j in (1, 2, 3)])

                o = bank_for(ACC[2])
                pe.after(hid_ready)
                n = GROUPS * NB
                for kv in range(2):
                    for h in range(2):
                        ins = nc.tensor.transpose(o[:, (2 * kv + h) * n:(2 * kv + h + 1) * n],
                                                  hid[0:n, kv, h * P:(h + 1) * P], ident[0:n, 0:n])
                m = pe.done(ins)
                m = dve.done(dve.after(m).tensor_copy(hidT[:, :, :, :].rearrange("p a b c -> p (a b c)"), o[:, 0:4 * n]))
                read_by(ACC[2], m)
                o = bank_for(ACC[3])
                pe.after(m)
                for h in range(2):
                    ins = nc.tensor.matmul(o[:, 0:n], w2[:, 0, h, :], hidT[:, 0, h, :], start=(h == 0), stop=(h == 1))
                m = pe.done(ins)
                kc_ready = act.done(act.after(m).activation(k_cmp[:, :], o[:, 0:n], ACTF.Copy))
                read_by(ACC[3], kc_ready)
                o = bank_for(ACC[3])
                for g in range(GROUPS):
                    for h in range(2):
                        ins = nc.tensor.matmul(o[0:NB, g * HD:(g + 1) * HD], hidT[:, 1, h, g * NB:(g + 1) * NB],
                                               w2[:, 1, h, 0:HD], start=(h == 0), stop=(h == 1))
                m = pe.done(ins)
                vc_ready = act.done(act.after(m).activation(
                    v_cmp[0:NB, :, :].rearrange("p g d -> p (g d)"), o[0:NB, 0:GROUPS * HD], ACTF.Copy))
                read_by(ACC[3], vc_ready)

                def vals_sink(b, o, m):
                    c = act.done(act.after(m).activation(vals[:, b, :], o, ACTF.Copy))
                    kept.append(c)
                    return (c,)
                token_tiles(VSW, SPARE, xT_ready, vals_sink)
                m = act.done(act.after(*kept).activation(gates[:, :, :], vals[:, :, VSW - GATES:VSW], ACTF.Sigmoid))
                cmp_gates = gates[:, :, :].rearrange("p b (h three) -> p b h three", three=3)[:, :, :, 0]
                gates_ready = dve.done(dve.after(m).tensor_tensor(
                    cmp_gates, cmp_gates, bcast(cst("cmp_row"), 2, [P, TB, HEADS]), ALU.mult))

                dist = cst("dist")
                cmp_dist = cst("cmp_dist").rearrange("p (b n) -> p b n", b=TB)
                made, soft, turned, read = {}, {}, {}, {}

                def scores(h):
                    g, half, base = h // 4, h // 2, 64 * (h % 2)
                    rows = slice(base, base + HD)
                    a, b = (0, 1) if h % 2 == 0 else (2, 3)
                    oa, ob = bank_for(a), bank_for(b)
                    pe.after(*kept, kc_ready)
                    q0, q1 = q[rows, half, 0:P], q[rows, half, P:SEQ]
                    for i, kk in enumerate((g, 2 + g)):
                        nc.tensor.matmul(oa[:, i * SEQ:(i + 1) * SEQ], q1, keys[rows, kk, :], start=True, stop=True)
                    for i, kk in enumerate((g, 2 + g)):
                        nc.tensor.matmul(ob[:, i * P:(i + 1) * P], q0, keys[rows, kk, 0:P], start=True, stop=True)
                    for i, qq in enumerate((q0, q1)):
                        ins = nc.tensor.matmul(ob[:, 2 * P + i * NB:2 * P + (i + 1) * NB], qq,
                                               k_cmp[rows, g * NB:(g + 1) * NB], start=True, stop=True)
                    made[h] = pe.done(ins)

                def softmax(h):
                    a, b = (0, 1) if h % 2 == 0 else (2, 3)
                    oa, ob = psum[a], psum[b]
                    z = h % 2
                    slope = -2.0 ** (-(h + 1))
                    free = (turned[h - 2],) if h >= 2 else ()
                    dve.after(made[h], *free)
                    m = dve.done(nc.vector.scalar_tensor_tensor(
                        s1[z][:, :, :], bcast(dist[:, P:3 * P], 1, [P, 2, SEQ]), slope,
                        oa[:, :].rearrange("p (a s) -> p a s", a=2), ALU.mult, ALU.add))
                    read_by(a, m)
                    nc.vector.scalar_tensor_tensor(
                        s0[z][:, :, :], bcast(dist[:, 0:P], 1, [P, 2, P]), slope,
                        ob[:, 0:2 * P].rearrange("p (a s) -> p a s", a=2), ALU.mult, ALU.add)
                    m = dve.done(nc.vector.scalar_tensor_tensor(
                        sc[z][:, :, :], cmp_dist, slope,
                        ob[:, 2 * P:2 * P + TB * NB].rearrange("p (a s) -> p a s", a=TB), ALU.mult, ALU.add))
                    read_by(b, m)
                    parts = [(s1[z], 0), (s0[z], 2), (sc[z], 4)]
                    dve.after(m)
                    for s, c in parts:
                        m = dve.done(nc.vector.tensor_reduce(nm[z][:, c:c + 2], s[:, :, :], AX_X, ALU.max, negate=True))
                    act.after(m)
                    for s, c in parts:
                        for i in range(2):
                            m = act.done(nc.scalar.activation(s[:, i, :], s[:, i, :], ACTF.Exp,
                                                              bias=nm[z][:, c + i:c + i + 1],
                                                              accum_out=sums[z][:, c + i:c + i + 1]))
                    m = dve.done(dve.after(m).reciprocal(sums[z][:, :], sums[z][:, :]))
                    dve.after(m, gates_ready)
                    for c, gate in ((0, gates[:, 1, 3 * h + 1:3 * h + 3]), (2, gates[:, 0, 3 * h + 1:3 * h + 3]),
                                    (4, gates[:, :, 3 * h])):
                        m = dve.done(nc.vector.tensor_tensor(wgt[z][:, c:c + 2], sums[z][:, c:c + 2], gate, ALU.mult))
                    dve.after(m)
                    for (s, c), w in zip(parts, (SEQ, P, NB)):
                        m = dve.done(nc.vector.tensor_tensor(s[:, :, :], s[:, :, :],
                                                             bcast(wgt[z][:, c:c + 2], 2, [P, 2, w]), ALU.mult))
                    soft[h] = m

                def transposes(h):
                    z = h % 2
                    oc, od = bank_for(4), bank_for(5)
                    pe.after(soft[h])
                    for i in range(2):
                        nc.tensor.transpose(oc[:, i * SEQ:i * SEQ + P], s0[z][:, i, :], ident)
                        nc.tensor.transpose(oc[:, i * SEQ + P:(i + 1) * SEQ], s1[z][:, i, 0:P], ident)
                        nc.tensor.transpose(od[:, i * P:(i + 1) * P], s1[z][:, i, P:SEQ], ident)
                    for i in range(TB):
                        ins = nc.tensor.transpose(od[0:NB, SEQ + i * P:SEQ + (i + 1) * P], sc[z][:, i, :], ident)
                    turned[h] = pe.done(ins)
                    free = (read[h - 2],) if h >= 2 else ()
                    act.after(turned[h], *free)
                    m = act.done(nc.scalar.activation(pT[z][:, 0:512], oc[:, :], ACTF.Copy))
                    read_by(4, m)
                    dve.after(turned[h], *free)
                    nc.vector.tensor_copy(pT[z][:, 512:512 + SEQ], od[:, 0:SEQ])
                    d = dve.done(nc.vector.tensor_copy(pT[z][0:NB, 768:1024], od[0:NB, SEQ:512]))
                    read_by(5, d)
                    soft[h] = (m, d)

                def values(h):
                    g, half, base, z = h // 4, h // 2, 64 * (h % 2), h % 2
                    rows = slice(base, base + HD)
                    bank = 6 + h % 2
                    o = bank_for(bank)[rows, 0:SEQ]
                    pe.after(*soft[h], vc_ready)
                    p = pT[z]
                    for i in range(2):
                        c = slice((2 * i + g) * HD, (2 * i + g + 1) * HD)
                        nc.tensor.matmul(o, vals[:, 0, c], p[:, i * SEQ:(i + 1) * SEQ], start=(i == 0), stop=False)
                        nc.tensor.matmul(o[:, P:SEQ], vals[:, 1, c], p[:, 512 + i * P:512 + (i + 1) * P],
                                         start=False, stop=False)
                    read[h] = pe.done(nc.tensor.matmul(o, v_cmp[0:NB, g, :], p[0:NB, 768:1024], start=False, stop=True))
                    hi, lo = oT_hi[rows, half, :], oT_lo[rows, half, :]
                    m = split_to(hi, lo, o, (read[h],))
                    read_by(bank, *m)
                    return m

                skewed(HEADS, lambda h: (scores(h), softmax(h)), transposes, values)
                kept.clear()
                meet()

        def hgrn(xT_ready, oT_hi, oT_lo):
            with ExitStack() as scope:
                def tile(name, shape, dt=F32):
                    return scope.enter_context(nc.sbuf_tensor("hg_" + name, shape, dt))

                names = ("q", "k", "g", "b", "k_end", "exp_b")
                own = tile("head", [P, len(names), SEQ])
                spare = xn[:, :, :].rearrange("p b d -> p (b d)").rearrange("p (n s) -> p n s", s=SEQ)
                head = [{n: t[:, i, :] for i, n in enumerate(names)} for t in (own, spare)]
                tmp, tmp2 = spare[:, len(names), :], spare[:, len(names) + 1, :]
                aT = [sig[0][:, i * P:(i + 1) * P] for i in range(2)]
                keT = [sig[1][:, i * P:(i + 1) * P] for i in range(2)]
                v = tile("v", [P, TB, HG * P])
                lbt = tile("lb", [P, 4 * HG])
                pair = [tile(f"pair{i}", [P, CH, P]) for i in range(2)]
                vm = tile("v_masked", [P, 4, P])
                state = tile("state", [P, CPB + 1, P])
                q_step = gains[:, 0:2 * D].rearrange("p (j t) -> p j t", j=CH)
                q_wide = tile("q_chunk", [P, CPB * (P + CH)])
                q_chunk = q_wide[:, 0:CPB * P].rearrange("p (c t) -> p c t", c=CPB)

                zeroed = pool.done(pool.after(*gains_read[0]).memset(q_step[:, :, :], 0.0))
                zeroed = pool.done(nc.gpsimd.memset(q_chunk[:, :, :], 0.0))
                step_cells = gains[:, :].rearrange("p (j x) -> p j x", j=CH)[:, :, 0:P].rearrange(
                    "p j (c s) -> p c j s", s=CH)[:, :, :, 0]
                chunk_cells = q_wide[:, :].rearrange("p (c x) -> p c x", c=CPB)[:, :, 0:CH]

                def v_sink(half):
                    def sink(b, o, m):
                        c = act.done(act.after(m).activation(v[:, b, half * SEQ:(half + 1) * SEQ], o, ACTF.Copy))
                        kept.append(c)
                        return (c,)
                    return sink
                for half in range(2):
                    token_tiles(SEQ, SPARE, xT_ready, v_sink(half))
                v_ready = tuple(kept)
                kept.clear()
                lb = small[:, 0:HG]
                lb_diff, lb_soft, lb_val, lb_rest = (lbt[:, i * HG:(i + 1) * HG] for i in range(4))
                m = dve.done(dve.after(s_mark).tensor_tensor(lb_diff, lb, lb, ALU.subtract))
                m = act.done(act.after(m).activation(lb_soft, lb_diff, ACTF.Exp))
                m = dve.done(dve.after(m).reciprocal(lb_val, lb_soft))
                m = dve.done(dve.after(m).tensor_tensor(lb_soft, lb_soft, lb_val, ALU.mult))
                m = dve.done(dve.after(m).tensor_tensor(lb_val, lb_soft, lb_soft, ALU.subtract))
                lb_ready = dve.done(dve.after(m).tensor_scalar(lb_rest, lb_val, -1.0, 1.0, ALU.mult, ALU.add))

                done = {}

                def gates(h):
                    z = head[h % 2]
                    free = done["read", h - 2] if h >= 2 else ()

                    def silu_sink(name):
                        def sink(o, m):
                            a = act.done(act.after(m, *free).activation(z[name], o, ACTF.Sigmoid))
                            d = dve.done(dve.after(a).tensor_tensor(z[name], z[name], o, ALU.mult))
                            done[name, h] = d
                            return (a, d)
                        return sink

                    def f_sink(o, m):
                        act.after(m, *free, *tmp_free[0])
                        nc.scalar.activation(tmp, o, ACTF.Sigmoid)
                        done["f", h] = act.done(nc.scalar.activation(z["k"], o, ACTF.Sigmoid, scale=-1.0))
                        return (done["f", h],)

                    feature_tiles(3, (4, 5), xT_ready, [silu_sink("q"), f_sink, silu_sink("g")])
                    val, rest = lb_val[:, h:h + 1], lb_rest[:, h:h + 1]
                    dve.after(done["f", h], lb_ready)
                    nc.vector.tensor_scalar(z["k"], z["k"], rest, None, ALU.mult)
                    m = dve.done(nc.vector.tensor_scalar(tmp, tmp, rest, val, ALU.mult, ALU.add))
                    m = dve.done(dve.after(m).tensor_scalar(tmp, tmp, F_FLOOR, None, ALU.max))
                    m = dve.done(dve.after(m).tensor_scalar(tmp2, tmp, LN_SPLIT, 1.0, ALU.mult, ALU.min))
                    m = dve.done(dve.after(m).tensor_scalar(tmp, tmp, LN_RANGE, None, ALU.max))
                    act.after(m)
                    nc.scalar.activation(tmp, tmp, ACTF.Ln)
                    m = act.done(nc.scalar.activation(tmp2, tmp2, ACTF.Ln))
                    m = dve.done(dve.after(m).tensor_tensor(tmp, tmp, tmp2, ALU.add))
                    m = dve.done(dve.after(m).tensor_tensor_scan(z["b"], cst("restart"), tmp, 0.0, ALU.mult, ALU.add))
                    chunks = z["b"].rearrange("p (c j) -> p c j", j=CH)
                    m = dve.done(dve.after(m).tensor_tensor(
                        tmp2.rearrange("p (c j) -> p c j", j=CH),
                        chunks[:, :, CH - 1:CH].to_broadcast([P, TB * CPB, CH]), chunks, ALU.subtract))
                    act.after(m)
                    nc.scalar.activation(z["k_end"], tmp2, ACTF.Exp)
                    m = act.done(nc.scalar.activation(z["exp_b"], z["b"], ACTF.Exp))
                    done["gates", h] = dve.done(dve.after(m).tensor_tensor(z["k_end"], z["k_end"], z["k"], ALU.mult))
                    tmp_free[0] = (done["gates", h],)

                tmp_free = [()]
                units = [(h, b) for h in range(HG) for b in range(TB)]

                def decays(u):
                    h, b = units[u]
                    z = head[h % 2]
                    free = (done["a", u - 2],) if u >= 2 else ()
                    bb = z["b"].rearrange("p (c j) -> p c j", j=CH)[:, b * CPB:(b + 1) * CPB, :]
                    p4 = pair[u % 2][:, :, :].rearrange("p j (c s) -> p j c s", c=CPB)
                    m = dve.done(dve.after(done["gates", h], *free).tensor_tensor(
                        p4, bcast(bb.rearrange("p c j -> p j c"), 3, [P, CH, CPB, CH]),
                        bcast(bb, 1, [P, CH, CPB, CH]), ALU.subtract))
                    flat = pair[u % 2][:, :, :].rearrange("p j s -> p (j s)")
                    m = dve.done(dve.after(m).tensor_scalar(flat, flat, 0.0, None, ALU.min))
                    done["exp", u] = act.done(act.after(m).activation(flat, flat, ACTF.Exp))

                def products(u):
                    h, b = units[u]
                    z = head[h % 2]
                    tok = slice(b * P, (b + 1) * P)
                    m = dve.done(dve.after(done["exp", u]).tensor_tensor(
                        pair[u % 2][:, :, :], pair[u % 2][:, :, :], bcast(z["k"][:, tok], 1, [P, CH, P]), ALU.mult))
                    free = (done["a", u - 1],) if u >= 1 else ()
                    q_ready = pool.done(pool.after(zeroed, done["q", h], *free).tensor_copy(
                        step_cells, z["q"][:, tok].rearrange("p (c j) -> p c j", j=CH)))
                    o = bank_for(6)
                    pe.after(done["gates", h])
                    t = pe.done(nc.tensor.transpose(o[:, 0:P], z["k_end"][:, tok], ident))
                    free = (done["kv", u - 2, 1],) if u >= 2 else ()
                    keys_ready = act.done(act.after(t, *free).activation(keT[u % 2], o[:, 0:P], ACTF.Copy))
                    read_by(6, keys_ready)

                    def chunk_products(half):
                        last = (u, 0) if half else (u - 1, 1)
                        free = (done["kv", last[0], last[1]],) if last[0] >= 0 else ()
                        v_masked = pool.done(pool.after(*v_ready, *free).tensor_tensor(
                            vm[:, :, :], bcast(v[:, b, h * P:(h + 1) * P], 1, [P, 4, P]),
                            bcast(cst("chunk_row")[:, 4 * half:4 * half + 4], 2, [P, 4, P]), ALU.mult))
                        o = bank_for(ACC[half])
                        pe.after(keys_ready, v_masked)
                        done["kv", u, half] = pe.done(nc.tensor.matmul(
                            o[:, :], keT[u % 2], vm[:, :, :].rearrange("p c v -> p (c v)"), start=True, stop=True))

                    chunk_products(0)
                    o = bank_for(7)
                    pe.after(m, q_ready)
                    for j in range(CH):
                        ins = nc.tensor.matmul(o[:, 0:P], pair[u % 2][:, j, :], q_step[:, j, :],
                                               start=(j == 0), stop=(j == CH - 1))
                    done["a", u] = pe.done(ins)
                    chunk_products(1)

                def outputs(u):
                    h, b = units[u]
                    z = head[h % 2]
                    tok = slice(b * P, (b + 1) * P)
                    free = (done["out", u - 2],) if u >= 2 else ()
                    own_pairs = dve.done(dve.after(done["a", u], *free).tensor_tensor(
                        aT[u % 2], psum[7][:, 0:P], cst("chunk_pair"), ALU.mult))
                    read_by(7, own_pairs)
                    free = (done["out", u - 1],) if u >= 1 else ()
                    by_chunk = lambda a: a[:, tok].rearrange("p (c j) -> p c j", j=CH)
                    q_ready = dve.done(dve.after(zeroed, done["q", h], *free).tensor_tensor(
                        chunk_cells, by_chunk(z["q"]), by_chunk(z["exp_b"]), ALU.mult))
                    if b == 0:
                        s = dve.done(nc.vector.memset(state[:, 0, :], 0.0))
                    else:
                        s = done["state", u - 1]
                    for half in range(2):
                        o = psum[ACC[half]]
                        for c4 in range(4):
                            c = b * CPB + 4 * half + c4
                            if c == TB * CPB - 1:
                                continue
                            end = c * CH + CH - 1
                            s = dve.done(dve.after(done["kv", u, half], s).scalar_tensor_tensor(
                                state[:, (c + 1) % (CPB + 1), :], state[:, c % (CPB + 1), :],
                                z["exp_b"][:, end:end + 1], o[:, c4 * P:(c4 + 1) * P], ALU.mult, ALU.add))
                        read_by(ACC[half], s)
                    done["state", u] = s
                    bank = ACC[2 + h % 2]
                    if b == 0:
                        bank_for(bank)
                    o = psum[bank][:, b * P:(b + 1) * P]
                    pe.after(own_pairs, q_ready, s, *v_ready)
                    nc.tensor.matmul(o, v[:, b, h * P:(h + 1) * P], aT[u % 2], start=True, stop=False)
                    for c in range(CPB):
                        ins = nc.tensor.matmul(o, state[:, (b * CPB + c) % (CPB + 1), :], q_chunk[:, c, :],
                                               start=False, stop=(c == CPB - 1))
                    done["out", u] = pe.done(ins)

                def norm(h):
                    z = head[h % 2]
                    bank = ACC[2 + h % 2]
                    o_psum = psum[bank][:, 0:SEQ]
                    made = done["out", 2 * h + 1]
                    m = act.done(act.after(made).activation(z["exp_b"], o_psum, ACTF.Square))
                    o = bank_for(6)
                    pe.after(m)
                    m = pe.done(nc.tensor.matmul(o[:, 0:SEQ], cst("mean"), z["exp_b"], start=True, stop=True))
                    m = dve.done(dve.after(m).tensor_scalar(z["k_end"], o[:, 0:SEQ], RMS_EPS, None, ALU.add))
                    read_by(6, m)
                    m = act.done(act.after(m).activation(z["k_end"], z["k_end"], ACTF.Sqrt))
                    m = dve.done(dve.after(m).reciprocal(z["k_end"], z["k_end"]))
                    m = dve.done(dve.after(m).scalar_tensor_tensor(z["k_end"], o_psum, small[:, HG:HG + 1],
                                                                   z["k_end"], ALU.mult, ALU.mult))
                    read_by(bank, m)
                    m = dve.done(dve.after(m, done["g", h]).tensor_tensor(z["k_end"], z["k_end"], z["g"], ALU.mult))
                    done["read", h] = split_to(oT_hi[:, HG + h, :], oT_lo[:, HG + h, :], z["k_end"], (m,))

                gates(0)
                gates(1)
                for step in range(len(units) + 2):
                    if step >= 2:
                        outputs(step - 2)
                        if units[step - 2][1] == TB - 1:
                            norm(units[step - 2][0])
                    if 1 <= step <= len(units):
                        products(step - 1)
                    if step < len(units):
                        decays(step)
                    h = step // TB + 1
                    if step % TB == 1 and 2 <= h < HG:
                        gates(h)
                meet()

        def mixer(xT_ready):
            with ExitStack() as scope:
                oT_hi = scope.enter_context(nc.sbuf_tensor("mix_oT_hi", [P, KD, SEQ], F32R))
                oT_lo = scope.enter_context(nc.sbuf_tensor("mix_oT_lo", [P, KD, SEQ], F32R))
                nsa(xT_ready, oT_hi, oT_lo)
                hgrn(xT_ready, oT_hi, oT_lo)
                gains_read[0] = ((pe, pe.count), (pool, pool.count))
                g_mark = load_gains(2)
                made = out_product(lambda k: oT_hi[:, k, :], lambda k: oT_lo[:, k, :],
                                   {k: ((act, act.count), (dve, dve.count)) for k in range(KD)}, 3, KD)
                return made, g_mark

        def add_mask(h, s, o, made, free):
            return dve.done(dve.after(made, *free).tensor_tensor(s, o, cst("causal"), ALU.add))

        def attention(n, tile, scores, add_bias, value, scale, dv, sink, score_banks, turn_banks, out_banks):
            s = [tile(f"s{i}", [P, 3 * P]) for i in range(2)]
            pT = [tile(f"pT{i}", [P, 3 * P]) for i in range(2)]
            nm = [tile(f"nm{i}", [P, 2]) for i in range(2)]
            sums = [tile(f"sums{i}", [P, 2]) for i in range(2)]
            soft, turned, read = {}, {}, {}
            spans = ((0, 0, P), (1, P, 3 * P))

            def softmax(h):
                z = h % 2
                bank = score_banks[z]
                o = bank_for(bank)
                scores(h, 0, o[:, 0:P], P)
                made = pe.done(scores(h, 1, o[:, P:3 * P], SEQ))
                free = (turned[h - 2],) if h >= 2 else ()
                m = add_bias(h, s[z][:, :], o[:, 0:3 * P], made, free)
                read_by(bank, m)
                dve.after(m)
                for b, c0, c1 in spans:
                    m = dve.done(nc.vector.tensor_reduce(nm[z][:, b:b + 1], s[z][:, c0:c1], AX_X, ALU.max, negate=True))
                if scale != 1.0:
                    m = dve.done(dve.after(m).tensor_scalar(nm[z][:, :], nm[z][:, :], scale, None, ALU.mult))
                act.after(m)
                for b, c0, c1 in spans:
                    m = act.done(nc.scalar.activation(s[z][:, c0:c1], s[z][:, c0:c1], ACTF.Exp, scale=scale,
                                                      bias=nm[z][:, b:b + 1], accum_out=sums[z][:, b:b + 1]))
                m = dve.done(dve.after(m).reciprocal(sums[z][:, :], sums[z][:, :]))
                dve.after(m)
                for b, c0, c1 in spans:
                    m = dve.done(nc.vector.tensor_scalar(s[z][:, c0:c1], s[z][:, c0:c1], sums[z][:, b:b + 1], None, ALU.mult))
                soft[h] = m

            def transposes(h):
                z = h % 2
                bank = turn_banks[z]
                o = bank_for(bank)
                pe.after(soft[h])
                for i in range(3):
                    ins = nc.tensor.transpose(o[:, i * P:(i + 1) * P], s[z][:, i * P:(i + 1) * P], ident)
                turned[h] = pe.done(ins)
                free = (read[h - 2],) if h >= 2 else ()
                soft[h] = act.done(act.after(turned[h], *free).activation(pT[z][:, :], o[:, 0:3 * P], ACTF.Copy))
                read_by(bank, soft[h])

            def values(h):
                z = h % 2
                bank = out_banks[z]
                base = dv * h % P
                o = bank_for(bank)[base:base + dv, 0:SEQ]
                pe.after(soft[h])
                nc.tensor.matmul(o, value(h, 0), pT[z][:, 0:SEQ], start=True, stop=False)
                read[h] = pe.done(nc.tensor.matmul(o[:, P:SEQ], value(h, 1), pT[z][:, SEQ:3 * P], start=False, stop=True))
                read_by(bank, *sink(h, o, read[h]))

            return softmax, transposes, values

        def fox(xT_ready):
            with ExitStack() as scope:
                def tile(name, shape, dt=F32):
                    return scope.enter_context(nc.sbuf_tensor("fox_" + name, shape, dt))

                oT_hi, oT_lo = tile("oT_hi", [P, KD, SEQ], F32R), tile("oT_lo", [P, KD, SEQ], F32R)
                v = tile("v", [P, TB, D])
                q = [tile(f"q{i}", [P, SEQ]) for i in range(2)]
                k = [tile(f"k{i}", [P, SEQ]) for i in range(2)]
                z_f, ones, cum = (tile(x, [FOX_H, SEQ]) for x in ("f", "ones", "cum"))
                spare = neg = tile("spare", [FOX_H, SEQ])
                k_cum = tile("k_cum", [P, FOX_H * SEQ])
                q_cum = tile("q_cum", [P, TB, FOX_H])
                bias = [tile(f"bias{i}", [P, 3 * P]) for i in range(2)]

                ones_ready = pool.done(pool.after().memset(ones[:, :], 1.0))

                fin = {}

                def f_sink(o, m):
                    fin["f"] = act.done(act.after(m, s_mark).activation(
                        z_f[:, :], o[0:FOX_H, :], ACTF.Identity, bias=small[0:FOX_H, HG + 1:HG + 2]))
                    return (fin["f"],)
                feature_tiles(1, (6, 7), xT_ready, [f_sink])
                m = act.done(act.after(fin["f"]).activation(spare[:, :], z_f[:, :], ACTF.Abs))
                m = act.done(act.after(m).activation(spare[:, :], spare[:, :], ACTF.Exp, scale=-1.0))
                m = act.done(act.after(m).activation(spare[:, :], spare[:, :], ACTF.Ln, bias=1.0))
                m = dve.done(dve.after(m).scalar_tensor_tensor(z_f[:, :], z_f[:, :], 0.0, spare[:, :], ALU.min, ALU.subtract))
                m = dve.done(dve.after(m, ones_ready).tensor_tensor_scan(cum[:, :], ones[:, :], z_f[:, :], 0.0, ALU.mult, ALU.add))
                o = bank_for(5)
                pe.after(m)
                for b in range(TB):
                    ins = nc.tensor.transpose(o[:, b * FOX_H:(b + 1) * FOX_H], cum[:, b * P:(b + 1) * P],
                                              ident[0:FOX_H, 0:FOX_H])
                q_cum_ready = dve.done(dve.after(pe.done(ins)).tensor_copy(
                    q_cum[:, :, :].rearrange("p b h -> p (b h)"), o[:, 0:TB * FOX_H]))
                read_by(5, q_cum_ready)
                m = dve.done(dve.after(m).tensor_scalar(neg[:, :], cum[:, :], -1.0, None, ALU.mult))
                m = small_landed.done(sp.after(m).dma_start(t["cum_scratch"], neg[:, :]), 16)
                k_cum_ready = small_landed.done(sp.after(m).dma_start(
                    k_cum[:, :], t["cum_scratch"].rearrange("h s -> (h s)").unsqueeze(0).to_broadcast([P, FOX_H * SEQ])), 16)
                def v_sink(i):
                    def sink(b, o, m):
                        c = act.done(act.after(m).activation(v[:, b, i * SEQ:(i + 1) * SEQ], o, ACTF.Copy))
                        kept.append(c)
                        return (c,)
                    return sink
                for i in range(4):
                    token_tiles(SEQ, (6, 7), xT_ready, v_sink(i))

                qk = {}
                softdone = {}
                biased = {}

                def scores(h, b, o, width):
                    z = h // 2 % 2
                    rows = slice(64 * (h % 2), 64 * (h % 2) + 64)
                    pe.after(*qk[h // 2])
                    return nc.tensor.matmul(o, q[z][rows, b * P:(b + 1) * P], k[z][rows, 0:width], start=True, stop=True)

                def key_bias(h):
                    z = h % 2
                    free = (biased[h - 2],) if h >= 2 else ()
                    pool.after(k_cum_ready, *free)
                    kc = k_cum[:, h * SEQ:(h + 1) * SEQ]
                    nc.gpsimd.tensor_tensor(bias[z][:, 0:P], cst("causal")[:, 0:P], kc[:, 0:P], ALU.add)
                    return pool.done(nc.gpsimd.tensor_tensor(bias[z][:, P:3 * P], cst("causal")[:, P:3 * P], kc, ALU.add))

                def add_bias(h, s, o, made, free):
                    ready = key_bias(h)
                    dve.after(made, ready, q_cum_ready, *free)
                    for b, c0, c1 in ((0, 0, P), (1, P, 3 * P)):
                        m = dve.done(nc.vector.scalar_tensor_tensor(
                            s[:, c0:c1], o[:, c0:c1], q_cum[:, b, h:h + 1], bias[h % 2][:, c0:c1], ALU.add, ALU.add))
                    biased[h] = m
                    return m

                def sink(h, o, m):
                    rows = slice(64 * (h % 2), 64 * (h % 2) + 64)
                    return split_to(oT_hi[rows, h // 2, :], oT_lo[rows, h // 2, :], o, (m, *kept))

                softmax, transposes, values = attention(
                    FOX_H, tile, scores, add_bias, lambda h, b: v[:, b, h * 64:(h + 1) * 64], 1.0, 64, sink,
                    (0, 1), (2, 3), (4, 5))

                def first(h):
                    if h % 2 == 0:
                        z = h // 2 % 2
                        got = []
                        free = (softdone[h // 2 - 2],) if h // 2 >= 2 else ()

                        def to(dst, scale):
                            def s(o, m):
                                got.append(act.done(act.after(m, *free).activation(dst[:, :], o, ACTF.Copy, scale=scale)))
                                return (got[-1],)
                            return s
                        feature_tiles(2, (6, 7), xT_ready, [to(q[z], 64 ** -0.5), to(k[z], 1.0)])
                        qk[h // 2] = got
                    if h == 0:
                        pe.after(*kept)
                    softmax(h)
                    if h % 2:
                        softdone[h // 2] = (pe, pe.count)

                skewed(FOX_H, first, transposes, values)
                kept.clear()
                made = out_product(lambda i: oT_hi[:, i, :], lambda i: oT_lo[:, i, :],
                                   {k: ((act, act.count), (dve, dve.count)) for k in range(KD)}, 3, KD)
                return made

        def shared_kv(xT_ready, g_mark, ckv_hi, ckv_lo, k_rope, tmp):
            got = []

            def c_sink(b, o, m):
                r = rms_rows(o, xn[:, b, 0:KL], KL, b, (m, g_mark), xn_read[0])
                got.append(r)
                return (r,)
            token_tiles(KL, SPARE, xT_ready, c_sink)
            gains_read[0] = tuple(got)
            fin = []

            def rope_sink(o, m):
                fin.append(dve.done(dve.after(m).tensor_tensor(k_rope[:, :], o, cst("cos"), ALU.mult)))
                return (fin[-1],)

            def swap_sink(o, m):
                a = dve.done(dve.after(m).tensor_tensor(tmp[:, :], o, cst("sin"), ALU.mult))
                fin.append(dve.done(dve.after(a, fin[0]).tensor_tensor(k_rope[:, :], k_rope[:, :], tmp[:, :], ALU.add)))
                return (a,)
            feature_tiles(2, SPARE, xT_ready, [rope_sink, swap_sink])
            marks = turn([(b, 0, xn[:, b, :], lambda b=b: got[b]) for b in range(TB)], KL // P, ckv_hi, ckv_lo, ())
            xn_read[0] = ((pe, pe.count),)
            return marks, fin[-1]

        def mla(xT_ready, g_mark, ckv_hi, ckv_lo, ckv_ready, k_rope, rope_ready):
            with ExitStack() as scope:
                def tile(name, shape, dt=F32):
                    return scope.enter_context(nc.sbuf_tensor("mla_" + name, shape, dt))

                o2_hi, o2_lo = tile("oT_hi", [P, KD, SEQ], F32R), tile("oT_lo", [P, KD, SEQ], F32R)
                cq_hi, cq_lo = tile("cqT_hi", [P, QL // P, SEQ], F32R), tile("cqT_lo", [P, QL // P, SEQ], F32R)
                qn2, kn2 = ([tile(f"{x}{i}", [P, 2, SEQ]) for i in range(2)] for x in ("q_nope", "k_nope"))
                qr2 = [tile(f"q_rope{i}", [P, SEQ]) for i in range(2)]
                v2 = [tile(f"v{i}", [P, TB, 2 * P]) for i in range(2)]
                qs = tile("q_swap", [P, SEQ])
                got = []

                def c_sink(b, o, m):
                    r = rms_rows(o, xn[:, b, 0:QL], QL, b, (m, g_mark), xn_read[0])
                    got.append(r)
                    return (r,)
                token_tiles(QL, SPARE, xT_ready, c_sink)
                x_free = (pe, pe.count)
                gains_read[0] = tuple(got)
                cq_ready = turn([(b, 0, xn[:, b, :], lambda b=b: got[b]) for b in range(TB)], QL // P, cq_hi, cq_lo, ())
                xn_read[0] = ((pe, pe.count),)

                pair_ready = {}
                pair_read = {}

                def project(p):
                    i, hi, lo, there = ws.take()
                    pe.after(*there)
                    free = pair_read.get(p - 2, ())
                    qn, kn, qr, v = qn2[p % 2], kn2[p % 2], qr2[p % 2], v2[p % 2]
                    marks = []
                    kq, kk = QL // P, KL // P

                    def one(bank, cols, k_tiles, a_hi, a_lo):
                        o = bank_for(bank)
                        ready = cq_ready if a_hi is cq_hi else ckv_ready
                        return o, pe.done(feature_major(o[:, 0:SEQ], hi, lo, cols, k_tiles, a_hi, a_lo, ready))
                    for j in range(2):
                        o, m = one(6 + j, lambda k: 4 * P * k + j * P, kq, cq_hi, cq_lo)
                        c = act.done(act.after(m, *free).activation(qn[:, j, :], o[:, 0:SEQ], ACTF.Copy))
                        read_by(6 + j, c)
                        marks.append(c)
                    o, m = one(6, lambda k: 4 * P * k + 2 * P, kq, cq_hi, cq_lo)
                    r = dve.done(dve.after(m, *free).tensor_tensor(qr[:, :], o[:, 0:SEQ], cst("cos"), ALU.mult))
                    read_by(6, r)
                    o, m = one(7, lambda k: 4 * P * k + 3 * P, kq, cq_hi, cq_lo)
                    r = dve.done(dve.after(m, *free).tensor_tensor(qs[:, :], o[:, 0:SEQ], cst("sin"), ALU.mult))
                    read_by(7, r)
                    marks.append(dve.done(dve.after(r).tensor_tensor(qr[:, :], qr[:, :], qs[:, :], ALU.add)))
                    at = kq * 4 * P
                    for j in range(2):
                        o, m = one(6 + j, lambda k: at + 2 * P * k + j * P, kk, ckv_hi, ckv_lo)
                        c = act.done(act.after(m, *free).activation(kn[:, j, :], o[:, 0:SEQ], ACTF.Copy))
                        read_by(6 + j, c)
                        marks.append(c)
                    at2 = at + kk * 2 * P
                    for b in range(TB):
                        o = bank_for(6 + b)
                        m = pe.done(token_major(o[:, 0:2 * P], hi, lo, lambda k: at2 + 2 * P * k, 2 * P, range(kk),
                                                lambda k: ckv_hi[:, k, :], lambda k: ckv_lo[:, k, :], b, True, True,
                                                ckv_ready))
                        c = act.done(act.after(m, *free).activation(v[:, b, :], o[:, 0:2 * P], ACTF.Copy))
                        read_by(6 + b, c)
                        marks.append(c)
                    ws.release(i, m)
                    pair_ready[p] = marks

                def scores(h, b, o, width):
                    j = h % 2
                    rows = slice(64 * j, 64 * j + 64)
                    pe.after(*pair_ready[h // 2], rope_ready)
                    qn, kn, qr = qn2[h // 2 % 2], kn2[h // 2 % 2], qr2[h // 2 % 2]
                    nc.tensor.matmul(o, qn[:, j, b * P:(b + 1) * P], kn[:, j, 0:width], start=True, stop=False)
                    return nc.tensor.matmul(o, qr[rows, b * P:(b + 1) * P], k_rope[rows, 0:width], start=False, stop=True)

                def halves(h):
                    return (xT_hi, xT_lo) if h < KD else (o2_hi, o2_lo)

                def sink(h, o, m):
                    hi, lo = halves(h)
                    return split_to(hi[:, h % KD, :], lo[:, h % KD, :], o, (m, x_free))

                softmax, transposes, values = attention(
                    MLA_H, tile, scores, add_mask, lambda h, b: v2[h // 2 % 2][:, b, h % 2 * P:h % 2 * P + P],
                    192 ** -0.5, P, sink, (0, 1), (2, 3), (4, 5))

                def first(h):
                    if h % 2 == 0:
                        project(h // 2)
                    softmax(h)

                def last(h):
                    values(h)
                    if h % 2:
                        pair_read[h // 2] = ((pe, pe.count),)

                skewed(MLA_H, first, transposes, last)
                made = out_product(lambda h: halves(h)[0][:, h % KD, :], lambda h: halves(h)[1][:, h % KD, :],
                                   {k: ((act, act.count), (dve, dve.count)) for k in range(MLA_H)}, 6, MLA_H)
                return made

        def ple(layer, xT_ready, xs_ready):
            meet()
            with ExitStack() as scope:
                def tile(name, shape, dt=F32):
                    return scope.enter_context(nc.sbuf_tensor(f"ple{layer}_" + name, shape, dt))

                pT = tile("pT", [P, 2, SEQ])
                pT_hi, pT_lo = tile("pT_hi", [P, 2, SEQ], F32R), tile("pT_lo", [P, 2, SEQ], F32R)
                proj = tile("proj", [P, TB, D])
                z = tile("z", [P, TB, D])
                bias = tile("bias", [P, D])
                small_landed.done(sp.after((pe, pe.count)).dma_start(pT[:, :, :], t["pT"][layer, :, :, :]), 16)
                landed = small_landed.done(sp.after().dma_start(
                    bias[:, :], t["gains"][14 + layer:15 + layer, 0:D].to_broadcast([P, D])), 16)
                ready = split_to(pT_hi[:, :, :], pT_lo[:, :, :], pT[:, :, :], (landed,))
                ready = {k: ready for k in range(2)}
                made = out_product(lambda k: pT_hi[:, k, :], lambda k: pT_lo[:, k, :], ready, 1, 2, per=2)
                for b in range(TB):
                    for half in range(2):
                        c = slice(512 * half, 512 * (half + 1))
                        m = act.done(act.after(made[b]).activation(proj[:, b, c], psum[ACC[2 * b + half]][:, :], ACTF.Copy))
                        read_by(ACC[2 * b + half], m)
                proj_ready = m
                made = out_product(lambda k: xT_hi[:, k, :], lambda k: xT_lo[:, k, :], xT_ready, 3, KD)
                xT_read[0] = (made[-1],)

            def add(b):
                for half in range(2):
                    c = slice(512 * half, 512 * (half + 1))
                    bank = ACC[2 * b + half]
                    m = dve.done(dve.after(made[b], landed).tensor_tensor(z[:, b, c], psum[bank][:, :], bias[:, c], ALU.add))
                    read_by(bank, m)
                    m = act.done(act.after(m).activation(z[:, b, c], z[:, b, c], ACTF.Sigmoid))
                    m = dve.done(dve.after(m, proj_ready).tensor_tensor(z[:, b, c], z[:, b, c], proj[:, b, c], ALU.mult))
                    m = dve.done(dve.after(m, xs_ready).tensor_tensor(x[:, b, c], x[:, b, c], z[:, b, c], ALU.add))
                return m
            return add

        stopping = False
        xT_read = [()]
        xn_read = [()]

        def add_block(b, scale, made, ready):
            for half in range(2):
                xs = x[:, b, 512 * half:512 * (half + 1)]
                bank = ACC[2 * b + half]
                m = dve.done(dve.after(made[b], *ready).scalar_tensor_tensor(
                    xs, psum[bank][:, :], scale, xs, ALU.mult, ALU.add))
                read_by(bank, m)
            return m

        def scale_x(x_ready):
            return act.done(act.after(*x_ready, (pe, pe.count)).activation(x[:, :, :], x[:, :, :], ACTF.Copy, scale=ALPHA))

        def turn_made(make, src):
            made = []

            def one(b, c):
                made.append(make(b, c))
                return made[-1]
            pieces = [(b, k0, src(b), lambda b=b, k0=k0: one(b, slice(k0 * P, (k0 + 4) * P)))
                      for b in range(TB) for k0 in range(0, KD, 4)]
            marks = turn(pieces, KD, xT_hi, xT_lo, xT_read[0])
            gains_read[0] = tuple(made)
            return marks, made

        def next_rms(add, g_mark, in_place=False):
            roots = [rms_root(x[:, b, :], D, b, (add(b),)) for b in range(TB)]
            dst = x if in_place else xn
            free = () if in_place else xn_read[0]
            marks, made = turn_made(lambda b, c: rms_apply(x[:, b, :], dst[:, b, :], b, c, (roots[b], g_mark, *free)),
                                    lambda b: dst[:, b, :])
            if not in_place:
                xn_read[0] = ((pe, pe.count),)
            return marks, made

        def next_ln(add, g_mark, turned=True):
            roots = []
            for b in range(TB):
                m = statistics(x[:, b, :], D, b, (add(b),))
                roots.append((root(b, mv[:, b, 1:2], LN_EPS, m), m))
            make = lambda b, c: ln_apply(b, c, (*roots[b], g_mark))
            if not turned:
                return None, [make(b, slice(0, D)) for b in range(TB)]
            marks, made = turn_made(make, lambda b: x[:, b, :])
            if stopping:
                return marks, made
            return marks, scale_x(made)

        def finish(ready):
            m = out_landed.done(sp.after(*ready).dma_start(out.rearrange("(b p) d -> p b d", p=P), x[:, :, :]), 16)
            sp.after(m)

        g_mark = g_first
        pe.after(c_mark)
        xT_ready, _ = next_rms(lambda b: x_mark[b], g_mark)
        g_mark = load_gains(1)
        made = ffn(xT_ready)
        xT_read[0] = (made[-1],)
        if stop == 1:
            return finish([add_block(b, 0.5, made, ()) for b in range(TB)])

        xT_ready, _ = next_rms(lambda b: add_block(b, 0.5, made, ()), g_mark)
        meet()
        made, g_mark = mixer(xT_ready)
        xT_read[0] = (made[-1],)
        if stop == 2:
            return finish([add_block(b, 1.0, made, ()) for b in range(TB)])

        xT_ready, _ = next_rms(lambda b: add_block(b, 1.0, made, ()), g_mark)
        g_mark = load_gains(3)
        made = ffn(xT_ready)
        xT_read[0] = (made[-1],)
        xT_ready, x_ready = next_rms(lambda b: add_block(b, 0.5, made, ()), g_mark, in_place=True)
        if stop == 3:
            return finish(x_ready)
        xs_ready = scale_x(x_ready)

        for layer in range(2):
            base = 4 + 4 * layer
            if layer == 1:
                ckv_hi = sb("ckvT_hi", [P, KL // P, SEQ], F32R)
                ckv_lo = sb("ckvT_lo", [P, KL // P, SEQ], F32R)
                k_rope = sb("k_rope", [P, SEQ])
                g_mark = load_gains(12)
                ckv_ready, rope_ready = shared_kv(xT_ready, g_mark, ckv_hi, ckv_lo, k_rope, sig[0])
            g_mark = load_gains(base)
            made = ffn(xT_ready)
            xT_read[0] = (made[-1],)
            stopping = stop == 4 + 4 * layer
            xT_ready, xs_ready = next_ln(lambda b: add_block(b, 0.5, made, (xs_ready,)), g_mark)
            if stopping:
                return finish(xs_ready)
            if layer == 0:
                g_mark = load_gains(base + 1)
                made = fox(xT_ready)
            else:
                made = mla(xT_ready, load_gains(13), ckv_hi, ckv_lo, ckv_ready, k_rope, rope_ready)
                g_mark = load_gains(base + 1)
            xT_read[0] = (made[-1],)
            stopping = stop == 5 + 4 * layer
            xT_ready, xs_ready = next_ln(lambda b: add_block(b, 1.0, made, (xs_ready,)), g_mark)
            if stopping:
                return finish(xs_ready)
            g_mark = load_gains(base + 2)
            made = ffn(xT_ready)
            xT_read[0] = (made[-1],)
            stopping = stop == 6 + 4 * layer
            xT_ready, xs_ready = next_ln(lambda b: add_block(b, 0.5, made, (xs_ready,)), g_mark)
            if stopping:
                return finish(xs_ready)
            g_mark = load_gains(base + 3)
            add = ple(layer, xT_ready, xs_ready)
            stopping = stop == 7 + 4 * layer
            xT_ready, xs_ready = next_ln(add, g_mark, turned=layer == 0)
            if stopping:
                return finish(xs_ready)
        finish(xs_ready)


def rows_of(w):
    return w.reshape(w.shape[0] // P, P, w.shape[1]).transpose(1, 0, 2)


def chunk(*parts):
    return np.concatenate([rows_of(w) for w in parts], 2).reshape(1, P, -1)


def ffn_chunks(w_gu, w_down):
    f = w_down.shape[0]
    pad = FF_TILES * P - f
    wide = lambda w: np.concatenate([w, np.zeros((D, pad), np.float32)], 1)
    gate = rows_of(wide(w_gu[:, :f])).reshape(P, KD, FF_TILES, 1, P)
    up = rows_of(wide(w_gu[:, f:])).reshape(P, KD, FF_TILES, 1, P)
    gu = np.concatenate([gate, up], 3).transpose(2, 0, 1, 3, 4).reshape(FF_TILES, P, GU)
    down = np.concatenate([w_down, np.zeros((pad, D), np.float32)], 0).reshape(FF_TILES, P, D)
    return np.concatenate([gu, down], 2)


def k_chunks(w, per=3):
    r = rows_of(w)
    n = r.shape[1] // per
    whole = r[:, :n * per].reshape(P, n, per * D).transpose(1, 0, 2)
    rest = r[:, n * per:].reshape(1, P, -1)
    return whole, rest


def layouts(a):
    t = {"const": const_table(), "x": a["x"][0]}
    t["ffn_a"] = ffn_chunks(a["ffn1_w_gu"][0], a["ffn1_w_down"][0])
    t["ffn_b"] = ffn_chunks(a["ffn2_w_gu"][0], a["ffn2_w_down"][0])
    for i, n in ((0, "c"), (1, "e")):
        t["ffn_" + n] = ffn_chunks(a["ffn1_w_in_2"][i], a["ffn1_w_out_2"][i])
    for i, n in ((0, "d"), (1, "f")):
        t["ffn_" + n] = ffn_chunks(a["ffn2_w_in_2"][i], a["ffn2_w_out_2"][i])
    w = a["w_in"][0]
    kv = GROUPS * HD
    sizes = (HEADS * HD, kv, kv, kv, kv, kv, kv, GATES, HG * P, HG * P, HG * P, HG * P)
    ends = np.cumsum(sizes)
    nq, kc, vc, ks, vs, kw, vw, gl, hq, hf, hi, hg = (w[:, e - s:e] for e, s in zip(ends, sizes))
    two = lambda m, g: np.concatenate([m[:, g * HD:(g + 1) * HD]] * 2, 1)
    tile = lambda m, j: m[:, j * P:(j + 1) * P]
    t["nsa_cmp_in"] = np.concatenate([chunk(two(kc, 0), two(kc, 1), two(vc, 0)),
                                      chunk(two(vc, 1), two(ks, 0), two(ks, 1))])
    t["nsa_qk"] = np.concatenate([chunk(two(kw, 0), two(kw, 1), tile(nq, 0)),
                                  chunk(tile(nq, 1), tile(nq, 2), tile(nq, 3))])
    t["nsa_v"] = chunk(vs, vw, gl)
    t["hg_v"] = np.concatenate([chunk(hi[:, :SEQ]), chunk(hi[:, SEQ:])])
    t["hg"] = np.concatenate([chunk(tile(hq, h), tile(hf, h), tile(hg, h)) for h in range(HG)])
    w1 = [rows_of(a[n][0]).reshape(P, 2, LP // 2 * CMP_HID).transpose(1, 0, 2) for n in ("cmp_k_w1", "cmp_v_w1")]
    t["cmp_w1"] = np.concatenate(w1)
    k2, v2 = rows_of(a["cmp_k_w2"][0]), rows_of(a["cmp_v_w2"][0])
    t["cmp_w2"] = np.stack([np.concatenate([m, m], 2) for m in (k2, v2)], 1)
    t["cmp_pos"] = np.stack([a[n][0].reshape(LP, P).T for n in ("cmp_pos_k", "cmp_pos_v")], 1)
    t["w_out1"], t["w_out2"] = k_chunks(a["w_out"][0])
    small = np.zeros((P, HG + 2), np.float32)
    small[:, 0:HG] = a["hgrn_lower_bound"][0].reshape(HG, P).T
    small[:, HG] = a["hgrn_out_norm"][0]
    small[:FOX_H, HG + 1] = a["fox_b_f_2"][0]
    t["small"] = small

    gains = np.zeros((16, 2 * D), np.float32)
    for i, g in enumerate((a["ffn1_norm"][0], a["mix_norm"][0], a["ffn2_norm"][0], a["final_norm"])):
        gains[i, :D] = g
    for i in range(2):
        for j in range(4):
            gains[4 + 4 * i + j, :D] = a["ln_g_2"][i, j]
            gains[4 + 4 * i + j, D:] = a["ln_b_2"][i, j]
        gains[14 + i, :D] = a["ple_b_gate_2"][i]
    gains[12, :KL] = a["kv_norm_2"]
    gains[13, :QL] = a["mla_q_norm_2"][0]
    t["gains"] = gains

    w = a["fox_w_in_2"][0]
    fq, fk, fv, ff = w[:, :D], w[:, D:2 * D], w[:, 2 * D:3 * D], w[:, 3 * D:]
    t["fox_v"] = np.concatenate([chunk(fv[:, i * SEQ:(i + 1) * SEQ]) for i in range(4)])
    t["fox_f"] = chunk(np.concatenate([ff, np.zeros((D, P - FOX_H), np.float32)], 1))
    t["fox_qk"] = np.concatenate([chunk(tile(fq, j), tile(fk, j)) for j in range(KD)])
    t["fox_o1"], t["fox_o2"] = k_chunks(a["fox_w_o_2"][0])
    for i in range(2):
        t[f"ple{i}_p"] = chunk(a["ple_w_proj_2"][i])
        t[f"ple{i}_g1"], t[f"ple{i}_g2"] = k_chunks(a["ple_w_gate_2"][i])
    t["pT"] = a["p_2"][:, 0].transpose(0, 2, 1).reshape(2, 2, P, SEQ).transpose(0, 2, 1, 3)
    down = a["kv_w_down_2"]
    half = ROPE // 2
    rope = down[:, KL:]
    swap = lambda m: np.concatenate([m[..., half:], m[..., :half]], -1)
    t["kv_down1"] = chunk(down[:, :KL])
    t["kv_down2"] = chunk(rope, rope, swap(rope), swap(rope))
    t["mla_dq"] = chunk(a["mla_w_dq_2"][0])
    uq, up = a["mla_w_uq_2"][0], a["kv_w_up_2"]
    pairs = []
    for p in range(MLA_H // 2):
        h0, h1 = 2 * p, 2 * p + 1
        pairs.append(np.concatenate([
            chunk(uq[:, h0, :P], uq[:, h1, :P], uq[:, h0, P:], uq[:, h1, P:], swap(uq[:, h0, P:]), swap(uq[:, h1, P:])),
            chunk(up[:, h0, :P], up[:, h1, :P]), chunk(up[:, h0, P:], up[:, h1, P:])], 2))
    t["mla_up"] = np.concatenate(pairs)
    t["mla_o1"], t["mla_o2"] = k_chunks(a["mla_w_o_2"][0])
    return {n: np.ascontiguousarray(v) for n, v in t.items()}


def kernel(**inputs):
    import concourse.bacc as bacc
    from concourse.bass_utils import run_bass_kernel_spmd

    nc = bacc.Bacc("TRN2", target_bir_lowering=False, num_devices=1)
    arrays, t = {}, {}
    for name, v in layouts({n: np.asarray(v) for n, v in inputs.items()}).items():
        arrays["in_" + name] = v
        t[name] = nc.dram_tensor("in_" + name, v.shape, F32, kind="ExternalInput").ap()
    t["cum_scratch"] = nc.dram_tensor("cum_scratch", (FOX_H, SEQ), F32, kind="Internal").ap()
    out = nc.dram_tensor("out", (SEQ, D), F32, kind="ExternalOutput").ap()
    build(nc, t, out)
    r = run_bass_kernel_spmd(nc, [arrays], core_ids=[0])
    return r.results[0]["out"].reshape(1, SEQ, D)
```

```python
from contextlib import ExitStack

import numpy as np

import concourse.bass as bass
from concourse import mybir

F32 = mybir.dt.float32
F32R = mybir.dt.float32r
ALU = mybir.AluOpType
ACTF = mybir.ActivationFunctionType
AX_X = mybir.AxisListType.X

P = 128
SEQ = 256
TB = SEQ // P
D = 1024
KD = D // P
RMS_EPS = 1e-6
LN_EPS = 1e-5
ALPHA = (2 * 2) ** 0.25
MASKED = -1e30

FF_TILES = 22
GU = KD * 2 * P
FF_COLS = GU + D

HEADS = 8
GROUPS = 2
HD = 64
CMP_LEN = 32
STRIDE = 16
NB = SEQ // STRIDE - 1
CMP_HID = 256
LP = CMP_LEN // 2
GATES = HEADS * 3
VSW = 2 * GROUPS * HD + GATES

HG = 4
CH = 16
CPB = P // CH
F_FLOOR = 1e-30
LN_SPLIT = 2.0 ** 50
LN_RANGE = 2.0 ** -50

FOX_H = 16
MLA_H = 16
QL = 384
KL = 256
ROPE = 64

CHUNK = 3072
RAW_SLOTS = 4

CONST_COLS = {}
_at = 0
for _name, _n in (("ident", P), ("causal", 3 * P), ("dist", 3 * P), ("cmp_dist", TB * NB),
                  ("cmp_row", TB), ("chunk_pair", P), ("chunk_row", CPB), ("restart", SEQ),
                  ("mean", P), ("cos", SEQ), ("sin", SEQ)):
    CONST_COLS[_name] = (_at, _n)
    _at += _n
N_CONST = _at + _at % 2


def const_table():
    t = np.zeros((P, N_CONST), np.float32)

    def put(name, value):
        a, n = CONST_COLS[name]
        t[:value.shape[0], a:a + n] = value.reshape(value.shape[0], n)

    put("ident", np.eye(P, dtype=np.float32))
    row = np.arange(P)[:, None]
    col = np.arange(P)[None, :]
    diag = np.where(col <= row, 0.0, MASKED).astype(np.float32)
    put("causal", np.concatenate([diag, np.zeros((P, P), np.float32), diag], 1))
    near = np.where(col <= row, row - col, 1e33).astype(np.float32)
    put("dist", np.concatenate([near, (row + P - col).astype(np.float32), near], 1))
    tok = np.arange(SEQ).reshape(TB, P).T
    end = np.arange(NB) * STRIDE + CMP_LEN - 1
    away = tok[:, :, None] - end[None, None, :]
    put("cmp_dist", np.where(away >= 0, away, 1e33).astype(np.float32))
    put("cmp_row", (tok >= CMP_LEN - 1).astype(np.float32))
    put("chunk_pair", ((row // CH == col // CH) & (row <= col)).astype(np.float32))
    put("chunk_row", (row // CH == np.arange(CPB)[None, :]).astype(np.float32))
    put("restart", np.broadcast_to((np.arange(SEQ) % CH != 0).astype(np.float32), (P, SEQ)))
    put("mean", np.full((P, P), 1.0 / P, np.float32))
    inv = np.float32(10000.0) ** (-np.arange(ROPE // 2, dtype=np.float32) * np.float32(2.0 / ROPE))
    ang = (np.arange(SEQ, dtype=np.float32)[:, None] * inv[None, :]).astype(np.float32)
    cos, sin = np.cos(ang).T.astype(np.float32), np.sin(ang).T.astype(np.float32)
    put("cos", np.concatenate([cos, cos, cos, cos], 0))
    put("sin", np.concatenate([-sin, sin, -sin, sin], 0))
    return t


class Engine:

    def __init__(self, queue, semaphore):
        self.queue, self.semaphore = queue, semaphore
        self.count = 0
        self.waited = {}

    def after(self, *marks):
        for who, value in marks:
            if self.waited.get(id(who), 0) < value:
                self.queue.wait_ge(who.semaphore, value)
                self.waited[id(who)] = value
        return self.queue

    def done(self, instruction, by=1):
        instruction.then_inc(self.semaphore, by)
        self.count += by
        return (self, self.count)


class WeightStream:

    def __init__(self, sp, act, dve, raw, hi, lo, slot_loads):
        self.sp, self.act, self.dve = sp, act, dve
        self.raw, self.hi, self.lo = raw, hi, lo
        self.slot_loads = slot_loads
        self.chunks = []
        self.loaded = {}
        self.split_at = {}
        self.released = {}
        self.at = 0
        self.seq = []

    def add(self, source, cols, split=True):
        self.chunks.append((source, cols, split))
        if split:
            self.seq.append(len(self.chunks) - 1)

    def load(self, i, *free):
        if i >= len(self.chunks):
            return
        source, cols, _ = self.chunks[i]
        if source is None:
            self.loaded[i] = free
            return
        slot = i % RAW_SLOTS
        loads = self.slot_loads[slot]
        queue = self.sp.after(*free)
        self.loaded[i] = loads.done(queue.dma_start(self.raw[slot][:, 0:cols], source), 16)

    def pair(self, i):
        return self.seq.index(i) % 2

    def split(self, i, a, b, *free, last=False, by=None):
        by = by or self.dve
        if i >= len(self.chunks):
            return
        raw = self.raw[i % RAW_SLOTS][:, a:b]
        hi, lo = self.hi[self.pair(i)][:, a:b], self.lo[self.pair(i)][:, a:b]
        h = self.act.done(self.act.after(self.loaded[i], *free).activation(hi, raw, ACTF.Copy))
        l = by.done(by.after(self.loaded[i], h, *free).tensor_tensor(
            lo, raw, hi.bitcast(F32), ALU.subtract))
        self.split_at.setdefault(i, []).append((a, b, h, l))
        if last:
            self.load(i + RAW_SLOTS, *(m for piece in self.split_at[i] for m in piece[2:]))

    def split_head(self, i, upto, *free):
        if i < len(self.chunks) and self.chunks[i][2]:
            cols = self.chunks[i][1]
            upto = min(cols, upto)
            self.split(i, 0, upto // 4 * 2, *free)
            self.split(i, upto // 4 * 2, upto, *free, last=(upto == cols))

    def split_whole(self, i):
        if i >= len(self.chunks) or not self.chunks[i][2] or self.chunks[i][0] is None:
            return
        cols = self.chunks[i][1]
        at = self.split_at[i][-1][1] if i in self.split_at else 0
        if at == cols:
            return
        k = self.seq.index(i)
        free = self.released.get(self.seq[k - 2], ()) if k >= 2 else ()
        if at == 0:
            self.split(i, 0, cols // 4 * 2, *free)
            at = cols // 4 * 2
        self.split(i, at, cols, *free, last=True)

    def split_part(self, i, part, parts):
        if i >= len(self.chunks) or not self.chunks[i][2] or self.chunks[i][0] is None:
            return
        cols = self.chunks[i][1]
        at = self.split_at[i][-1][1] if i in self.split_at else 0
        a, b = max(at, cols * part // parts), cols * (part + 1) // parts
        if a < b:
            self.split(i, a, b, *self.released.get(self.seq[self.seq.index(i) - 2], ()), last=b == cols)

    def split_behind(self, upto, parts, by):
        i = self.at
        if i >= len(self.chunks) or not self.chunks[i][2] or i in self.split_at:
            return
        cols = self.chunks[i][1]
        upto = min(upto, cols)
        free = self.released.get(self.seq[self.seq.index(i) - 2], ())
        for part in range(parts):
            a, b = upto * part // parts, upto * (part + 1) // parts
            self.split(i, a, b, *free, last=b == cols, by=by)

    def split_parts(self, i, counts, at):
        for part in range(sum(counts[:at]), sum(counts[:at + 1])):
            self.split_part(i, part, sum(counts))

    def take(self, ahead=True):
        i = self.at
        self.at += 1
        if not self.chunks[i][2]:
            self.split_whole(i + 1)
            return i, self.raw[i % RAW_SLOTS], None, (self.loaded[i],)
        self.split_whole(i)
        if ahead:
            self.split_whole(i + 1)
        return i, self.hi[self.pair(i)], self.lo[self.pair(i)], tuple(m for s in self.split_at[i] for m in s[2:])

    def reserve(self, ahead):
        i = self.at + ahead
        return i, self.raw[i % RAW_SLOTS], self.loaded[i]

    def give_back(self, i, *marks):
        self.load(i + RAW_SLOTS, *marks)

    def release(self, i, mark):
        self.released[i] = (mark,)
        if not self.chunks[i][2]:
            self.load(i + RAW_SLOTS, mark)


def build(nc, t, out):
    with ExitStack() as ctx:
        def sb(name, shape, dt=F32):
            return ctx.enter_context(nc.sbuf_tensor(name, shape, dt))

        def counter(queue, name):
            return Engine(queue, ctx.enter_context(nc.semaphore(name)))

        pe = counter(nc.tensor, "pe_done")
        act = counter(nc.scalar, "act_done")
        dve = counter(nc.vector, "dve_done")
        pool = counter(nc.gpsimd, "pool_done")
        sp = counter(nc.sync, "sp_done")
        slot_loads = [counter(None, f"weights_landed_{i}") for i in range(RAW_SLOTS)]
        small_landed = counter(None, "small_landed")
        gains_landed = counter(None, "gains_landed")
        out_landed = counter(None, "out_landed")

        raw = [sb(f"w_raw{i}", [P, CHUNK]) for i in range(RAW_SLOTS)]
        w_hi = [sb(f"w_hi{i}", [P, CHUNK], F32R) for i in range(2)]
        w_lo = [sb(f"w_lo{i}", [P, CHUNK], F32R) for i in range(2)]
        x = sb("x", [P, TB, D])
        xn = sb("xn", [P, TB, D])
        xT_hi = sb("xT_hi", [P, KD, SEQ], F32R)
        xT_lo = sb("xT_lo", [P, KD, SEQ], F32R)
        gains = sb("gains", [P, 2 * D + CH])
        const = sb("const", [P, N_CONST])
        sig = [sb(f"ff_silu{i}", [P, SEQ]) for i in range(2)]
        hT_hi = [sb(f"hT_hi{i}", [P, SEQ], F32R) for i in range(2)]
        hT_lo = [sb(f"hT_lo{i}", [P, SEQ], F32R) for i in range(2)]
        row_sums = sb("row_sums", [P, TB, 2])
        square_sums = sb("square_sums", [P, TB, 2])
        minus_mean = sb("minus_mean", [P, TB])
        rstd = sb("rstd", [P, TB])
        expo = sb("minus_half", [P, 1])
        small = sb("small", [P, 64])
        psum = [ctx.enter_context(nc.psum_tensor(f"bank{i}", [P, 512], F32)) for i in range(8)]
        psum_read = [() for _ in range(8)]

        def cst(name, rows=P):
            a, n = CONST_COLS[name]
            return const[0:rows, a:a + n]

        ident = cst("ident")
        x_landed = [counter(None, f"x_landed_{b}") for b in range(TB)]
        x_mark = [x_landed[b].done(sp.after().dma_start(x[:, b, :], t["x"][b * P:(b + 1) * P, :]), 16) for b in range(TB)]
        g_first = gains_landed.done(sp.after().dma_start(gains[:, 0:D], t["gains"][0:1, 0:D].to_broadcast([P, D])), 16)
        minus_half = pool.done(pool.after().memset(expo[:, :], -0.5))

        ws = WeightStream(sp, act, dve, raw, w_hi, w_lo, slot_loads)

        def add_all(name, split=True):
            if name is None:
                ws.add(None, 0, split)
                return
            n, _, cols = t[name].shape
            for i in range(n):
                ws.add(t[name][i, :, :], cols, split)

        for name, split in (("ffn_a", True), ("nsa_a", True), ("nsa_b", True), ("hg_fq", True),
                            ("hg_g", True), ("nsa_v", True), ("cmp_w1", False), ("nsa_c", True),
                            ("hg_v", True), (None, False), (None, False), (None, False), ("w_out1", True),
                            ("w_out2", True), ("ffn_b", True),
                            ("ffn_c", True), ("fox_f", True), ("fox_v", True), ("fox_qk", True),
                            ("fox_o1", True), ("fox_o2", True), ("ffn_d", True), ("ple0_p", True),
                            ("ple0_g1", True), ("ple0_g2", True),
                            ("ffn_e", True), ("kv_down1", True), ("kv_down2", True), ("mla_dq", True),
                            ("mla_up", True), ("mla_o1", True), ("mla_o2", True), ("ffn_f", True), ("ple1_p", True),
                            ("ple1_g1", True), ("ple1_g2", True)):
            add_all(name, split)
        ident_landed, const_landed = counter(None, "ident_landed"), counter(None, "const_landed")
        ident_mark = ident_landed.done(sp.after().dma_start(const[:, 0:P], t["const"][:, 0:P]), 16)
        for i in range(RAW_SLOTS):
            ws.load(i)
        c_mark = const_landed.done(sp.after().dma_start(const[:, P:N_CONST], t["const"][:, P:N_CONST]), 16)
        s_mark = small_landed.done(sp.after().dma_start(small[:, 0:HG + 2], t["small"]), 16)

        everyone = (pe, act, dve, pool)

        def meet():
            marks = [(e, e.count) for e in everyone if e.count]
            for e in everyone:
                e.after(*(m for m in marks if m[0] is not e))

        def bank_for(i):
            pe.after(*psum_read[i])
            psum_read[i] = ()
            return psum[i]

        def read_by(i, *marks):
            psum_read[i] = psum_read[i] + marks

        def taking_turns(banks):
            order = list(banks)

            def next_bank():
                order.append(order.pop(0))
                return order[-1], bank_for(order[-1])
            return next_bank

        def feature_major(o, hi, lo, cols, k_tiles, a_hi, a_lo, ready, ks=None):
            last = 3 * k_tiles - 1
            ks = range(k_tiles) if ks is None else ks
            n = 3 * ks[0]
            for k in ks:
                c = slice(cols(k), cols(k) + P)
                pe.after(*ready[k])
                for w, a in ((hi, a_hi), (hi, a_lo), (lo, a_hi)):
                    ins = nc.tensor.matmul(o, w[:, c], a[:, k, :], start=(n == 0), stop=(n == last))
                    n += 1
            return ins

        def token_major(o, hi, lo, cols, width, ks, a_hi, a_lo, b, first, final, ready):
            total = 3 * len(ks)
            n = 0
            for j, k in enumerate(ks):
                c = slice(cols(j), cols(j) + width)
                tok = slice(b * P, (b + 1) * P)
                pe.after(*ready[k])
                for a, w in ((a_hi, hi), (a_lo, hi), (a_hi, lo)):
                    ins = nc.tensor.matmul(o, a(k)[:, tok], w[:, c], start=(first and n == 0),
                                           stop=(final and n == total - 1))
                    n += 1
            return ins

        ACC = (0, 1, 2, 3)
        SPARE = (4, 5, 6, 7)

        def load_gains(row):
            src = t["gains"][row:row + 1, :].to_broadcast([P, 2 * D])
            return gains_landed.done(sp.after(*gains_read[0]).dma_start(gains[:, 0:2 * D], src), 16)

        gains_read = [()]

        def mean_of(dst, parts, plus, ready):
            first, second = parts
            m = dve.done(dve.after(*ready).tensor_scalar(dst, first, 1.0 / D, plus, ALU.mult, ALU.add))
            return dve.done(dve.after(m).scalar_tensor_tensor(dst, second, 1.0 / D, dst, ALU.mult, ALU.add))

        def squares(src, b, ready, bias=0.0):
            act.after(*ready, *xn_read[0])
            for half in range(2):
                c = slice(512 * half, 512 * (half + 1))
                m = act.done(nc.scalar.activation(xn[:, b, c], src[:, c], ACTF.Square, bias=bias,
                                                  accum_out=square_sums[:, b, half:half + 1]))
            return m

        def root(b, ready):
            return pool.done(pool.after(ready, minus_half).tensor_tensor(
                rstd[:, b:b + 1], rstd[:, b:b + 1], expo[:, 0:1], ALU.pow))

        def halves_of(sums, b):
            return sums[:, b, 0:1], sums[:, b, 1:2]

        def rms_root(src, b, ready):
            m = squares(src, b, ready)
            return lambda: root(b, mean_of(rstd[:, b:b + 1], halves_of(square_sums, b), RMS_EPS, (m,)))

        def ln_root(b, ready):
            m = dve.done(dve.after(*ready).tensor_scalar(minus_mean[:, b:b + 1], row_sums[:, b, 0:1], -1.0 / D, None,
                                                         ALU.mult))
            mean = dve.done(dve.after(m).scalar_tensor_tensor(
                minus_mean[:, b:b + 1], row_sums[:, b, 1:2], -1.0 / D, minus_mean[:, b:b + 1], ALU.mult, ALU.add))
            m = squares(x[:, b, :], b, (mean,), bias=minus_mean[:, b:b + 1])
            return mean, lambda: root(b, mean_of(rstd[:, b:b + 1], halves_of(square_sums, b), LN_EPS, (m,)))

        def rms_apply(src, dst, b, c, ready):
            return dve.done(dve.after(*ready).scalar_tensor_tensor(
                dst[:, c], src[:, c], rstd[:, b:b + 1], gains[:, c], ALU.mult, ALU.mult))

        def rms_rows(src, dst, gain, stat, b, ready):
            width = src.shape[-1]
            ssq, rs = stat[:, b, 0:1], stat[:, b, 1:2]
            m = act.done(act.after(*ready).activation(dst, src, ACTF.Square, accum_out=ssq))
            m = dve.done(dve.after(m).tensor_scalar(rs, ssq, 1.0 / width, RMS_EPS, ALU.mult, ALU.add))
            m = pool.done(pool.after(m, minus_half).tensor_tensor(rs, rs, expo[:, 0:1], ALU.pow))
            return dve.done(dve.after(m, *ready).scalar_tensor_tensor(dst, src, rs, gain, ALU.mult, ALU.mult))

        def ln_apply(b, c, ready):
            xb = x[:, b, c]
            rstd_ready, *others = ready
            m = dve.done(dve.after(*others).scalar_tensor_tensor(
                xb, xb, minus_mean[:, b:b + 1], gains[:, c], ALU.add, ALU.mult))
            return dve.done(dve.after(m, rstd_ready).scalar_tensor_tensor(
                xb, xb, rstd[:, b:b + 1], gains[:, D + c.start:D + c.stop], ALU.mult, ALU.add))

        def turn(pieces, kts, dst_hi, dst_lo, free):
            marks = {k: () for k in range(kts)}
            later = None
            for b, k0, src, make in pieces:
                made = make()
                n = min(4, kts - k0)
                bank = SPARE[2 * b + k0 // 4]
                o = bank_for(bank)
                pe.after(made)
                for i in range(n):
                    ins = nc.tensor.transpose(o[:, i * P:(i + 1) * P], src[:, (k0 + i) * P:(k0 + i + 1) * P], ident)
                turned = pe.done(ins)
                hi, lo = (z[:, k0:k0 + n, b * P:(b + 1) * P] for z in (dst_hi, dst_lo))
                got = o[:, 0:n * P].rearrange("p (k t) -> p k t", t=P)
                h = act.done(act.after(turned, *free).activation(hi, got, ACTF.Copy))
                if later:
                    later()

                def later(h=h, turned=turned, hi=hi, lo=lo, got=got, bank=bank, ks=range(k0, k0 + n)):
                    l = dve.done(dve.after(turned, h).tensor_tensor(lo, got, hi.bitcast(F32), ALU.subtract))
                    read_by(bank, h, l)
                    for k in ks:
                        marks[k] += (h, l)
            later()
            return marks

        def split_to(hi, lo, src, ready, free=()):
            h = act.done(act.after(*ready, *free).activation(hi, src, ACTF.Copy))
            l = dve.done(dve.after(h, *ready, *free).tensor_tensor(lo, src, hi.bitcast(F32), ALU.subtract))
            return h, l

        def ffn(xT_ready):
            first = ws.at
            n = FF_TILES
            ws.at += n
            h_ready = {}
            h_read = {}
            down = {}

            def gate_up(i):
                c = first + i
                w = ws.pair(c)
                bank = SPARE[i % 4]
                o = bank_for(bank)
                pe.after(*(m for s in ws.split_at[c] if s[0] < GU for m in s[2:]))
                if i == 0:
                    up = bank_for(ACC[3])
                    for ks in (range(KD // 2), range(KD // 2, KD)):
                        for dst, at in ((o, 0), (up, P)):
                            ins = feature_major(dst[:, at // P * SEQ:(at // P + 1) * SEQ], w_hi[w], w_lo[w],
                                                lambda k: 2 * P * k + at, KD, xT_hi, xT_lo, xT_ready, ks)
                    return pe.done(ins)
                feature_major(o[:, 0:SEQ], w_hi[w], w_lo[w], lambda k: 2 * P * k, KD, xT_hi, xT_lo, xT_ready)
                return pe.done(feature_major(o[:, SEQ:2 * SEQ], w_hi[w], w_lo[w],
                                             lambda k: 2 * P * k + P, KD, xT_hi, xT_lo, xT_ready))

            def activate(i, made):
                bank = SPARE[i % 4]
                up_bank = ACC[3] if i == 0 else bank
                o, up = psum[bank], psum[up_bank]
                s = i % 2
                free = (h_read[i - 2],) if i >= 2 else ()
                a = act.done(act.after(made, *free).activation(sig[s][:, :], o[:, 0:SEQ], ACTF.Silu))
                m = dve.done(dve.after(a).tensor_tensor(sig[s][:, :], sig[s][:, :], up[:, SEQ:2 * SEQ], ALU.mult))
                read_by(bank, a, m)
                read_by(up_bank, m)
                h, l = split_to(hT_hi[s][:, :], hT_lo[s][:, :], sig[s][:, :], (m,), free)
                h_ready[i] = (h, l)

            def down_product(tiles):
                if tiles[0] == 0:
                    for a in ACC:
                        bank_for(a)
                marks = []
                for b in range(TB):
                    marks.append([])
                    for half in range(2):
                        for i in tiles:
                            c = first + i
                            w = ws.pair(c)
                            s = i % 2
                            pe.after(*(m for q in ws.split_at[c] if q[1] > GU for m in q[2:]))
                            ins = token_major(psum[ACC[2 * b + half]][:, :], w_hi[w], w_lo[w],
                                              lambda j: GU + 512 * half, 512, (0,),
                                              lambda k: hT_hi[s], lambda k: hT_lo[s], b, i == 0, i == n - 1,
                                              (h_ready[i],))
                        marks[b].append(pe.done(ins))
                last = marks[-1][-1]
                for i in tiles:
                    h_read[i] = down[i] = last
                    ws.released[first + i] = (last,)
                return marks

            made = {}
            ws.split_whole(first)
            for i in range(n):
                c = first + i
                made[i] = gate_up(i)
                if i + 1 < n:
                    free = (made[i - 1],) if i >= 1 else ws.released.get(c - 1, ())
                    ws.split(c + 1, 0, GU // 2, *free)
                    ws.split(c + 1, GU // 2, GU, *free)
                else:
                    ws.split_head(first + n, GU, made[i - 1])
                activate(i, made[i])
                if 1 <= i < n - 1:
                    down_product((i - 1,))
                if i + 1 < n:
                    free = (down[i - 1],) if i >= 1 else ws.released.get(c - 1, ())
                    ws.split(c + 1, GU, FF_COLS, *free, last=True)
            marks = down_product((n - 2, n - 1))
            return marks

        def out_product(a_hi, a_lo, ready, n_chunks, k_tiles, per=3, then_norm=True):
            for a in ACC:
                bank_for(a)
            for c in range(n_chunks):
                last = then_norm and c == n_chunks - 1
                i, hi, lo, there = ws.take(ahead=not last)
                if last:
                    ws.split_behind(GU, 4, pool)
                ks = list(range(c * per, min(c * per + per, k_tiles)))
                pe.after(*there)
                marks = []
                for b in range(TB):
                    marks.append([])
                    for half in range(2):
                        marks[b].append(pe.done(token_major(
                            psum[ACC[2 * b + half]][:, :], hi, lo, lambda j: D * j + 512 * half, 512, ks, a_hi, a_lo,
                            b, c == 0, ks[-1] == k_tiles - 1, ready)))
                ws.release(i, marks[-1][-1])
            return marks

        def bcast(ap, axis, shape):
            return ap.unsqueeze(axis).to_broadcast(shape)

        def feature_tiles(n, banks, ready, sinks, a_hi=None, a_lo=None, k_tiles=KD, halves=False):
            i, hi, lo, there = ws.take()
            if halves:
                held = [bank_for(banks[j]) for j in range(n)]
                for ks in (range(KD // 2), range(KD // 2, KD)):
                    pe.after(*(m for piece in ws.split_at[i] if piece[0] < n * P * (ks[-1] + 1) for m in piece[2:]))
                    for j in range(n):
                        m = pe.done(feature_major(held[j][:, 0:SEQ], hi, lo, lambda k: (n * k + j) * P, KD,
                                                  xT_hi, xT_lo, ready, ks))
                        if ks[0]:
                            read_by(banks[j], *sinks[j](held[j][:, 0:SEQ], m))
                ws.release(i, m)
                return
            pe.after(*there)
            for j in range(n):
                bank = banks[j % len(banks)]
                o = bank_for(bank)
                m = pe.done(feature_major(o[:, 0:SEQ], hi, lo, lambda k: (n * k + j) * P, k_tiles,
                                          a_hi or xT_hi, a_lo or xT_lo, ready))
                read_by(bank, *sinks[j](o[:, 0:SEQ], m))
            ws.release(i, m)

        def token_tiles(width, banks, ready, sink, a_hi=None, a_lo=None, k_tiles=KD):
            i, hi, lo, there = ws.take()
            pe.after(*there)
            for b in range(TB):
                bank = banks[b % len(banks)]
                o = bank_for(bank)
                m = pe.done(token_major(o[:, 0:width], hi, lo, lambda k: width * k, width, range(k_tiles),
                                        lambda k: (a_hi or xT_hi)[:, k, :], lambda k: (a_lo or xT_lo)[:, k, :],
                                        b, True, True, ready))
                read_by(bank, *sink(b, o[:, 0:width], m))
            ws.release(i, m)

        def keep(dst, scale=1.0):
            def sink(o, m):
                c = act.done(act.after(m).activation(dst, o, ACTF.Copy, scale=scale))
                kept.append(c)
                return (c,)
            return sink

        kept = []

        def mixer(xT_ready):
            with ExitStack() as scope:
                def tile(name, shape, dt=F32, on=scope):
                    return on.enter_context(nc.sbuf_tensor("mix_" + name, shape, dt))

                oT_hi, oT_lo = tile("oT_hi", [P, KD, SEQ], F32R), tile("oT_lo", [P, KD, SEQ], F32R)
                q = tile("q", [P, HEADS // GROUPS, SEQ])
                keys = tile("keys", [P, 2, SEQ])
                vals = tile("vals", [P, TB, VSW])
                k_cmp = tile("k_cmp", [P, GROUPS * NB])
                v_cmp = tile("v_cmp", [P, GROUPS, HD])
                gates = tile("gates", [P, TB, GATES])
                hq, hk = (xn[:, i, :].rearrange("p (h s) -> p h s", h=HG) for i in range(2))
                b_sum, k_end, exp_b = (tile(n, [P, HG, SEQ]) for n in ("b", "k_end", "exp_b"))
                hv, hg = tile("hg_v", [P, TB, HG * P]), tile("hg_gate", [P, TB, HG * P])
                out_gain = tile("out_gain", [P, P])
                lbt = tile("lower_bound", [P, 4 * HG])
                ssq = [tile(f"squares{i}", [P, 1]) for i in range(2)]
                q_step = gains[:, 0:2 * D].rearrange("p (j t) -> p j t", j=CH)
                zeroed_step = pool.done(pool.after(*gains_read[0]).memset(q_step[:, :, :], 0.0))
                gain_landed = small_landed.done(sp.after().dma_start(
                    out_gain[:, :], t["gains"][0:1, D:D + P].to_broadcast([P, P])), 16)

                with ExitStack() as cmp_scope:
                    pairs = tile("pairs", [P, 2 * GROUPS, SEQ], on=cmp_scope)
                    blocks = tile("blocks", [P, 2, LP, GROUPS * NB], on=cmp_scope)
                    pos = tile("pos", [P, 2, LP], on=cmp_scope)
                    w2 = tile("w2", [P, 2, 2, P], on=cmp_scope)
                    hidT = tile("hidT", [P, 2, 2, GROUPS * NB], on=cmp_scope)
                    landed = small_landed.done(sp.after().dma_start(pos[:, :, :], t["cmp_pos"]), 16)
                    landed = small_landed.done(sp.after().dma_start(w2[:, :, :, :], t["cmp_w2"]), 16)

                    def pair_sink(kv):
                        def sink(o, m):
                            act.after(m)
                            for g in range(GROUPS):
                                i, rows = 2 * kv + g, slice(64 * g, 64 * g + 64)
                                nc.scalar.activation(pairs[0:64, i, :], o[rows, :], ACTF.Copy)
                                nc.scalar.activation(pairs[64:P, i, 0:SEQ - 1], o[rows, 1:SEQ], ACTF.Copy)
                                z = act.done(nc.scalar.activation(pairs[64:P, i, SEQ - 1:SEQ], o[rows, SEQ - 1:SEQ], ACTF.Copy))
                            kept.append(z)
                            return (z,)
                        return sink

                    feature_tiles(3, ACC, xT_ready, [pair_sink(0), pair_sink(1), keep(keys[:, 0, :])], halves=True)
                    pairs_ready = kept[1]
                    for kv in range(2):
                        for g in range(GROUPS):
                            row = pairs[:, 2 * kv + g, :]
                            for part in range(2):
                                lp = slice(part * LP // 2, (part + 1) * LP // 2)
                                cells = row[:, STRIDE * part:STRIDE * (part + NB)].rearrange(
                                    "p (b l two) -> p l b two", l=LP // 2, two=2)[:, :, :, 0]
                                blocks_ready = dve.done(dve.after(landed, pairs_ready).tensor_tensor(
                                    blocks[:, kv, lp, g * NB:(g + 1) * NB], cells,
                                    bcast(pos[:, kv, lp], 2, [P, LP // 2, NB]), ALU.add))
                    lb = small[:, 0:HG]
                    lb_diff, lb_soft, lb_val, lb_rest = (lbt[:, i * HG:(i + 1) * HG] for i in range(4))
                    m = dve.done(dve.after(s_mark).tensor_tensor(lb_diff, lb, lb, ALU.subtract))
                    m = act.done(act.after(m).activation(lb_soft, lb_diff, ACTF.Exp))
                    m = dve.done(dve.after(m).reciprocal(lb_val, lb_soft))
                    m = dve.done(dve.after(m).tensor_tensor(lb_soft, lb_soft, lb_val, ALU.mult))
                    m = dve.done(dve.after(m).tensor_tensor(lb_val, lb_soft, lb_soft, ALU.subtract))
                    lb_ready = dve.done(dve.after(m).tensor_scalar(lb_rest, lb_val, -1.0, 1.0, ALU.mult, ALU.add))
                    feature_tiles(3, SPARE, xT_ready, [keep(keys[:, 1, :])] + [keep(q[:, j, :], HD ** -0.5) for j in (0, 1)])

                    def query_sink(h):
                        def sink(o, m):
                            a = act.done(act.after(m, *xn_read[0]).activation(hq[:, h, :], o, ACTF.Sigmoid))
                            d = dve.done(dve.after(a).tensor_tensor(hq[:, h, :], hq[:, h, :], o, ALU.mult))
                            q_made.append(d)
                            return (a, d)
                        return sink

                    def forget_sink(h):
                        def sink(o, m):
                            act.after(m, *xn_read[0])
                            nc.scalar.activation(exp_b[:, h, :], o, ACTF.Sigmoid)
                            f_made.append(act.done(nc.scalar.activation(hk[:, h, :], o, ACTF.Sigmoid, scale=-1.0)))
                            return (f_made[-1],)
                        return sink
                    q_made, f_made = [], []
                    for h in range(HG):
                        feature_tiles(2, SPARE, xT_ready, [forget_sink(h), query_sink(h)])
                        dve.after(f_made[h], lb_ready)
                        nc.vector.tensor_scalar(hk[:, h, :], hk[:, h, :], lb_rest[:, h:h + 1], None, ALU.mult)
                        f_ready = dve.done(nc.vector.tensor_scalar(exp_b[:, h, :], exp_b[:, h, :], lb_rest[:, h:h + 1],
                                                                   lb_val[:, h:h + 1], ALU.mult, ALU.add))

                    def gate_sink(half):
                        def sink(b, o, m):
                            dst = hg[:, b, half * SEQ:(half + 1) * SEQ]
                            a = act.done(act.after(m).activation(dst, o, ACTF.Sigmoid))
                            d = dve.done(dve.after(a).tensor_tensor(dst, dst, o, ALU.mult))
                            g_made.append(d)
                            return (a, d)
                        return sink
                    g_made = []
                    for half in range(2):
                        token_tiles(SEQ, SPARE, xT_ready, gate_sink(half))

                    def vals_sink(b, o, m):
                        c = act.done(act.after(m).activation(vals[:, b, :], o, ACTF.Copy))
                        kept.append(c)
                        return (c,)
                    token_tiles(VSW, SPARE, xT_ready, vals_sink)
                    m = act.done(act.after(*kept).activation(gates[:, :, :], vals[:, :, VSW - GATES:VSW], ACTF.Sigmoid))
                    cmp_gates = gates[:, :, :].rearrange("p b (h three) -> p b h three", three=3)[:, :, :, 0]
                    gates_ready = dve.done(dve.after(m).tensor_tensor(
                        cmp_gates, cmp_gates, bcast(cst("cmp_row"), 2, [P, TB, HEADS]), ALU.mult))
                    flat = lambda a: a[:, :, :].rearrange("p h s -> p (h s)")
                    f, f2 = flat(exp_b), flat(k_end)
                    m = dve.done(dve.after(f_ready).tensor_scalar(f, f, F_FLOOR, None, ALU.max))
                    m = dve.done(dve.after(m).tensor_scalar(f2, f, LN_SPLIT, 1.0, ALU.mult, ALU.min))
                    m = dve.done(dve.after(m).tensor_scalar(f, f, LN_RANGE, None, ALU.max))
                    act.after(m)
                    nc.scalar.activation(f, f, ACTF.Ln)
                    logs = act.done(nc.scalar.activation(f2, f2, ACTF.Ln))
                    by_head = hg[:, :, :].rearrange("p b (h v) -> p (b h) v", v=P)
                    g_ready = dve.done(dve.after(*g_made, gain_landed).tensor_tensor(
                        by_head, by_head, bcast(out_gain[:, :], 1, [P, TB * HG, P]), ALU.mult))
                    m = dve.done(dve.after(logs).tensor_tensor(f, f, f2, ALU.add))
                    dve.after(m)
                    for h in range(HG):
                        m = dve.done(nc.vector.tensor_tensor_scan(b_sum[:, h, :], cst("restart"), exp_b[:, h, :], 0.0,
                                                                  ALU.mult, ALU.add))
                    b_ready = m
                    by_chunk = lambda a: a[:, :, :].rearrange("p h (c j) -> p (h c) j", j=CH)
                    m = dve.done(dve.after(m).tensor_tensor(
                        by_chunk(k_end), by_chunk(b_sum)[:, :, CH - 1:CH].to_broadcast([P, HG * TB * CPB, CH]),
                        by_chunk(b_sum), ALU.subtract))
                    act.after(m)
                    nc.scalar.activation(flat(k_end), flat(k_end), ACTF.Exp)
                    expb_ready = m = act.done(nc.scalar.activation(flat(exp_b), flat(b_sum), ACTF.Exp))
                    k_end_ready = dve.done(dve.after(m).tensor_tensor(flat(k_end), flat(k_end), flat(hk), ALU.mult))

                    for kv in range(2):
                        o = bank_for(ACC[kv])
                        for part in range(2):
                            i, w, _, there = ws.take()
                            pe.after(blocks_ready, *there)
                            for j in range(LP // 2):
                                lp = part * LP // 2 + j
                                ins = nc.tensor.matmul(o[0:GROUPS * NB, 0:CMP_HID], blocks[:, kv, lp, :],
                                                       w[:, j * CMP_HID:(j + 1) * CMP_HID],
                                                       start=(lp == 0), stop=(lp == LP - 1))
                            m = pe.done(ins)
                            ws.release(i, m)
                        m = act.done(act.after(m).activation(sig[kv][0:GROUPS * NB, 0:CMP_HID],
                                                             o[0:GROUPS * NB, 0:CMP_HID], ACTF.Gelu_apprx_tanh))
                        read_by(ACC[kv], m)
                    hid_ready = m
                    done = {}
                    units = [(h, b) for h in range(HG) for b in range(TB)]
                    areas = {}

                    def pair(u):
                        return areas[u % 2][1][:, 0:CH * P].rearrange("p (j t) -> p j t", j=CH)

                    def decays(u):
                        h, b = units[u]
                        free = (done["a", u - 2],) if u >= 2 else areas[u][2]
                        bb = b_sum[:, h, b * P:(b + 1) * P].rearrange("p (c j) -> p c j", j=CH)
                        m = dve.done(dve.after(b_ready, *free).tensor_tensor(
                            pair(u).rearrange("p j (c s) -> p j c s", c=CPB),
                            bcast(bb.rearrange("p c j -> p j c"), 3, [P, CH, CPB, CH]),
                            bcast(bb, 1, [P, CH, CPB, CH]), ALU.subtract))
                        flat = pair(u).rearrange("p j s -> p (j s)")
                        m = dve.done(dve.after(m).tensor_scalar(flat, flat, 0.0, None, ALU.min))
                        done["exp", u] = act.done(act.after(m).activation(flat, flat, ACTF.Exp))

                    first_area = areas[0] = ws.reserve(3)
                    decays(0)
                    feature_tiles(2, SPARE, xT_ready, [keep(q[:, j, :], HD ** -0.5) for j in (2, 3)])

                    def hv_sink(half):
                        def sink(b, o, m):
                            c = act.done(act.after(m).activation(hv[:, b, half * SEQ:(half + 1) * SEQ], o, ACTF.Copy))
                            kept.append(c)
                            return (c,)
                        return sink
                    n = GROUPS * NB
                    for half in range(2):
                        token_tiles(SEQ, SPARE, xT_ready, hv_sink(half))
                        if half == 0:
                            o = bank_for(ACC[2])
                            pe.after(hid_ready)
                            for kv in range(2):
                                for j in range(2):
                                    ins = nc.tensor.transpose(o[:, (2 * kv + j) * n:(2 * kv + j + 1) * n],
                                                              sig[kv][0:n, j * P:(j + 1) * P], ident[0:n, 0:n])
                            m = pe.done(ins)
                            hidT_ready = dve.done(dve.after(m).tensor_copy(
                                hidT[:, :, :, :].rearrange("p a b c -> p (a b c)"), o[:, 0:4 * n]))
                            read_by(ACC[2], hidT_ready)
                    o = bank_for(ACC[3])
                    pe.after(hidT_ready)
                    for j in range(2):
                        nc.tensor.matmul(o[:, 0:n], w2[:, 0, j, :], hidT[:, 0, j, :], start=(j == 0), stop=(j == 1))
                    for g in range(GROUPS):
                        for j in range(2):
                            ins = nc.tensor.matmul(o[0:NB, P + g * HD:P + (g + 1) * HD], hidT[:, 1, j, g * NB:(g + 1) * NB],
                                                   w2[:, 1, j, 0:HD], start=(j == 0), stop=(j == 1))
                    m = pe.done(ins)
                    act.after(m)
                    nc.scalar.activation(k_cmp[:, :], o[:, 0:n], ACTF.Copy)
                    cmp_ready = act.done(nc.scalar.activation(
                        v_cmp[0:NB, :, :].rearrange("p g d -> p (g d)"), o[0:NB, P:P + GROUPS * HD], ACTF.Copy))
                    read_by(ACC[3], cmp_ready)
                kept_ready = tuple(kept)
                kept.clear()

                s1 = [tile(f"s1_{i}", [P, 2, SEQ]) for i in range(2)]
                s0 = [tile(f"s0_{i}", [P, 2, P]) for i in range(2)]
                sc = [tile(f"sc_{i}", [P, TB, NB]) for i in range(2)]
                nm = [tile(f"nm_{i}", [P, 6]) for i in range(2)]
                sums = [tile(f"sums_{i}", [P, 6]) for i in range(2)]
                wgt = [tile(f"wgt_{i}", [P, 6]) for i in range(2)]
                o_gated = [tile(f"o_gated{i}", [P, P]) for i in range(2)]
                rms = [tile(f"rms{i}", [P, 1]) for i in range(2)]
                scratch = [first_area] + [ws.reserve(i) for i in (1, 2)]
                ws.at += 3
                area = [slot for _, slot, _ in scratch]
                areas[1] = scratch[1]
                area_free = sum((free for _, _, free in scratch), ())
                ws.split_whole(ws.at)
                pT = [area[i][:, CH * P:CH * P + 1024] for i in range(2)]
                n_state = (CPB + 1) * P
                state = area[2][:, 0:n_state].rearrange("p (c v) -> p c v", v=P)
                q_wide = area[2][:, n_state:n_state + CPB * (P + CH)]
                vm = tile("v_masked", [P, 4, P])
                q_chunk = q_wide[:, 0:CPB * P].rearrange("p (c t) -> p c t", c=CPB)
                zeroed = pool.done(pool.after(*area_free).memset(q_chunk[:, :, :], 0.0))
                step_cells = gains[:, :].rearrange("p (j x) -> p j x", j=CH)[:, :, 0:P].rearrange(
                    "p j (c s) -> p c j s", s=CH)[:, :, :, 0]
                chunk_cells = q_wide[:, :].rearrange("p (c x) -> p c x", c=CPB)[:, :, 0:CH]
                aT = [sig[0][:, i * P:(i + 1) * P] for i in range(2)]
                keT = [sig[1][:, i * P:(i + 1) * P] for i in range(2)]

                KV = (5, 6)
                next_bank = taking_turns((0, 1, 2, 3, 4, 7))

                dist = cst("dist")
                cmp_dist = cst("cmp_dist").rearrange("p (b n) -> p b n", b=TB)
                made, soft, turned, read = {}, {}, {}, {}

                def scores(h):
                    g, qt = h // 4, h % 4
                    rows = slice(64 * g, 64 * g + HD)
                    (ba, oa), (bb, ob) = next_bank(), next_bank()
                    pe.after(*kept_ready, cmp_ready)
                    q0, q1 = q[rows, qt, 0:P], q[rows, qt, P:SEQ]
                    for i in range(2):
                        nc.tensor.matmul(oa[:, i * SEQ:(i + 1) * SEQ], q1, keys[rows, i, :], start=True, stop=True)
                    for i in range(2):
                        nc.tensor.matmul(ob[:, i * P:(i + 1) * P], q0, keys[rows, i, 0:P], start=True, stop=True)
                    for i, qq in enumerate((q0, q1)):
                        ins = nc.tensor.matmul(ob[:, 2 * P + i * NB:2 * P + (i + 1) * NB], qq,
                                               k_cmp[rows, g * NB:(g + 1) * NB], start=True, stop=True)
                    made[h] = (pe.done(ins), ba, bb)

                def branches(z):
                    return [(s1[z], 0), (s0[z], 2), (sc[z], 4)]

                def weights(h):
                    scored, ba, bb = made[h]
                    oa, ob = psum[ba], psum[bb]
                    z = h % 2
                    slope = -2.0 ** (-(h + 1))
                    free = (turned[h - 2],) if h >= 2 else ()
                    dve.after(scored, *free)
                    m = dve.done(nc.vector.scalar_tensor_tensor(
                        s1[z][:, :, :], bcast(dist[:, P:3 * P], 1, [P, 2, SEQ]), slope,
                        oa[:, :].rearrange("p (a s) -> p a s", a=2), ALU.mult, ALU.add))
                    read_by(ba, m)
                    nc.vector.scalar_tensor_tensor(
                        s0[z][:, :, :], bcast(dist[:, 0:P], 1, [P, 2, P]), slope,
                        ob[:, 0:2 * P].rearrange("p (a s) -> p a s", a=2), ALU.mult, ALU.add)
                    m = dve.done(nc.vector.scalar_tensor_tensor(
                        sc[z][:, :, :], cmp_dist, slope,
                        ob[:, 2 * P:2 * P + TB * NB].rearrange("p (a s) -> p a s", a=TB), ALU.mult, ALU.add))
                    read_by(bb, m)
                    dve.after(m)
                    for s, c in branches(z):
                        m = dve.done(nc.vector.tensor_reduce(nm[z][:, c:c + 2], s[:, :, :], AX_X, ALU.max, negate=True))
                    act.after(m)
                    for s, c in branches(z):
                        for i in range(2):
                            m = act.done(nc.scalar.activation(s[:, i, :], s[:, i, :], ACTF.Exp,
                                                              bias=nm[z][:, c + i:c + i + 1],
                                                              accum_out=sums[z][:, c + i:c + i + 1]))
                    soft[h] = m

                def gated_weights(h):
                    z = h % 2
                    m = dve.done(dve.after(soft[h]).reciprocal(sums[z][:, :], sums[z][:, :]))
                    dve.after(m, gates_ready)
                    for c, gate in ((0, gates[:, 1, 3 * h + 1:3 * h + 3]), (2, gates[:, 0, 3 * h + 1:3 * h + 3]),
                                    (4, gates[:, :, 3 * h])):
                        m = dve.done(nc.vector.tensor_tensor(wgt[z][:, c:c + 2], sums[z][:, c:c + 2], gate, ALU.mult))
                    dve.after(m)
                    for (s, c), w in zip(branches(z), (SEQ, P, NB)):
                        m = dve.done(nc.vector.tensor_tensor(s[:, :, :], s[:, :, :],
                                                             bcast(wgt[z][:, c:c + 2], 2, [P, 2, w]), ALU.mult))
                    soft[h] = m

                def transposes(h):
                    z = h % 2
                    (bc, oc), (bd, od) = next_bank(), next_bank()
                    pe.after(soft[h])
                    for i in range(2):
                        nc.tensor.transpose(oc[:, i * SEQ:i * SEQ + P], s0[z][:, i, :], ident)
                        nc.tensor.transpose(oc[:, i * SEQ + P:(i + 1) * SEQ], s1[z][:, i, 0:P], ident)
                        nc.tensor.transpose(od[:, i * P:(i + 1) * P], s1[z][:, i, P:SEQ], ident)
                    for i in range(TB):
                        ins = nc.tensor.transpose(od[0:NB, SEQ + i * P:SEQ + (i + 1) * P], sc[z][:, i, :], ident)
                    turned[h] = pe.done(ins)
                    free = (read[h - 2],) if h >= 2 else area_free
                    act.after(turned[h], *free)
                    m = act.done(nc.scalar.activation(pT[z][:, 0:512], oc[:, :], ACTF.Copy))
                    read_by(bc, m)
                    act.done(nc.scalar.activation(pT[z][:, 512:512 + SEQ], od[:, 0:SEQ], ACTF.Copy))
                    d = act.done(nc.scalar.activation(pT[z][0:NB, 768:1024], od[0:NB, SEQ:512], ACTF.Copy))
                    read_by(bd, d)
                    soft[h] = d

                def values(h):
                    g, kt, z = h // 4, h // 2, h % 2
                    rows = slice(64 * (h % 2), 64 * (h % 2) + HD)
                    bank, o = next_bank()
                    o = o[rows, 0:SEQ]
                    pe.after(soft[h])
                    p = pT[z]
                    for i in range(2):
                        c = slice((2 * i + g) * HD, (2 * i + g + 1) * HD)
                        nc.tensor.matmul(o, vals[:, 0, c], p[:, i * SEQ:(i + 1) * SEQ], start=(i == 0), stop=False)
                        nc.tensor.matmul(o[:, P:SEQ], vals[:, 1, c], p[:, 512 + i * P:512 + (i + 1) * P],
                                         start=False, stop=False)
                    read[h] = pe.done(nc.tensor.matmul(o, v_cmp[0:NB, g, :], p[0:NB, 768:1024], start=False, stop=True))
                    m = split_to(oT_hi[rows, kt, :], oT_lo[rows, kt, :], o, (read[h],))
                    read_by(bank, *m)


                def keyed(u):
                    h, b = units[u]
                    tok = slice(b * P, (b + 1) * P)
                    done["keyed", u] = dve.done(dve.after(done["exp", u]).tensor_tensor(
                        pair(u), pair(u), bcast(hk[:, h, tok], 1, [P, CH, P]), ALU.mult))
                    free = (done["a", u - 1],) if u >= 1 else ()
                    done["q_step", u] = pool.done(pool.after(zeroed_step, *q_made, *free).tensor_copy(
                        step_cells, hq[:, h, tok].rearrange("p (c j) -> p c j", j=CH)))

                def turn_keys(u):
                    h, b = units[u]
                    bank, o = next_bank()
                    o = o[:, 0:P]
                    pe.after(k_end_ready)
                    m = pe.done(nc.tensor.transpose(o, k_end[:, h, b * P:(b + 1) * P], ident))
                    free = (done["kv", u - 2, 1],) if u >= 2 else ()
                    done["keT", u] = act.done(act.after(m, *free).activation(keT[u % 2], o, ACTF.Copy))
                    read_by(bank, done["keT", u])

                def chunk_products(u, half):
                    h, b = units[u]
                    last = (u, 0) if half else (u - 1, 1)
                    free = (done["kv", last[0], last[1]],) if last[0] >= 0 else (cmp_ready,)
                    v_masked = pool.done(pool.after(*kept_ready, *free).tensor_tensor(
                        vm[:, :, :], bcast(hv[:, b, h * P:(h + 1) * P], 1, [P, 4, P]),
                        bcast(cst("chunk_row")[:, 4 * half:4 * half + 4], 2, [P, 4, P]), ALU.mult))
                    o = bank_for(KV[half])[:, :]
                    pe.after(done["keT", u], v_masked)
                    done["kv", u, half] = pe.done(nc.tensor.matmul(
                        o, keT[u % 2], vm[:, :, :].rearrange("p c v -> p (c v)"), start=True, stop=True))

                def pair_products(u):
                    bank, o = next_bank()
                    o = o[:, 0:P]
                    pe.after(done["keyed", u], done["q_step", u])
                    for j in range(CH):
                        ins = nc.tensor.matmul(o, pair(u)[:, j, :], q_step[:, j, :],
                                               start=(j == 0), stop=(j == CH - 1))
                    done["a", u] = pe.done(ins)
                    done["a bank", u] = bank

                def own_pairs(u):
                    free = (done["out", u - 2],) if u >= 2 else ()
                    bank = done["a bank", u]
                    done["aT", u] = dve.done(dve.after(done["a", u], *free).tensor_tensor(
                        aT[u % 2], psum[bank][:, 0:P], cst("chunk_pair"), ALU.mult))
                    read_by(bank, done["aT", u])

                def states(u):
                    h, b = units[u]
                    tok = slice(b * P, (b + 1) * P)
                    free = (done["out", u - 1],) if u >= 1 else ()
                    in_chunks = lambda a: a[:, h, tok].rearrange("p (c j) -> p c j", j=CH)
                    done["q_chunk", u] = dve.done(dve.after(zeroed, expb_ready, *q_made, *free).tensor_tensor(
                        chunk_cells, in_chunks(hq), in_chunks(exp_b), ALU.mult))
                    if b == 0:
                        s = dve.done(nc.vector.memset(state[:, 0, :], 0.0))
                    else:
                        s = done["state", u - 1]
                    for half in range(2):
                        for c4 in range(4):
                            c = b * CPB + 4 * half + c4
                            if c == TB * CPB - 1:
                                continue
                            end = c * CH + CH - 1
                            s = dve.done(dve.after(done["kv", u, half], s).scalar_tensor_tensor(
                                state[:, (c + 1) % (CPB + 1), :], state[:, c % (CPB + 1), :],
                                exp_b[:, h, end:end + 1], psum[KV[half]][:, c4 * P:(c4 + 1) * P], ALU.mult, ALU.add))
                        read_by(KV[half], s)
                    done["state", u] = s

                def outputs(u):
                    h, b = units[u]
                    z = u % 2
                    bank, o = next_bank()
                    o = o[:, 0:P]
                    pe.after(done["aT", u], done["q_chunk", u], done["state", u], *kept_ready)
                    nc.tensor.matmul(o, aT[z], hv[:, b, h * P:(h + 1) * P], start=True, stop=False)
                    for c in range(CPB):
                        ins = nc.tensor.matmul(o, q_chunk[:, c, :], state[:, (b * CPB + c) % (CPB + 1), :],
                                               start=False, stop=(c == CPB - 1))
                    done["out", u] = pe.done(ins)
                    free = (done["turned", u - 2],) if u >= 2 else ()
                    m = act.done(act.after(done["out", u], *free).activation(
                        o_gated[z][:, :], o, ACTF.Square, accum_out=ssq[z][:, :]))
                    done["o", u] = act.done(act.after(m).activation(o_gated[z][:, :], o, ACTF.Copy))
                    read_by(bank, done["o", u])

                def gate_output(u):
                    h, b = units[u]
                    z = u % 2
                    m = dve.done(dve.after(done["o", u]).tensor_scalar(rms[z][:, :], ssq[z][:, :], 1.0 / P, RMS_EPS,
                                                                       ALU.mult, ALU.add))
                    m = pool.done(pool.after(m, minus_half).tensor_tensor(
                        rms[z][:, :], rms[z][:, :], expo[:, 0:1], ALU.pow))
                    done["gated", u] = dve.done(dve.after(m, g_ready).scalar_tensor_tensor(
                        o_gated[z][:, :], o_gated[z][:, :], rms[z][:, :], hg[:, b, h * P:(h + 1) * P],
                        ALU.mult, ALU.mult))

                def turn_output(u):
                    h, b = units[u]
                    bank, o = next_bank()
                    o = o[:, 0:P]
                    pe.after(done["gated", u])
                    done["turned", u] = pe.done(nc.tensor.transpose(o, o_gated[u % 2][:, :], ident))
                    kt = KD - HG + h
                    tok = slice(b * P, (b + 1) * P)
                    read_by(bank, *split_to(oT_hi[:, kt, tok], oT_lo[:, kt, tok], o, (done["turned", u],)))

                steps = len(units)
                on = lambda stage, i: stage(i) if 0 <= i < steps else None
                for k in range(steps + 2):
                    on(turn_keys, k)
                    on(keyed, k)
                    on(scores, k)
                    on(gate_output, k - 2)
                    on(weights, k)
                    on(states, k - 1)
                    on(values, k - 2)
                    on(turn_output, k - 2)
                    on(pair_products, k)
                    on(lambda u: chunk_products(u, 0), k)
                    on(decays, k + 1)
                    on(outputs, k - 1)
                    on(gated_weights, k)
                    on(lambda u: chunk_products(u, 1), k)
                    on(transposes, k - 1)
                    on(own_pairs, k)
                for i, (index, _, _) in enumerate(scratch):
                    ws.give_back(index, *((done["a", steps - 2 + i], read[steps - 2 + i]) if i < 2 else
                                          ((pe, pe.count), (dve, dve.count))))
                gains_read[0] = ((pe, pe.count), (pool, pool.count))
                g_mark = load_gains(2)
                meet()
                made = out_product(lambda k: oT_hi[:, k, :], lambda k: oT_lo[:, k, :],
                                   {k: ((act, act.count), (dve, dve.count)) for k in range(KD)}, 3, KD)
                return made, g_mark

        def add_mask(h, s, o, made, free):
            return dve.done(dve.after(made, *free).tensor_tensor(s, o, cst("causal"), ALU.add))

        def attention(n, tile, scores, add_bias, value, scale, dv, sink, next_bank):
            s = [tile(f"s{i}", [P, 3 * P]) for i in range(3)]
            pT = [tile(f"pT{i}", [P, 3 * P]) for i in range(2)]
            nm = [tile(f"nm{i}", [P, 2]) for i in range(3)]
            sums = [tile(f"sums{i}", [P, 2]) for i in range(3)]
            soft, turned, read = {}, {}, {}
            spans = ((0, 0, P), (1, P, 3 * P))

            def softmax(h):
                z = h % 3
                bank, o = next_bank()
                scores(h, 0, o[:, 0:P], P)
                made = pe.done(scores(h, 1, o[:, P:3 * P], SEQ))
                free = (turned[h - 3],) if h >= 3 else ()
                m = add_bias(h, s[z][:, :], o[:, 0:3 * P], made, free)
                read_by(bank, m)
                dve.after(m)
                for b, c0, c1 in spans:
                    m = dve.done(nc.vector.tensor_reduce(nm[z][:, b:b + 1], s[z][:, c0:c1], AX_X, ALU.max, negate=True))
                if scale != 1.0:
                    m = dve.done(dve.after(m).tensor_scalar(nm[z][:, :], nm[z][:, :], scale, None, ALU.mult))
                act.after(m)
                for b, c0, c1 in spans:
                    m = act.done(nc.scalar.activation(s[z][:, c0:c1], s[z][:, c0:c1], ACTF.Exp, scale=scale,
                                                      bias=nm[z][:, b:b + 1], accum_out=sums[z][:, b:b + 1]))
                soft[h] = m

            def normalise(h):
                z = h % 3
                m = dve.done(dve.after(soft[h]).reciprocal(sums[z][:, :], sums[z][:, :]))
                dve.after(m)
                for b, c0, c1 in spans:
                    m = dve.done(nc.vector.tensor_scalar(s[z][:, c0:c1], s[z][:, c0:c1], sums[z][:, b:b + 1], None, ALU.mult))
                soft[h] = m

            def transposes(h):
                z = h % 2
                bank, o = next_bank()
                pe.after(soft[h])
                for i in range(3):
                    ins = nc.tensor.transpose(o[:, i * P:(i + 1) * P], s[h % 3][:, i * P:(i + 1) * P], ident)
                turned[h] = pe.done(ins)
                free = (read[h - 2],) if h >= 2 else ()
                soft[h] = act.done(act.after(turned[h], *free).activation(pT[z][:, :], o[:, 0:3 * P], ACTF.Copy))
                read_by(bank, soft[h])

            def values(h):
                z = h % 2
                base = dv * h % P
                bank, o = next_bank()
                o = o[base:base + dv, 0:SEQ]
                pe.after(soft[h])
                nc.tensor.matmul(o, value(h, 0), pT[z][:, 0:SEQ], start=True, stop=False)
                read[h] = pe.done(nc.tensor.matmul(o[:, P:SEQ], value(h, 1), pT[z][:, SEQ:3 * P], start=False, stop=True))
                read_by(bank, *sink(h, o, read[h]))

            return softmax, normalise, transposes, values

        def fox(xT_ready):
            with ExitStack() as scope:
                def tile(name, shape, dt=F32):
                    return scope.enter_context(nc.sbuf_tensor("fox_" + name, shape, dt))

                oT_hi, oT_lo = tile("oT_hi", [P, KD, SEQ], F32R), tile("oT_lo", [P, KD, SEQ], F32R)
                v = xn
                q = [tile(f"q{i}", [P, SEQ]) for i in range(2)]
                k = [tile(f"k{i}", [P, SEQ]) for i in range(2)]
                z_f, ones, cum = (tile(x, [FOX_H, SEQ]) for x in ("f", "ones", "cum"))
                spare = neg = tile("spare", [FOX_H, SEQ])
                k_cum = tile("k_cum", [P, FOX_H * SEQ])
                q_cum = tile("q_cum", [P, TB, FOX_H])
                bias = [tile(f"bias{i}", [P, 3 * P]) for i in range(2)]

                ones_ready = pool.done(pool.after().memset(ones[:, :], 1.0))

                fin = {}

                def f_sink(o, m):
                    fin["f"] = act.done(act.after(m, s_mark).activation(
                        z_f[:, :], o[0:FOX_H, :], ACTF.Identity, bias=small[0:FOX_H, HG + 1:HG + 2]))
                    return (fin["f"],)
                feature_tiles(1, (6, 7), xT_ready, [f_sink])
                def v_sink(i):
                    def sink(b, o, m):
                        c = act.done(act.after(m, *xn_read[0]).activation(v[:, b, i * SEQ:(i + 1) * SEQ], o, ACTF.Copy))
                        kept.append(c)
                        return (c,)
                    return sink
                token_tiles(SEQ, (6, 7), xT_ready, v_sink(0))
                m = act.done(act.after(fin["f"]).activation(spare[:, :], z_f[:, :], ACTF.Abs))
                m = act.done(act.after(m).activation(spare[:, :], spare[:, :], ACTF.Exp, scale=-1.0))
                m = act.done(act.after(m).activation(spare[:, :], spare[:, :], ACTF.Ln, bias=1.0))
                m = dve.done(dve.after(m).scalar_tensor_tensor(z_f[:, :], z_f[:, :], 0.0, spare[:, :], ALU.min, ALU.subtract))
                cum_ready = m = dve.done(dve.after(m, ones_ready).tensor_tensor_scan(cum[:, :], ones[:, :], z_f[:, :], 0.0, ALU.mult, ALU.add))
                m = dve.done(dve.after(m).tensor_scalar(neg[:, :], cum[:, :], -1.0, None, ALU.mult))
                m = small_landed.done(sp.after(m).dma_start(t["cum_scratch"], neg[:, :]), 16)
                k_cum_ready = small_landed.done(sp.after(m).dma_start(
                    k_cum[:, :], t["cum_scratch"].rearrange("h s -> (h s)").unsqueeze(0).to_broadcast([P, FOX_H * SEQ])), 16)
                token_tiles(SEQ, (6, 7), xT_ready, v_sink(1))
                o = bank_for(5)
                pe.after(cum_ready)
                for b in range(TB):
                    ins = nc.tensor.transpose(o[:, b * FOX_H:(b + 1) * FOX_H], cum[:, b * P:(b + 1) * P],
                                              ident[0:FOX_H, 0:FOX_H])
                q_cum_ready = dve.done(dve.after(pe.done(ins)).tensor_copy(
                    q_cum[:, :, :].rearrange("p b h -> p (b h)"), o[:, 0:TB * FOX_H]))
                read_by(5, q_cum_ready)
                for i in (2, 3):
                    token_tiles(SEQ, (6, 7), xT_ready, v_sink(i))

                qk = {}
                softdone = {}
                biased = {}

                def scores(h, b, o, width):
                    z = h // 2 % 2
                    rows = slice(64 * (h % 2), 64 * (h % 2) + 64)
                    pe.after(*qk[h // 2])
                    return nc.tensor.matmul(o, q[z][rows, b * P:(b + 1) * P], k[z][rows, 0:width], start=True, stop=True)

                def key_bias(h):
                    z = h % 2
                    free = (biased[h - 2],) if h >= 2 else ()
                    pool.after(k_cum_ready, *free)
                    kc = k_cum[:, h * SEQ:(h + 1) * SEQ]
                    nc.gpsimd.tensor_tensor(bias[z][:, 0:P], cst("causal")[:, 0:P], kc[:, 0:P], ALU.add)
                    return pool.done(nc.gpsimd.tensor_tensor(bias[z][:, P:3 * P], cst("causal")[:, P:3 * P], kc, ALU.add))

                def add_bias(h, s, o, made, free):
                    ready = key_bias(h)
                    dve.after(made, ready, q_cum_ready, *free)
                    for b, c0, c1 in ((0, 0, P), (1, P, 3 * P)):
                        m = dve.done(nc.vector.scalar_tensor_tensor(
                            s[:, c0:c1], o[:, c0:c1], q_cum[:, b, h:h + 1], bias[h % 2][:, c0:c1], ALU.add, ALU.add))
                    biased[h] = m
                    return m

                def sink(h, o, m):
                    rows = slice(64 * (h % 2), 64 * (h % 2) + 64)
                    return split_to(oT_hi[rows, h // 2, :], oT_lo[rows, h // 2, :], o, (m, *kept))

                next_bank = taking_turns(range(8))
                softmax, normalise, transposes, values = attention(
                    FOX_H, tile, scores, add_bias, lambda h, b: v[:, b, h * 64:(h + 1) * 64], 1.0, 64, sink, next_bank)

                fox_weights = {}
                QK_PIECES = (2, 0, 2, 0)

                def take(p):
                    fox_weights[p] = ws.take(ahead=p == 0)
                    pe.after(*fox_weights[p][3])
                    qk[p] = []

                def project(p, part):
                    i, hi, lo, _ = fox_weights[p]
                    bank, o = next_bank()
                    m = pe.done(feature_major(o[:, 0:SEQ], hi, lo, lambda k: (2 * k + part) * P, KD, xT_hi, xT_lo, xT_ready))
                    dst, scale = ((q, 64 ** -0.5), (k, 1.0))[part]
                    c = act.done(act.after(m, *softdone.get(p - 2, ())).activation(
                        dst[p % 2][:, :], o[:, 0:SEQ], ACTF.Copy, scale=scale))
                    read_by(bank, c)
                    qk[p].append(c)
                    if part == 1:
                        ws.release(i, m)

                take(0)
                project(0, 0)
                project(0, 1)
                pe.after(*kept)
                for h in range(FOX_H + 3):
                    if h < FOX_H:
                        softmax(h)
                        if h % 2:
                            softdone[h // 2] = ((pe, pe.count),)
                    if 1 <= h <= FOX_H:
                        normalise(h - 1)
                    nxt = h // 2 + 1
                    if h % 2 == 0 and nxt < FOX_H // 2:
                        take(nxt)
                    behind = fox_weights[min(nxt, FOX_H // 2 - 1)][0] + 1
                    ws.split_parts(behind, QK_PIECES, h % 2 * 2)
                    if nxt < FOX_H // 2:
                        project(nxt, h % 2)
                    if 2 <= h < FOX_H + 2:
                        transposes(h - 2)
                    ws.split_parts(behind, QK_PIECES, h % 2 * 2 + 1)
                    if h >= 3:
                        values(h - 3)
                kept.clear()
                xn_read[0] = ((pe, pe.count),)
                made = out_product(lambda i: oT_hi[:, i, :], lambda i: oT_lo[:, i, :],
                                   {k: ((act, act.count), (dve, dve.count)) for k in range(KD)}, 3, KD)
                return made

        def shared_kv():
            stat = sb("kv_stat", [P, TB, 2])
            tmp = sig[0]
            work = {}

            def project(xT_ready):
                def c_sink(b, o, m):
                    work["c", b] = (o, m)
                    return ()

                def rope_sink(name):
                    def sink(o, m):
                        work[name] = (o, m)
                        return ()
                    return sink
                token_tiles(KL, ACC[0:2], xT_ready, c_sink)
                feature_tiles(2, ACC[2:4], xT_ready, [rope_sink("rope"), rope_sink("swap")])
                xT_read[0] = ((pe, pe.count),)

            def finish(gain_mark):
                for b in range(TB):
                    o, m = work["c", b]
                    work["n", b] = rms_rows(o, xn[:, b, 512:512 + KL], kvq_gain[:, 0:KL], stat, b,
                                            (m, gain_mark, *xn_read[0]))
                    read_by(ACC[b], work["n", b])
                o, m = work["rope"]
                r = dve.done(dve.after(m).tensor_tensor(k_rope[:, :], o, cst("cos"), ALU.mult))
                read_by(ACC[2], r)
                o, m = work["swap"]
                a = dve.done(dve.after(m).tensor_tensor(tmp[:, :], o, cst("sin"), ALU.mult))
                read_by(ACC[3], a)
                return dve.done(dve.after(a, r).tensor_tensor(k_rope[:, :], k_rope[:, :], tmp[:, :], ALU.add))

            def turn_kv():
                return turn([(b, 0, xn[:, b, 512:512 + KL], lambda b=b: work["n", b]) for b in range(TB)],
                            KL // P, ckv_hi, ckv_lo, ())
            return project, finish, turn_kv

        def mla(xT_ready, gain_mark, turn_kv, rope_ready):
            with ExitStack() as scope:
                def tile(name, shape, dt=F32):
                    return scope.enter_context(nc.sbuf_tensor("mla_" + name, shape, dt))

                o2_hi, o2_lo = tile("oT_hi", [P, KD, SEQ], F32R), tile("oT_lo", [P, KD, SEQ], F32R)
                cq_hi, cq_lo = tile("cqT_hi", [P, QL // P, SEQ], F32R), tile("cqT_lo", [P, QL // P, SEQ], F32R)
                qn2, kn2 = ([tile(f"{x}{i}", [P, 2, SEQ]) for i in range(2)] for x in ("q_nope", "k_nope"))
                qr2 = [tile(f"q_rope{i}", [P, SEQ]) for i in range(2)]
                v2 = [tile(f"v{i}", [P, TB, 2 * P]) for i in range(2)]
                qs = tile("q_swap", [P, SEQ])
                got = []

                def c_sink(b, o, m):
                    r = rms_rows(o, xn[:, b, 0:QL], kvq_gain[:, KL:KL + QL], q_stat, b, (m, gain_mark, *xn_read[0]))
                    got.append(r)
                    return (r,)
                q_stat = tile("q_stat", [P, TB, 2])
                token_tiles(QL, SPARE, xT_ready, c_sink)
                x_free = (pe, pe.count)
                ckv_ready = turn_kv()
                cq_ready = turn([(b, 0, xn[:, b, :], lambda b=b: got[b]) for b in range(TB)], QL // P, cq_hi, cq_lo, ())
                xn_read[0] = ((pe, pe.count),)

                kq, kk = QL // P, KL // P
                at_k, at_v = kq * 4 * P, kq * 4 * P + kk * 2 * P
                next_bank = taking_turns(range(8))
                weights, qk_ready, v_ready = {}, {}, {}
                scored, valued = {}, {}

                def tile_of(p, cols, k_tiles, a_hi, a_lo, ready):
                    _, hi, lo, _ = weights[p]
                    bank, o = next_bank()
                    return bank, o[:, 0:SEQ], pe.done(feature_major(o[:, 0:SEQ], hi, lo, cols, k_tiles, a_hi, a_lo, ready))

                def copied(bank, dst, o, m, free):
                    c = act.done(act.after(m, *free).activation(dst, o, ACTF.Copy))
                    read_by(bank, c)
                    return c

                def project_keys(p):
                    weights[p] = ws.take(ahead=p == 0)
                    pe.after(*weights[p][3])
                    qk_ready[p] = []
                    for j in range(2):
                        bank, o, m = tile_of(p, lambda k: at_k + 2 * P * k + j * P, kk, ckv_hi, ckv_lo, ckv_ready)
                        qk_ready[p].append(copied(bank, kn2[p % 2][:, j, :], o, m, scored.get(p - 2, ())))

                def project_queries(p):
                    qn, qr = qn2[p % 2], qr2[p % 2]
                    free = scored.get(p - 2, ())
                    bank, o, m = tile_of(p, lambda k: 4 * P * k + 2 * P, kq, cq_hi, cq_lo, cq_ready)
                    r = dve.done(dve.after(m, *free).tensor_tensor(qr[:, :], o, cst("cos"), ALU.mult))
                    read_by(bank, r)
                    bank, o, m = tile_of(p, lambda k: 4 * P * k + 3 * P, kq, cq_hi, cq_lo, cq_ready)
                    r = dve.done(dve.after(m, *free).tensor_tensor(qs[:, :], o, cst("sin"), ALU.mult))
                    read_by(bank, r)
                    qk_ready[p].append(dve.done(dve.after(r).tensor_tensor(qr[:, :], qr[:, :], qs[:, :], ALU.add)))
                    for j in range(2):
                        bank, o, m = tile_of(p, lambda k: 4 * P * k + j * P, kq, cq_hi, cq_lo, cq_ready)
                        qk_ready[p].append(copied(bank, qn[:, j, :], o, m, free))

                def project_values(p):
                    i, hi, lo, _ = weights[p]
                    v_ready[p] = []
                    for b in range(TB):
                        bank, o = next_bank()
                        m = pe.done(token_major(o[:, 0:2 * P], hi, lo, lambda k: at_v + 2 * P * k, 2 * P, range(kk),
                                                lambda k: ckv_hi[:, k, :], lambda k: ckv_lo[:, k, :], b, True, True,
                                                ckv_ready))
                        v_ready[p].append(copied(bank, v2[p % 2][:, b, :], o[:, 0:2 * P], m, valued.get(p - 2, ())))
                    ws.release(i, m)

                def scores(h, b, o, width):
                    j = h % 2
                    rows = slice(64 * j, 64 * j + 64)
                    pe.after(*qk_ready[h // 2], rope_ready)
                    qn, kn, qr = qn2[h // 2 % 2], kn2[h // 2 % 2], qr2[h // 2 % 2]
                    nc.tensor.matmul(o, qn[:, j, b * P:(b + 1) * P], kn[:, j, 0:width], start=True, stop=False)
                    return nc.tensor.matmul(o, qr[rows, b * P:(b + 1) * P], k_rope[rows, 0:width], start=False, stop=True)

                def halves(h):
                    return (xT_hi, xT_lo) if h < KD else (o2_hi, o2_lo)

                def sink(h, o, m):
                    hi, lo = halves(h)
                    return split_to(hi[:, h % KD, :], lo[:, h % KD, :], o, (m, x_free))

                softmax, normalise, transposes, values = attention(
                    MLA_H, tile, scores, add_mask, lambda h, b: v2[h // 2 % 2][:, b, h % 2 * P:h % 2 * P + P],
                    192 ** -0.5, P, sink, next_bank)

                project_keys(0)
                project_queries(0)
                n_pairs = MLA_H // 2
                for h in range(MLA_H + 3):
                    p = h // 2
                    if h < MLA_H:
                        softmax(h)
                        if h % 2:
                            scored[p] = ((pe, pe.count),)
                    if 1 <= h <= MLA_H:
                        normalise(h - 1)
                    if h % 2 and p + 1 < n_pairs:
                        project_queries(p + 1)
                    if h % 2:
                        ws.split_parts(weights[min(p + 1, n_pairs - 1)][0] + 1, (3, 3), 0)
                    if 2 <= h < MLA_H + 2:
                        transposes(h - 2)
                    if h % 2:
                        ws.split_parts(weights[min(p + 1, n_pairs - 1)][0] + 1, (3, 3), 1)
                    if h >= 3:
                        pe.after(*v_ready[(h - 3) // 2])
                        values(h - 3)
                        if h % 2 == 0:
                            valued[(h - 3) // 2] = ((pe, pe.count),)
                    if h % 2 == 0 and p < n_pairs:
                        project_values(p)
                        if p + 1 < n_pairs:
                            project_keys(p + 1)
                made = out_product(lambda h: halves(h)[0][:, h % KD, :], lambda h: halves(h)[1][:, h % KD, :],
                                   {k: ((act, act.count), (dve, dve.count)) for k in range(MLA_H)}, 6, MLA_H)
                return made

        def ple(layer, scope):
            def tile(name, shape, dt=F32):
                return scope.enter_context(nc.sbuf_tensor(f"ple{layer}_" + name, shape, dt))

            pT = tile("pT", [P, 2, SEQ])
            pT_hi, pT_lo = tile("pT_hi", [P, 2, SEQ], F32R), tile("pT_lo", [P, 2, SEQ], F32R)
            proj = tile("proj", [P, TB, D])
            z = tile("z", [P, TB, D])
            bias = tile("bias", [P, D])
            free = [(e, e.count) for e in everyone]
            small_landed.done(sp.after(*free).dma_start(pT[:, :, :], t["pT"][layer, :, :, :]), 16)
            landed = small_landed.done(sp.after().dma_start(
                bias[:, :], t["gains"][14 + layer:15 + layer, 0:D].to_broadcast([P, D])), 16)
            made, kept_proj = {}, {}

            def project():
                ready = split_to(pT_hi[:, :, :], pT_lo[:, :, :], pT[:, :, :], (landed,))
                made["proj"] = out_product(lambda k: pT_hi[:, k, :], lambda k: pT_lo[:, k, :],
                                           {k: ready for k in range(2)}, 1, 2, per=2, then_norm=False)

            def keep_projection(b):
                for half in range(2):
                    c = slice(512 * half, 512 * (half + 1))
                    kept_proj[b] = act.done(act.after(made["proj"][b][half], *free).activation(
                        proj[:, b, c], psum[ACC[2 * b + half]][:, :], ACTF.Copy))
                    read_by(ACC[2 * b + half], kept_proj[b])

            def gate(xT_ready):
                made["gate"] = out_product(lambda k: xT_hi[:, k, :], lambda k: xT_lo[:, k, :], xT_ready, 3, KD)
                return made["gate"]

            def add(b, xs_ready):
                for half in range(2):
                    c = slice(512 * half, 512 * (half + 1))
                    bank = ACC[2 * b + half]
                    m = dve.done(dve.after(made["gate"][b][half], landed).tensor_tensor(
                        z[:, b, c], psum[bank][:, :], bias[:, c], ALU.add))
                    read_by(bank, m)
                    made["z", half] = act.done(act.after(m).activation(z[:, b, c], z[:, b, c], ACTF.Sigmoid))
                for half in range(2):
                    c = slice(512 * half, 512 * (half + 1))
                    m = dve.done(dve.after(made["z", half], kept_proj[b]).tensor_tensor(
                        z[:, b, c], z[:, b, c], proj[:, b, c], ALU.mult))
                    m = dve.done(dve.after(m, xs_ready).scalar_tensor_tensor(
                        x[:, b, c], z[:, b, c], 1.0, x[:, b, c], ALU.mult, ALU.add,
                        accum_out=row_sums[:, b, half:half + 1]))
                return m
            return project, keep_projection, gate, add

        xT_read = [()]
        xn_read = [()]

        def add_block(b, scale, made, ready):
            for half in range(2):
                xs = x[:, b, 512 * half:512 * (half + 1)]
                bank = ACC[2 * b + half]
                m = dve.done(dve.after(made[b][half], *ready).scalar_tensor_tensor(
                    xs, psum[bank][:, :], scale, xs, ALU.mult, ALU.add,
                    accum_out=row_sums[:, b, half:half + 1]))
                read_by(bank, m)
            return m

        def scale_x(x_ready):
            return act.done(act.after(*x_ready, (pe, pe.count)).activation(x[:, :, :], x[:, :, :], ACTF.Copy, scale=ALPHA))

        def turn_made(roots, make, src):
            made, rstd_ready = [], {}

            def one(b, c):
                if b not in rstd_ready:
                    rstd_ready[b] = roots[b]()
                made.append(make(b, c, rstd_ready[b]))
                return made[-1]
            pieces = [(b, k0, src(b), lambda b=b, k0=k0: one(b, slice(k0 * P, (k0 + 4) * P)))
                      for k0 in range(0, KD, 4) for b in range(TB)]
            marks = turn(pieces, KD, xT_hi, xT_lo, xT_read[0])
            gains_read[0] = tuple(made)
            return marks, made

        def next_rms(add, g_mark, in_place=False):
            roots = [rms_root(x[:, b, :], b, (add(b),)) for b in range(TB)]
            dst = x if in_place else xn
            free = () if in_place else xn_read[0]
            marks, made = turn_made(
                roots, lambda b, c, r: rms_apply(x[:, b, :], dst[:, b, :], b, c, (r, g_mark, *free)), lambda b: dst[:, b, :])
            if not in_place:
                xn_read[0] = ((pe, pe.count),)
            return marks, made

        def next_ln(add, g_mark, turned=True, during=(lambda: None,) * 3):
            means, roots = zip(*(ln_root(b, (add(b),)) for b in range(TB)))
            during[0]()
            during[1]()
            make = lambda b, c, r: ln_apply(b, c, (r, means[b], g_mark))
            if not turned:
                return None, [make(b, slice(0, D), roots[b]()) for b in range(TB)]
            marks, made = turn_made(roots, make, lambda b: x[:, b, :])
            during[2]()
            return marks, scale_x(made)

        def finish(ready):
            m = out_landed.done(sp.after(*ready).dma_start(out.rearrange("(b p) d -> p b d", p=P), x[:, :, :]), 16)
            sp.after(m)

        g_mark = g_first
        pe.after(ident_mark)
        xT_ready, _ = next_rms(lambda b: x_mark[b], g_mark)
        g_mark = load_gains(1)
        ws.split_behind(GU, 4, dve)
        made = ffn(xT_ready)
        xT_read[0] = (made[-1][-1],)

        xT_ready, _ = next_rms(lambda b: add_block(b, 0.5, made, ()), g_mark)
        pe.after(c_mark)
        meet()
        made, g_mark = mixer(xT_ready)
        xT_read[0] = (made[-1][-1],)

        xT_ready, _ = next_rms(lambda b: add_block(b, 1.0, made, ()), g_mark)
        g_mark = load_gains(3)
        made = ffn(xT_ready)
        xT_read[0] = (made[-1][-1],)
        xT_ready, x_ready = next_rms(lambda b: add_block(b, 0.5, made, ()), g_mark, in_place=True)
        xs_ready = scale_x(x_ready)

        for layer in range(2):
            base = 4 + 4 * layer
            if layer == 1:
                ckv_hi = sb("ckvT_hi", [P, KL // P, SEQ], F32R)
                ckv_lo = sb("ckvT_lo", [P, KL // P, SEQ], F32R)
                k_rope = sb("k_rope", [P, SEQ])
                kvq_gain = sb("kv_and_query_gain", [P, KL + QL])
                small_landed.done(sp.after(*((e, e.count) for e in everyone)).dma_start(
                    kvq_gain[:, 0:KL], t["gains"][12:13, 0:KL].to_broadcast([P, KL])), 16)
                kvq_mark = small_landed.done(sp.after().dma_start(
                    kvq_gain[:, KL:KL + QL], t["gains"][13:14, 0:QL].to_broadcast([P, QL])), 16)
                project_kv, finish_kv, turn_kv = shared_kv()
            g_mark = load_gains(base)
            made = ffn(xT_ready)
            xT_read[0] = (made[-1][-1],)
            idle = lambda: None
            xT_ready, xs_ready = next_ln(lambda b: add_block(b, 0.5, made, (xs_ready,)), g_mark,
                                         during=(lambda: project_kv(xT_ready) if layer else None, idle, idle))
            if layer == 0:
                g_mark = load_gains(base + 1)
                made = fox(xT_ready)
            else:
                g_mark = load_gains(base + 1)
                made = mla(xT_ready, kvq_mark, turn_kv, finish_kv(kvq_mark))
            xT_read[0] = (made[-1][-1],)
            xT_ready, xs_ready = next_ln(lambda b: add_block(b, 1.0, made, (xs_ready,)), g_mark)
            ple_scope = ctx.enter_context(ExitStack())
            project, keep_projection, gate, add_gated = ple(layer, ple_scope)
            g_mark = load_gains(base + 2)
            made = ffn(xT_ready)
            xT_read[0] = (made[-1][-1],)
            xT_ready, xs_ready = next_ln(lambda b: add_block(b, 0.5, made, (xs_ready,)), g_mark,
                                         during=(project, lambda: keep_projection(0), lambda: keep_projection(1)))
            g_mark = load_gains(base + 3)
            made = gate(xT_ready)
            xT_read[0] = (made[-1][-1],)
            xT_ready, xs_ready = next_ln(lambda b: add_gated(b, xs_ready), g_mark, turned=layer == 0)
            ple_scope.close()
        finish(xs_ready)


def rows_of(w):
    return w.reshape(w.shape[0] // P, P, w.shape[1]).transpose(1, 0, 2)


def chunk(*parts):
    return np.concatenate([rows_of(w) for w in parts], 2).reshape(1, P, -1)


def ffn_chunks(w_gu, w_down):
    f = w_down.shape[0]
    pad = FF_TILES * P - f
    wide = lambda w: np.concatenate([w, np.zeros((D, pad), np.float32)], 1)
    gate = rows_of(wide(w_gu[:, :f])).reshape(P, KD, FF_TILES, 1, P)
    up = rows_of(wide(w_gu[:, f:])).reshape(P, KD, FF_TILES, 1, P)
    gu = np.concatenate([gate, up], 3).transpose(2, 0, 1, 3, 4).reshape(FF_TILES, P, GU)
    down = np.concatenate([w_down, np.zeros((pad, D), np.float32)], 0).reshape(FF_TILES, P, D)
    return np.concatenate([gu, down], 2)


def k_chunks(w, per=3):
    r = rows_of(w)
    n = r.shape[1] // per
    whole = r[:, :n * per].reshape(P, n, per * D).transpose(1, 0, 2)
    rest = r[:, n * per:].reshape(1, P, -1)
    return whole, rest


def layouts(a):
    t = {"const": const_table(), "x": a["x"][0]}
    t["ffn_a"] = ffn_chunks(a["ffn1_w_gu"][0], a["ffn1_w_down"][0])
    t["ffn_b"] = ffn_chunks(a["ffn2_w_gu"][0], a["ffn2_w_down"][0])
    for i, n in ((0, "c"), (1, "e")):
        t["ffn_" + n] = ffn_chunks(a["ffn1_w_in_2"][i], a["ffn1_w_out_2"][i])
    for i, n in ((0, "d"), (1, "f")):
        t["ffn_" + n] = ffn_chunks(a["ffn2_w_in_2"][i], a["ffn2_w_out_2"][i])
    w = a["w_in"][0]
    kv = GROUPS * HD
    sizes = (HEADS * HD, kv, kv, kv, kv, kv, kv, GATES, HG * P, HG * P, HG * P, HG * P)
    ends = np.cumsum(sizes)
    nq, kc, vc, ks, vs, kw, vw, gl, hq, hf, hi, hg = (w[:, e - s:e] for e, s in zip(ends, sizes))
    tile = lambda m, j: m[:, j * P:(j + 1) * P]
    heads = lambda j: np.concatenate([nq[:, h * HD:(h + 1) * HD] for h in (j, j + HEADS // GROUPS)], 1)
    t["nsa_a"] = chunk(kc, vc, ks)
    t["nsa_b"] = chunk(kw, heads(0), heads(1))
    t["nsa_c"] = chunk(heads(2), heads(3))
    t["nsa_v"] = chunk(vs, vw, gl)
    t["hg_v"] = np.concatenate([chunk(hi[:, :SEQ]), chunk(hi[:, SEQ:])])
    t["hg_g"] = np.concatenate([chunk(hg[:, :SEQ]), chunk(hg[:, SEQ:])])
    t["hg_fq"] = np.concatenate([chunk(tile(hf, h), tile(hq, h)) for h in range(HG)])
    w1 = [rows_of(a[n][0]).reshape(P, 2, LP // 2 * CMP_HID).transpose(1, 0, 2) for n in ("cmp_k_w1", "cmp_v_w1")]
    t["cmp_w1"] = np.concatenate(w1)
    k2, v2 = rows_of(a["cmp_k_w2"][0]), rows_of(a["cmp_v_w2"][0])
    t["cmp_w2"] = np.stack([np.concatenate([m, m], 2) for m in (k2, v2)], 1)
    t["cmp_pos"] = np.stack([a[n][0].reshape(LP, P).T for n in ("cmp_pos_k", "cmp_pos_v")], 1)
    t["w_out1"], t["w_out2"] = k_chunks(a["w_out"][0])
    small = np.zeros((P, HG + 2), np.float32)
    small[:, 0:HG] = a["hgrn_lower_bound"][0].reshape(HG, P).T
    small[:FOX_H, HG + 1] = a["fox_b_f_2"][0]
    t["small"] = small

    gains = np.zeros((16, 2 * D), np.float32)
    for i, g in enumerate((a["ffn1_norm"][0], a["mix_norm"][0], a["ffn2_norm"][0], a["final_norm"])):
        gains[i, :D] = g
    gains[0, D:D + P] = a["hgrn_out_norm"][0]
    for i in range(2):
        for j in range(4):
            gains[4 + 4 * i + j, :D] = a["ln_g_2"][i, j]
            gains[4 + 4 * i + j, D:] = a["ln_b_2"][i, j]
        gains[14 + i, :D] = a["ple_b_gate_2"][i]
    gains[12, :KL] = a["kv_norm_2"]
    gains[13, :QL] = a["mla_q_norm_2"][0]
    t["gains"] = gains

    w = a["fox_w_in_2"][0]
    fq, fk, fv, ff = w[:, :D], w[:, D:2 * D], w[:, 2 * D:3 * D], w[:, 3 * D:]
    t["fox_v"] = np.concatenate([chunk(fv[:, i * SEQ:(i + 1) * SEQ]) for i in range(4)])
    t["fox_f"] = chunk(np.concatenate([ff, np.zeros((D, P - FOX_H), np.float32)], 1))
    t["fox_qk"] = np.concatenate([chunk(tile(fq, j), tile(fk, j)) for j in range(KD)])
    t["fox_o1"], t["fox_o2"] = k_chunks(a["fox_w_o_2"][0])
    for i in range(2):
        t[f"ple{i}_p"] = chunk(a["ple_w_proj_2"][i])
        t[f"ple{i}_g1"], t[f"ple{i}_g2"] = k_chunks(a["ple_w_gate_2"][i])
    t["pT"] = a["p_2"][:, 0].transpose(0, 2, 1).reshape(2, 2, P, SEQ).transpose(0, 2, 1, 3)
    down = a["kv_w_down_2"]
    half = ROPE // 2
    rope = down[:, KL:]
    swap = lambda m: np.concatenate([m[..., half:], m[..., :half]], -1)
    t["kv_down1"] = chunk(down[:, :KL])
    t["kv_down2"] = chunk(rope, rope, swap(rope), swap(rope))
    t["mla_dq"] = chunk(a["mla_w_dq_2"][0])
    uq, up = a["mla_w_uq_2"][0], a["kv_w_up_2"]
    pairs = []
    for p in range(MLA_H // 2):
        h0, h1 = 2 * p, 2 * p + 1
        pairs.append(np.concatenate([
            chunk(uq[:, h0, :P], uq[:, h1, :P], uq[:, h0, P:], uq[:, h1, P:], swap(uq[:, h0, P:]), swap(uq[:, h1, P:])),
            chunk(up[:, h0, :P], up[:, h1, :P]), chunk(up[:, h0, P:], up[:, h1, P:])], 2))
    t["mla_up"] = np.concatenate(pairs)
    t["mla_o1"], t["mla_o2"] = k_chunks(a["mla_w_o_2"][0])
    return {n: np.ascontiguousarray(v) for n, v in t.items()}


def kernel(**inputs):
    import concourse.bacc as bacc
    from concourse.bass_utils import run_bass_kernel_spmd

    nc = bacc.Bacc("TRN2", target_bir_lowering=False, num_devices=1)
    arrays, t = {}, {}
    for name, v in layouts({n: np.asarray(v) for n, v in inputs.items()}).items():
        arrays["in_" + name] = v
        t[name] = nc.dram_tensor("in_" + name, v.shape, F32, kind="ExternalInput").ap()
    t["cum_scratch"] = nc.dram_tensor("cum_scratch", (FOX_H, SEQ), F32, kind="Internal").ap()
    out = nc.dram_tensor("out", (SEQ, D), F32, kind="ExternalOutput").ap()
    build(nc, t, out)
    r = run_bass_kernel_spmd(nc, [arrays], core_ids=[0])
    return r.results[0]["out"].reshape(1, SEQ, D)
```
